# Optimizing a Trainium2 kernel written in Bass

```python
import jax, jax.numpy as jnp
from jax import lax
import numpy as np
import math

D_MODEL = 1024
BATCH = 1
SEQ = 512
DEPTH = 2

HEAD_DIM = 64
SB_HEADS = D_MODEL // HEAD_DIM
SW_Q_HEADS = D_MODEL // HEAD_DIM
SW_KV_HEADS = max(1, SW_Q_HEADS // 8)
SW_GROUP = SW_Q_HEADS // SW_KV_HEADS
SW_IN = (SW_Q_HEADS + 2 * SW_KV_HEADS) * HEAD_DIM
WINDOW = 128
BLOCK = 128
ROPE_THETA = 500000.0
ROT_DIM = HEAD_DIM // 4
D_FF = ((8 * D_MODEL // 3 + 255) // 256) * 256
N_MIXERS = 2
N_SB_LAYERS = (DEPTH + 1) // 2
N_SW_LAYERS = DEPTH // 2
EPS = 1e-6


def rms_norm(x, gain):
    xf = x.astype(jnp.float32)
    y = xf * lax.rsqrt(jnp.mean(xf * xf, axis=-1, keepdims=True) + EPS)
    return (y * gain.astype(jnp.float32)).astype(x.dtype)

def swiglu(h, w_gate_up, w_down):
    gate, up = jnp.split(h @ w_gate_up, 2, axis=-1)
    return (jax.nn.silu(gate) * up) @ w_down

def rope_angles(positions):
    inv_freq = ROPE_THETA ** (-jnp.arange(0, ROT_DIM, 2, dtype=jnp.float32) / ROT_DIM)
    ang = positions.astype(jnp.float32)[..., None] * inv_freq
    return jnp.cos(ang), jnp.sin(ang)

def apply_partial_rope(x, cos, sin):
    half = ROT_DIM // 2
    x1 = x[..., :half].astype(jnp.float32)
    x2 = x[..., half:ROT_DIM].astype(jnp.float32)
    rot = jnp.concatenate([x1 * cos - x2 * sin, x2 * cos + x1 * sin], axis=-1).astype(x.dtype)
    return jnp.concatenate([rot, x[..., ROT_DIM:]], axis=-1)

def stick_breaking_attention(h, w_in, w_out):
    b, s, _ = h.shape
    q, k, v = jnp.split(h @ w_in, 3, axis=-1)
    q = q.reshape(b, s, SB_HEADS, HEAD_DIM).transpose(0, 2, 1, 3)
    k = k.reshape(b, s, SB_HEADS, HEAD_DIM).transpose(0, 2, 1, 3)
    v = v.reshape(b, s, SB_HEADS, HEAD_DIM).transpose(0, 2, 1, 3)
    scale = HEAD_DIM ** -0.5
    outs = []
    for blk in range(s // BLOCK):
        t0 = blk * BLOCK
        kv_len = t0 + BLOCK
        qb = q[:, :, t0:kv_len]
        kb = k[:, :, :kv_len]
        vb = v[:, :, :kv_len]
        z = jnp.einsum('bhtd,bhsd->bhts', qb, kb).astype(jnp.float32) * scale
        causal = (np.arange(kv_len)[None, :] < (t0 + np.arange(BLOCK))[:, None])
        log_beta = jax.nn.log_sigmoid(z)
        log_keep = jnp.where(causal, log_beta - z, 0.0)
        later = lax.cumsum(log_keep, axis=3, reverse=True) - log_keep
        weights = jnp.where(causal, jnp.exp(log_beta + later), 0.0)
        outs.append(jnp.einsum('bhts,bhsd->bhtd', weights.astype(vb.dtype), vb))
    o = jnp.concatenate(outs, axis=2).transpose(0, 2, 1, 3).reshape(b, s, SB_HEADS * HEAD_DIM)
    return o @ w_out

def sliding_window_attention(h, positions, w_in, w_out, q_gain, k_gain, sinks):
    b, s, _ = h.shape
    nb = s // BLOCK
    qkv = h @ w_in
    nq = SW_Q_HEADS * HEAD_DIM
    nk = SW_KV_HEADS * HEAD_DIM
    q = qkv[..., :nq].reshape(b, s, SW_KV_HEADS, SW_GROUP, HEAD_DIM)
    k = qkv[..., nq:nq + nk].reshape(b, s, SW_KV_HEADS, HEAD_DIM)
    v = qkv[..., nq + nk:].reshape(b, s, SW_KV_HEADS, HEAD_DIM)
    q = rms_norm(q, q_gain)
    k = rms_norm(k, k_gain)
    cos, sin = rope_angles(positions)
    q = apply_partial_rope(q, cos[:, :, None, None, :], sin[:, :, None, None, :])
    k = apply_partial_rope(k, cos[:, :, None, :], sin[:, :, None, :])
    pad = jnp.zeros((b, BLOCK, SW_KV_HEADS, HEAD_DIM), k.dtype)
    k_pad = jnp.concatenate([pad, k], axis=1).reshape(b, nb + 1, BLOCK, SW_KV_HEADS, HEAD_DIM)
    v_pad = jnp.concatenate([pad, v], axis=1).reshape(b, nb + 1, BLOCK, SW_KV_HEADS, HEAD_DIM)
    k_band = jnp.concatenate([k_pad[:, :-1], k_pad[:, 1:]], axis=2)
    v_band = jnp.concatenate([v_pad[:, :-1], v_pad[:, 1:]], axis=2)
    qb = q.reshape(b, nb, BLOCK, SW_KV_HEADS, SW_GROUP, HEAD_DIM)
    scores = jnp.einsum('bntkgd,bnskd->bnkgts', qb, k_band).astype(jnp.float32) * (HEAD_DIM ** -0.5)
    blk_start = np.arange(nb)[:, None, None] * BLOCK
    q_pos = blk_start + np.arange(BLOCK)[None, :, None]
    k_pos = blk_start - BLOCK + np.arange(2 * BLOCK)[None, None, :]
    mask = (k_pos >= 0) & (k_pos <= q_pos) & (q_pos - k_pos < WINDOW)
    scores = jnp.where(mask[None, :, None, None], scores, -jnp.inf)
    sink = sinks.astype(jnp.float32).reshape(SW_KV_HEADS, SW_GROUP)[None, None, :, :, None, None]
    m = jnp.maximum(jnp.max(scores, axis=-1, keepdims=True), sink)
    p = jnp.exp(scores - m)
    probs = p / (jnp.sum(p, axis=-1, keepdims=True) + jnp.exp(sink - m))
    o = jnp.einsum('bnkgts,bnskd->bntkgd', probs.astype(v_band.dtype), v_band)
    return o.reshape(b, s, SW_Q_HEADS * HEAD_DIM) @ w_out

def first_inputs(seed: int = 0) -> dict:
    key = jax.random.key(seed)
    ks = jax.random.split(key, 14)
    f32 = jnp.float32
    x = jax.random.normal(ks[0], (BATCH, SEQ, D_MODEL), f32)
    offsets = jax.random.randint(ks[1], (BATCH, 1), 0, 1024, dtype=jnp.int32)
    positions = offsets + jnp.arange(SEQ, dtype=jnp.int32)[None, :]
    norm_gains = 1.0 + 0.02 * jax.random.normal(ks[2], (DEPTH, 3, D_MODEL), f32)
    ffn_w_gate_up = jax.random.normal(ks[3], (DEPTH, 2, D_MODEL, 2 * D_FF), f32) * D_MODEL ** -0.5
    ffn_w_down = jax.random.normal(ks[4], (DEPTH, 2, D_FF, D_MODEL), f32) * D_FF ** -0.5
    sb_w_in = jax.random.normal(ks[5], (N_SB_LAYERS, D_MODEL, 3 * SB_HEADS * HEAD_DIM), f32) * D_MODEL ** -0.5
    sb_w_out = jax.random.normal(ks[6], (N_SB_LAYERS, SB_HEADS * HEAD_DIM, D_MODEL), f32) * (SB_HEADS * HEAD_DIM) ** -0.5
    sw_w_in = jax.random.normal(ks[7], (N_SW_LAYERS, D_MODEL, SW_IN), f32) * D_MODEL ** -0.5
    sw_w_out = jax.random.normal(ks[8], (N_SW_LAYERS, SW_Q_HEADS * HEAD_DIM, D_MODEL), f32) * (SW_Q_HEADS * HEAD_DIM) ** -0.5
    sw_q_gain = 1.0 + 0.02 * jax.random.normal(ks[9], (N_SW_LAYERS, HEAD_DIM), f32)
    sw_k_gain = 1.0 + 0.02 * jax.random.normal(ks[10], (N_SW_LAYERS, HEAD_DIM), f32)
    sw_sinks = 0.5 * jax.random.normal(ks[11], (N_SW_LAYERS, SW_Q_HEADS), f32)
    return {'x': x, 'positions': positions, 'norm_gains': norm_gains,
            'ffn_w_gate_up': ffn_w_gate_up, 'ffn_w_down': ffn_w_down,
            'sb_w_in': sb_w_in, 'sb_w_out': sb_w_out,
            'sw_w_in': sw_w_in, 'sw_w_out': sw_w_out,
            'sw_q_gain': sw_q_gain, 'sw_k_gain': sw_k_gain, 'sw_sinks': sw_sinks}

def first_block(x, positions, norm_gains, ffn_w_gate_up, ffn_w_down, sb_w_in, sb_w_out,
              sw_w_in, sw_w_out, sw_q_gain, sw_k_gain, sw_sinks):
    for i in range(DEPTH):
        slot = i // N_MIXERS
        x = x + 0.5 * swiglu(rms_norm(x, norm_gains[i, 0]), ffn_w_gate_up[i, 0], ffn_w_down[i, 0])
        h = rms_norm(x, norm_gains[i, 1])
        if i % N_MIXERS == 0:
            x = x + stick_breaking_attention(h, sb_w_in[slot], sb_w_out[slot])
        else:
            x = x + sliding_window_attention(h, positions, sw_w_in[slot], sw_w_out[slot],
                                             sw_q_gain[slot], sw_k_gain[slot], sw_sinks[slot])
        x = x + 0.5 * swiglu(rms_norm(x, norm_gains[i, 2]), ffn_w_gate_up[i, 1], ffn_w_down[i, 1])
    return x


DEPTH_2 = 1

CHUNK = 64
N_META = 16
N_PAD = CHUNK - N_META

SSD_EXPAND = 2
SSD_D_INNER = SSD_EXPAND * D_MODEL
SSD_HEAD_DIM = 64
SSD_N_HEADS = SSD_D_INNER // SSD_HEAD_DIM
SSD_N_GROUPS = 8
SSD_HEADS_PER_GROUP = SSD_N_HEADS // SSD_N_GROUPS
SSD_D_STATE = 128
SSD_CONV_W = 4
SSD_CONV_DIM = SSD_D_INNER + 2 * SSD_N_GROUPS * SSD_D_STATE

SC_WIDTH = D_MODEL
SC_CONV_W = 3

N_BRANCH = 2

PEER_HEADS = 8
PEER_N_KEYS = 128
PEER_N_EXPERTS = PEER_N_KEYS * PEER_N_KEYS
PEER_D_KEY = 256
PEER_HALF = PEER_D_KEY // 2
PEER_TOPK = 16
PEER_BLOCK = CHUNK

PROJ_SIZES = (
    SSD_D_INNER,
    SSD_D_INNER,
    SSD_N_GROUPS * SSD_D_STATE,
    SSD_N_GROUPS * SSD_D_STATE,
    SSD_N_HEADS,
    SC_WIDTH,
    SC_WIDTH,
    SC_WIDTH,
    N_BRANCH * D_MODEL,
)
PROJ_TOTAL = sum(PROJ_SIZES)


def rmsnorm(x, g):
    xf = x.astype(jnp.float32)
    y = xf * lax.rsqrt(jnp.mean(xf * xf, axis=-1, keepdims=True) + EPS)
    return (y * g).astype(x.dtype)

def group_rmsnorm(y, g, groups):
    shp = y.shape
    yg = y.reshape(shp[:-1] + (groups, shp[-1] // groups)).astype(jnp.float32)
    yg = yg * lax.rsqrt(jnp.mean(yg * yg, axis=-1, keepdims=True) + EPS)
    return yg.reshape(shp) * g

def causal_dwconv(x, w):
    K = w.shape[-1]
    L = x.shape[1]
    xp = jnp.pad(x, ((0, 0), (K - 1, 0), (0, 0)))
    y = xp[:, 0:L, :] * w[:, 0]
    for k in range(1, K):
        y = y + xp[:, k:k + L, :] * w[:, k]
    return y

def ssd_chunked_scan(xdt, adt, bm, cm):
    b, L = xdt.shape[:2]
    nc = L // CHUNK

    def to_chunks(t):
        return jnp.moveaxis(t.reshape((b, nc, CHUNK) + t.shape[2:]), 1, 0)

    causal = jnp.tril(jnp.ones((CHUNK, CHUNK), dtype=bool))[None, :, :, None, None]

    def step(state, inp):
        xc, ac, bc, cc = inp
        acum = jnp.cumsum(ac.astype(jnp.float32), axis=1)
        seg = acum[:, :, None] - acum[:, None, :]
        decay = jnp.exp(jnp.where(causal, seg, -jnp.inf))
        cb = jnp.einsum('blgn,bsgn->blsg', cc, bc).astype(jnp.float32)
        y_diag = jnp.einsum('blsgr,bsgrp->blgrp', cb[..., None] * decay, xc)
        y_off = jnp.einsum('blgn,bgrpn->blgrp', cc, state) * jnp.exp(acum)[..., None]
        to_end = jnp.exp(acum[:, -1:] - acum)
        new_state = (state * jnp.exp(acum[:, -1])[..., None, None]
                     + jnp.einsum('blgn,blgr,blgrp->bgrpn', bc, to_end, xc))
        return new_state, y_diag + y_off

    state0 = jnp.zeros((b, SSD_N_GROUPS, SSD_HEADS_PER_GROUP, SSD_HEAD_DIM, SSD_D_STATE), jnp.float32)
    _, y = lax.scan(step, state0, (to_chunks(xdt), to_chunks(adt), to_chunks(bm), to_chunks(cm)))
    return jnp.moveaxis(y, 0, 1).reshape((b, L) + xdt.shape[2:])

def ssd_branch(z, xs, bs, cs, dt, valid, conv_w, conv_b, dt_bias, a_log, d_skip, norm_g, w_out):
    b, L, _ = xs.shape
    xbc = jnp.concatenate([xs, bs, cs], axis=-1)
    xbc = jax.nn.silu(causal_dwconv(xbc, conv_w) + conv_b) * valid
    xs = xbc[..., :SSD_D_INNER]
    bs = xbc[..., SSD_D_INNER:SSD_D_INNER + SSD_N_GROUPS * SSD_D_STATE]
    cs = xbc[..., SSD_D_INNER + SSD_N_GROUPS * SSD_D_STATE:]
    dt = jax.nn.softplus(dt.astype(jnp.float32) + dt_bias)
    a = -jnp.exp(a_log.astype(jnp.float32))
    xh = xs.reshape(b, L, SSD_N_GROUPS, SSD_HEADS_PER_GROUP, SSD_HEAD_DIM)
    dtg = dt.reshape(b, L, SSD_N_GROUPS, SSD_HEADS_PER_GROUP)
    y = ssd_chunked_scan(xh * dtg[..., None],
                         dtg * a.reshape(SSD_N_GROUPS, SSD_HEADS_PER_GROUP),
                         bs.reshape(b, L, SSD_N_GROUPS, SSD_D_STATE),
                         cs.reshape(b, L, SSD_N_GROUPS, SSD_D_STATE))
    y = y + xh * d_skip.reshape(SSD_N_GROUPS, SSD_HEADS_PER_GROUP)[..., None]
    y = y.reshape(b, L, SSD_D_INNER)
    y = group_rmsnorm(y * jax.nn.silu(z.astype(jnp.float32)), norm_g, SSD_N_GROUPS)
    return y.astype(xs.dtype) @ w_out

def shortconv_branch(sb, sc, sx, conv_w, w_out):
    return (sb * causal_dwconv(sc * sx, conv_w)) @ w_out

def peer_ffn(h, w_q, sub_keys, expert_u, expert_v):
    T, D = h.shape
    blocks = h.reshape(T // PEER_BLOCK, PEER_BLOCK, D)

    def one(xb):
        q = (xb @ w_q).reshape(PEER_BLOCK, PEER_HEADS, 2, PEER_HALF)
        s = jnp.einsum('thjd,hjkd->thjk', q, sub_keys).astype(jnp.float32)
        sv, si = lax.top_k(s, PEER_TOPK)
        cand = sv[:, :, 0, :, None] + sv[:, :, 1, None, :]
        cs, ci = lax.top_k(cand.reshape(PEER_BLOCK, PEER_HEADS, PEER_TOPK * PEER_TOPK), PEER_TOPK)
        i1 = jnp.take_along_axis(si[:, :, 0], ci // PEER_TOPK, axis=-1)
        i2 = jnp.take_along_axis(si[:, :, 1], ci % PEER_TOPK, axis=-1)
        eidx = i1 * PEER_N_KEYS + i2
        g = jax.nn.softmax(cs, axis=-1)
        u = expert_u[eidx]
        v = expert_v[eidx]
        act = jax.nn.gelu(jnp.einsum('td,thkd->thk', xb, u).astype(jnp.float32), approximate=False)
        return jnp.einsum('thk,thkd->td', (g * act).astype(v.dtype), v)

    return lax.map(one, blocks).reshape(T, D)

def second_inputs(seed: int = 0) -> dict:
    key = jax.random.key(seed)
    ks = jax.random.split(key, 22)
    f32 = jnp.float32

    def nrm(k, shape, scale):
        return jax.random.normal(k, shape, f32) * scale

    x = nrm(ks[0], (BATCH, SEQ, D_MODEL), 1.0)
    meta_tokens = nrm(ks[1], (N_META, D_MODEL), 1.0)
    ln_mix = 1.0 + nrm(ks[2], (DEPTH_2, D_MODEL), 0.02)
    w_in = nrm(ks[3], (DEPTH_2, D_MODEL, PROJ_TOTAL), D_MODEL ** -0.5)
    ssd_conv_w = nrm(ks[4], (DEPTH_2, SSD_CONV_DIM, SSD_CONV_W), SSD_CONV_W ** -0.5)
    ssd_conv_b = nrm(ks[5], (DEPTH_2, SSD_CONV_DIM), 0.01)
    dt0 = jnp.exp(jax.random.uniform(ks[6], (DEPTH_2, SSD_N_HEADS), f32, math.log(1e-3), math.log(1e-1)))
    ssd_dt_bias = dt0 + jnp.log(-jnp.expm1(-dt0))
    ssd_a_log = jnp.log(jax.random.uniform(ks[7], (DEPTH_2, SSD_N_HEADS), f32, 1.0, 16.0))
    ssd_d = 1.0 + nrm(ks[8], (DEPTH_2, SSD_N_HEADS), 0.02)
    ssd_norm = 1.0 + nrm(ks[9], (DEPTH_2, SSD_D_INNER), 0.02)
    ssd_w_out = nrm(ks[10], (DEPTH_2, SSD_D_INNER, D_MODEL), SSD_D_INNER ** -0.5)
    sc_conv_w = nrm(ks[11], (DEPTH_2, SC_WIDTH, SC_CONV_W), SC_CONV_W ** -0.5)
    sc_w_out = nrm(ks[12], (DEPTH_2, SC_WIDTH, D_MODEL), SC_WIDTH ** -0.5)
    w_o = nrm(ks[13], (DEPTH_2, D_MODEL, D_MODEL), D_MODEL ** -0.5)
    ln_ffn = 1.0 + nrm(ks[14], (DEPTH_2, D_MODEL), 0.02)
    peer_w_q = nrm(ks[15], (DEPTH_2, D_MODEL, PEER_HEADS * PEER_D_KEY), D_MODEL ** -0.5)
    peer_sub_keys = nrm(ks[16], (DEPTH_2, PEER_HEADS, 2, PEER_N_KEYS, PEER_HALF), PEER_HALF ** -0.5)
    peer_u = nrm(ks[17], (DEPTH_2, PEER_N_EXPERTS, D_MODEL), D_MODEL ** -0.5)
    peer_v = nrm(ks[18], (DEPTH_2, PEER_N_EXPERTS, D_MODEL), PEER_HEADS ** -0.5)
    ln_final = 1.0 + nrm(ks[19], (D_MODEL,), 0.02)
    return {"x": x, "meta_tokens": meta_tokens, "ln_mix": ln_mix, "w_in": w_in,
            "ssd_conv_w": ssd_conv_w, "ssd_conv_b": ssd_conv_b, "ssd_dt_bias": ssd_dt_bias,
            "ssd_a_log": ssd_a_log, "ssd_d": ssd_d, "ssd_norm": ssd_norm, "ssd_w_out": ssd_w_out,
            "sc_conv_w": sc_conv_w, "sc_w_out": sc_w_out, "w_o": w_o, "ln_ffn": ln_ffn,
            "peer_w_q": peer_w_q, "peer_sub_keys": peer_sub_keys, "peer_u": peer_u,
            "peer_v": peer_v, "ln_final": ln_final}

def second_block(x, meta_tokens, ln_mix, w_in, ssd_conv_w, ssd_conv_b, ssd_dt_bias, ssd_a_log, ssd_d,
              ssd_norm, ssd_w_out, sc_conv_w, sc_w_out, w_o, ln_ffn, peer_w_q, peer_sub_keys,
              peer_u, peer_v, ln_final):
    b = x.shape[0]
    pad = jnp.zeros((b, N_PAD, D_MODEL), x.dtype)
    meta = jnp.broadcast_to(meta_tokens[None].astype(x.dtype), (b, N_META, D_MODEL))
    h = jnp.concatenate([pad, meta, x], axis=1)
    lp = h.shape[1]
    valid = (jnp.arange(lp) >= N_PAD)[None, :, None].astype(x.dtype)
    split_idx = [int(c) for c in np.cumsum(PROJ_SIZES)[:-1]]

    for l in range(DEPTH_2):
        u = rmsnorm(h, ln_mix[l]) * valid
        proj = u @ w_in[l]
        z, xs, bs, cs, dt, sb, sc, sx, gates = jnp.split(proj, split_idx, axis=-1)
        y_ssd = ssd_branch(z, xs, bs, cs, dt, valid, ssd_conv_w[l], ssd_conv_b[l], ssd_dt_bias[l],
                           ssd_a_log[l], ssd_d[l], ssd_norm[l], ssd_w_out[l])
        y_sc = shortconv_branch(sb, sc, sx, sc_conv_w[l], sc_w_out[l])
        g = jax.nn.sigmoid(gates.astype(jnp.float32))
        merged = (g[..., :D_MODEL] * y_ssd + g[..., D_MODEL:] * y_sc).astype(x.dtype)
        h = h + merged @ w_o[l]
        u = rmsnorm(h, ln_ffn[l]) * valid
        ff = peer_ffn(u.reshape(-1, D_MODEL), peer_w_q[l], peer_sub_keys[l], peer_u[l], peer_v[l])
        h = h + ff.reshape(h.shape).astype(h.dtype)

    out = rmsnorm(h[:, N_PAD + N_META:], ln_final)
    return out


def setup_inputs(seed=0):
    out = dict(first_inputs(seed))
    for name, value in second_inputs(seed + 1).items():
        if name != "x":
            out[name + "_2"] = value
    return out


def reference(
    x, positions, norm_gains, ffn_w_gate_up, ffn_w_down, sb_w_in, sb_w_out, sw_w_in, sw_w_out,
    sw_q_gain, sw_k_gain, sw_sinks, meta_tokens_2, ln_mix_2, w_in_2, ssd_conv_w_2, ssd_conv_b_2,
    ssd_dt_bias_2, ssd_a_log_2, ssd_d_2, ssd_norm_2, ssd_w_out_2, sc_conv_w_2, sc_w_out_2,
    w_o_2, ln_ffn_2, peer_w_q_2, peer_sub_keys_2, peer_u_2, peer_v_2, ln_final_2,
):
    x = first_block(
        x, positions, norm_gains, ffn_w_gate_up, ffn_w_down, sb_w_in, sb_w_out, sw_w_in,
        sw_w_out, sw_q_gain, sw_k_gain, sw_sinks,
    )
    return second_block(
        x, meta_tokens_2, ln_mix_2, w_in_2, ssd_conv_w_2, ssd_conv_b_2, ssd_dt_bias_2,
        ssd_a_log_2, ssd_d_2, ssd_norm_2, ssd_w_out_2, sc_conv_w_2, sc_w_out_2, w_o_2, ln_ffn_2,
        peer_w_q_2, peer_sub_keys_2, peer_u_2, peer_v_2, ln_final_2,
    )


_drawn_inputs = setup_inputs


def setup_inputs(seed=0):
    import zlib

    import numpy as np

    out = dict(_drawn_inputs(seed))
    spreads = {}
    factors = {'sw_q_gain': 7.105,
     'sw_k_gain': 7.379,
     'sw_sinks': 45.138,
     'ssd_conv_b_2': 5.909,
     'ssd_d_2': 16.78,
     'ssd_norm_2': 4.543,
     'ln_ffn_2': 3.38}
    for name, (base, spread) in spreads.items():
        noise = np.random.default_rng([zlib.crc32(name.encode()), seed]).standard_normal(out[name].shape)
        drawn = base * np.exp(spread * noise) if base else spread * noise
        out[name] = __import__('jax').numpy.asarray(drawn.astype(out[name].dtype))
    for name, factor in factors.items():
        out[name] = (out[name] * factor).astype(out[name].dtype)
    return out
```

```python
from contextlib import ExitStack

import numpy as np

import concourse.bass as bass
from concourse import mybir

F32 = mybir.dt.float32
F32R = mybir.dt.float32r
I32 = mybir.dt.int32
U32 = mybir.dt.uint32
ALU = mybir.AluOpType
ACT = mybir.ActivationFunctionType
AX = mybir.AxisListType.X

P = 128
T = 512
D = 1024
KD = D // P
TC = T // P
BANK = 512
TILE = 2048
HEAD = 64
EPS = 1e-6

F_FF = 2816
KF = F_FF // P
KH = KF // 2

META = 16
TM = META + T


class Chip:
    pass


def sem(c, name):
    return c.ctx.enter_context(c.nc.semaphore(name))


def shared(c, kind, names):
    if kind not in c.stages:
        c.stages[kind] = [0, [sem(c, f"{kind}_{n}") for n in names]]
    stage = c.stages[kind]
    stage[0] += 1
    return [stage[0] - 1] + stage[1]


def load_tile(c, sp, use, slot, parts):
    sp.wait_ge(c.begun, 1)
    sp.wait_ge(c.lo_ready, 2 * use + slot + 1)
    for dst, src in parts:
        sp.dma_start(dst, src).then_inc(c.tile_loaded[slot], 16)


def split_hi(c, act, use, slot, cols=TILE):
    act.wait_ge(c.tile_loaded[slot], 32 * use + 32)
    act.wait_ge(c.tile_used, 2 * use + slot + 1)
    c.nc.scalar.copy(c.hi[:, slot, :cols], c.raw[:, slot, :cols]).then_inc(c.hi_ready, 1)


def split_lo(c, dve, use, slot, cols=TILE):
    dve.wait_ge(c.hi_ready, 2 * use + slot + 1)
    c.nc.vector.tensor_tensor(c.lo[:, slot, :cols], c.raw[:, slot, :cols],
                              c.hi[:, slot, :cols].bitcast(F32), ALU.subtract).then_inc(c.lo_ready, 1)


def wait_tile(c, pe, use, slot):
    pe.wait_ge(c.lo_ready, 2 * use + slot + 3)


def products(c, out, pairs):
    last = len(pairs) - 1
    for n, ((w_hi, w_lo), (x_hi, x_lo)) in enumerate(pairs):
        c.nc.tensor.matmul(out, w_hi, x_hi, start=(n == 0), stop=False)
        c.nc.tensor.matmul(out, w_hi, x_lo, start=False, stop=False)
        mm = c.nc.tensor.matmul(out, w_lo, x_hi, start=False, stop=(n == last))
    return mm


def w_tile(c, slot, k, width):
    return [part[:, slot, :k * width].rearrange("p (k n) -> p k n", k=k) for part in (c.hi, c.lo)]


def raw_tile(c, slot, k, width):
    return c.raw[:, slot, :k * width].rearrange("p (k n) -> p k n", k=k)


def wide_parts(c, slot, w, col, width=256):
    v = w.rearrange("(k p) n -> p k n", p=P)
    dst = raw_tile(c, slot, KD, width)
    return [(dst[:, k:k + KD // 2, :], v[:, k:k + KD // 2, bass.ds(col, width)]) for k in (0, KD // 2)]


def pair_parts(c, slot, w, col_a, col_b):
    v = w.rearrange("(k p) n -> p k n", p=P)
    dst = c.raw[:, slot, :].rearrange("p (j k n) -> p j k n", j=2, k=KD)
    return [(dst[:, j], v[:, :, bass.ds(col, P)]) for j, col in enumerate((col_a, col_b))]


def tall_parts(c, slot, w, row, k, col):
    v = w.rearrange("(k p) n -> p k n", p=P)
    dst = raw_tile(c, slot, k, P)
    a = k // 2
    return [(dst[:, lo:hi, :], v[:, row + lo:row + hi, bass.ds(col, P)]) for lo, hi in ((0, a), (a, k))]


VECTORS = (("norm_gains", 48), ("ln_mix", 8), ("ssd_conv_b", 32), ("ssd_norm", 16), ("ln_ffn", 8), ("ln_final", 8))
ROWS = (("sw_q_gain", HEAD), ("sw_k_gain", HEAD), ("sw_sinks", 16), ("ssd_dt_bias", 32), ("ssd_a_log", 32), ("ssd_d", 32))


def setup(c, w, first):
    nc = c.nc
    n_vec = sum(n for _, n in VECTORS)
    n_row = sum(n for _, n in ROWS)
    with ExitStack() as ph:
        vec_rows = ph.enter_context(nc.sbuf_tensor("vec_rows", [n_vec, P], F32))
        row = ph.enter_context(nc.sbuf_tensor("row", [1, n_row], F32))
        x_rows = ph.enter_context(nc.sbuf_tensor("x_rows", [P, TC, D], F32))
        made, turned, vec_loaded = (sem(c, n) for n in ("const_made", "in_turned", "vec_loaded"))
        loaded = [sem(c, f"in_loaded{t}") for t in range(TC)]
        taken = sem(c, "in_taken")
        ps = c.psum
        block = ph.enter_context(nc.Block())

        @block.sync
        def _(sp):
            at = 0
            for name, n in VECTORS:
                src = w[name]
                flat = src.rearrange("a b d -> (a b d)") if len(src.shape) == 3 else (
                    src.rearrange("a d -> (a d)") if len(src.shape) == 2 else src)
                sp.dma_start(vec_rows[at:at + n, :], flat.rearrange("(r p) -> r p", p=P)).then_inc(vec_loaded, 16)
                at += n
            at = 0
            for name, n in ROWS:
                src = w[name]
                sp.dma_start(row[0:1, at:at + n], src[0:1, :]).then_inc(vec_loaded, 16)
                at += n
            for t in range(TC):
                sp.dma_start(x_rows[:, t, :], w["x"][0, t * P:(t + 1) * P, :]).then_inc(loaded[t], 16)
            first(sp)

        @block.gpsimd
        def _(pool):
            pool.memset(c.ones[:, :], 1.0).then_inc(made, 1)
            pool.memset(c.neg_ones[:, :], -1.0).then_inc(made, 1)
            pool.memset(c.ident[:, :], 0.0).then_inc(made, 1)
            pool.memset(c.swa_mask[:, :, :], 0.0).then_inc(made, 1)
            pool.memset(c.causal_cap[:, :], 3e38).then_inc(made, 1)
            pool.wait_ge(made, 5)
            pool.affine_select(out=c.ident[:, :], in_=c.ident[:, :], compare_op=ALU.not_equal, fill=1.0,
                               base=0, pattern=[[-1, P]], channel_multiplier=1).then_inc(made, 1)
            pool.affine_select(out=c.tri_up[:, :], in_=c.ones[:, :], compare_op=ALU.is_ge, fill=0.0,
                               base=0, pattern=[[1, P]], channel_multiplier=-1).then_inc(made, 1)
            pool.affine_select(out=c.neg_tri[:, :], in_=c.neg_ones[:, :], compare_op=ALU.is_ge, fill=0.0,
                               base=0, pattern=[[-1, P]], channel_multiplier=1).then_inc(made, 1)
            pool.affine_select(out=c.causal_cap[:, :], in_=c.causal_cap[:, :], compare_op=ALU.is_gt, fill=0.0,
                               base=0, pattern=[[1, P]], channel_multiplier=-1).then_inc(made, 1)
            pool.affine_select(out=c.swa_mask[:, :, 0:P], in_=c.swa_mask[:, :, 0:P], compare_op=ALU.is_gt, fill=-3e38,
                               base=0, pattern=[[0, TC], [1, P]], channel_multiplier=-1).then_inc(made, 1)
            pool.affine_select(out=c.swa_mask[:, :, P:2 * P], in_=c.swa_mask[:, :, P:2 * P], compare_op=ALU.is_ge,
                               fill=-3e38, base=0, pattern=[[0, TC], [-1, P]], channel_multiplier=1).then_inc(made, 1)
            pool.wait_ge(made, 11)
            pool.memset(c.swa_mask[:, 0, 0:P], -3e38).then_inc(made, 1)
            pool.iota(c.iota[:, :], pattern=[[1, P]], base=0, channel_multiplier=0,
                      allow_small_or_imprecise_dtypes=True).then_inc(made, 1)

        @block.tensor
        def _(pe):
            pe.sem_inc(c.begun, 1)
            pe.sem_inc(c.tile_used, 2)
            pe.sem_inc(c.lo_ready, 2)
            pe.wait_ge(made, 13)
            pe.wait_ge(vec_loaded, 16 * (len(VECTORS) + len(ROWS)))
            nc.tensor.transpose(ps[:, 4, 0:n_vec], vec_rows[:, :], c.ident[0:n_vec, 0:n_vec]).then_inc(turned, 1)
            nc.tensor.matmul(ps[:, 5, 0:n_row], c.ones[0:1, :], row[0:1, :], start=True, stop=True).then_inc(turned, 1)
            for t in range(TC):
                pe.wait_ge(loaded[t], 16)
                if t >= 2:
                    pe.wait_ge(taken, 4 + t - 2 - 1)
                for k in range(KD):
                    b = 2 * (t % 2) + k // 4
                    mm = nc.tensor.transpose(ps[:, b, (k % 4) * P:(k % 4 + 1) * P], x_rows[:, t, k * P:(k + 1) * P],
                                             c.ident[:, :])
                mm.then_inc(turned, 1)

        @block.vector
        def _(dve):
            dve.wait_ge(turned, 2)
            nc.vector.tensor_copy(c.vec[:, 0:n_vec], ps[:, 4, 0:n_vec]).then_inc(taken, 1)
            nc.vector.tensor_copy(c.rows[:, 0:n_row], ps[:, 5, 0:n_row]).then_inc(taken, 1)
            for t in range(TC):
                dve.wait_ge(turned, 3 + t)
                src = ps[:, 2 * (t % 2):2 * (t % 2) + 2, :].rearrange("p b (k n) -> p (b k) n", n=P)
                nc.vector.tensor_copy(c.x_t[:, :, t * P:(t + 1) * P], src).then_inc(taken, 1)


def vec_at(name):
    at = 0
    for n, size in VECTORS:
        if n == name:
            return at
        at += size


def vec_col(c, name, i):
    at = vec_at(name) + i
    return c.vec[:, at:at + 1]


def row_of(c, name):
    at = 0
    for n, size in ROWS:
        if n == name:
            return c.rows[:, at:at + size]
        at += size


def norm(c, tag, gain, h, src=None, width=T, out_f32=None):
    nc = c.nc
    src = c.x_t if src is None else src
    banks = [(0, width)] if width <= BANK else [(0, width // 2), (width // 2, width)]
    with ExitStack() as ph:
        sq = ph.enter_context(nc.sbuf_tensor(f"sq_{tag}", [P, KD, width], F32))
        rstd = ph.enter_context(nc.sbuf_tensor(f"rstd_{tag}", [P, width], F32))
        run, squared, summed, rooted, steps, scaled, hi_done = shared(
            c, "norm", ("squared", "summed", "rooted", "steps", "scaled", "hi_done"))
        ps = c.psum[:, 0:len(banks), 0:banks[0][1]]
        block = ph.enter_context(nc.Block())

        @block.scalar
        def _(act):
            for n in range(2):
                half = slice(n * KD // 2, (n + 1) * KD // 2)
                nc.scalar.activation(sq[:, half], src[:, half], ACT.Square).then_inc(squared, 1)
            act.wait_ge(steps, run * 3 + 2)
            nc.scalar.activation(rstd[:, :], rstd[:, :], ACT.Sqrt).then_inc(rooted, 1)
            if h is not None:
                for k in range(KD):
                    act.wait_ge(scaled, run * KD + k + 1)
                    nc.scalar.copy(h[0][:, k, :], sq[:, k, :]).then_inc(hi_done, 1)

        @block.vector
        def _(dve):
            dve.wait_ge(squared, run * 2 + 2)
            nc.vector.tensor_tensor(sq[:, 0:4], sq[:, 0:4], sq[:, 4:8], ALU.add).then_inc(steps, 1)
            dve.wait_ge(summed, run + 1)
            nc.vector.tensor_scalar(rstd[:, :].rearrange("p (b n) -> p b n", b=len(banks)), ps,
                                    1.0 / D, EPS, ALU.mult, ALU.add).then_inc(steps, 1)
            dve.wait_ge(rooted, run + 1)
            nc.vector.reciprocal(rstd[:, :], rstd[:, :]).then_inc(steps, 1)
            dve.wait_ge(steps, run * 3 + 3)
            dst = sq if out_f32 is None else out_f32
            for k in range(KD):
                nc.vector.scalar_tensor_tensor(dst[:, k, :], src[:, k, :], gain(k), rstd[:, :], ALU.mult,
                                               ALU.mult).then_inc(scaled, 1)
            if h is not None:
                for k in range(KD):
                    dve.wait_ge(hi_done, run * KD + k + 1)
                    nc.vector.tensor_tensor(h[1][:, k, :], sq[:, k, :], h[0][:, k, :].bitcast(F32), ALU.subtract)

        @block.tensor
        def _(pe):
            pe.wait_ge(steps, run * 3 + 1)
            for b, (lo, hi) in enumerate(banks):
                for k in range(4):
                    mm = nc.tensor.matmul(ps[:, b, :], c.ones[:, :], sq[:, k, lo:hi], start=(k == 0), stop=(k == 3))
            mm.then_inc(summed, 1)


def ffn_first(c, w_gu, use):
    def go(sp):
        load_tile(c, sp, use, 0, wide_parts(c, 0, w_gu, 0))
        load_tile(c, sp, use, 1, wide_parts(c, 1, w_gu, F_FF))
    return go


def ffn(c, tag, w_gu, w_down, h, following):
    nc = c.nc
    n_up = F_FF // 256
    u0 = c.use
    u1 = u0 + n_up
    with ExitStack() as ph:
        a_hi = ph.enter_context(nc.sbuf_tensor(f"a_hi_{tag}", [P, KF, T], F32R))
        a_lo = ph.enter_context(nc.sbuf_tensor(f"a_lo_{tag}", [P, KF, T], F32R))
        a = ph.enter_context(nc.sbuf_tensor(f"a_{tag}", [P, 2, T], F32))
        silu = ph.enter_context(nc.sbuf_tensor(f"silu_{tag}", [P, 2, T], F32))
        run, gated, up_taken, a_hi_done, a_lo_done, out_taken = shared(
            c, "ffn", ("gated", "up_taken", "a_hi_done", "a_lo_done", "out_taken"))
        m0, n0 = run * n_up, run * KD
        ps = c.psum
        block = ph.enter_context(nc.Block())

        @block.sync
        def _(sp):
            with sp.Fori(1, n_up) as i:
                load_tile(c, sp, u0 + i, 0, wide_parts(c, 0, w_gu, i * 256))
                load_tile(c, sp, u0 + i, 1, wide_parts(c, 1, w_gu, i * 256 + F_FF))
            with sp.Fori(0, KD) as n:
                for j in range(2):
                    load_tile(c, sp, u1 + n, j, tall_parts(c, j, w_down, j * KH, KH, n * P))
            following(sp)

        @block.scalar
        def _(act):
            def body(i, cols):
                act.wait_ge(c.tile_used, 2 * (u0 + i) + 3)
                if not (isinstance(i, int) and i == 0):
                    act.wait_ge(up_taken, m0 + i)
                nc.scalar.activation(silu[:, :, :], ps[:, 0:2, :], ACT.Silu).then_inc(gated, 1)
                split_hi(c, act, u0 + i + 1, 0, cols)
                act.wait_ge(up_taken, m0 + i + 1)
                nc.scalar.copy(a_hi[:, bass.ds(i * 2, 2), :], a[:, :, :]).then_inc(a_hi_done, 1)
                split_hi(c, act, u0 + i + 1, 1, cols)

            split_hi(c, act, u0, 0)
            split_hi(c, act, u0, 1)
            body(0, TILE)
            with act.Fori(1, n_up - 1) as i:
                body(i, TILE)
            body(n_up - 1, KH * P)
            with act.Fori(1, KD) as n:
                split_hi(c, act, u1 + n, 0, KH * P)
                split_hi(c, act, u1 + n, 1, KH * P)

        @block.vector
        def _(dve):
            def body(i, cols):
                split_lo(c, dve, u0 + i + 1, 0, cols)
                dve.wait_ge(gated, m0 + i + 1)
                dve.wait_ge(c.tile_used, 2 * (u0 + i) + 4)
                if not (isinstance(i, int) and i == 0):
                    dve.wait_ge(a_lo_done, m0 + i)
                nc.vector.tensor_tensor(a[:, :, :], silu[:, :, :], ps[:, 2:4, :], ALU.mult).then_inc(up_taken, 1)
                split_lo(c, dve, u0 + i + 1, 1, cols)
                dve.wait_ge(a_hi_done, m0 + i + 1)
                nc.vector.tensor_tensor(a_lo[:, bass.ds(i * 2, 2), :], a[:, :, :],
                                        a_hi[:, bass.ds(i * 2, 2), :].bitcast(F32),
                                        ALU.subtract).then_inc(a_lo_done, 1)

            split_lo(c, dve, u0, 0)
            split_lo(c, dve, u0, 1)
            body(0, TILE)
            with dve.Fori(1, n_up - 1) as i:
                body(i, TILE)
            body(n_up - 1, KH * P)

            def add_out(n, bank):
                dve.wait_ge(c.tile_used, 2 * (u1 + n) + 4)
                nc.vector.scalar_tensor_tensor(c.x_t[:, n, :] if isinstance(n, int) else
                                               c.x_t[:, bass.ds(n, 1), :].rearrange("p k t -> p (k t)"),
                                               ps[:, 4 + bank, :], 0.5,
                                               c.x_t[:, n, :] if isinstance(n, int) else
                                               c.x_t[:, bass.ds(n, 1), :].rearrange("p k t -> p (k t)"),
                                               ALU.mult, ALU.add).then_inc(out_taken, 1)

            with dve.Fori(0, KD // 2 - 1) as m:
                for bank in range(2):
                    for j in range(2):
                        split_lo(c, dve, u1 + m * 2 + bank + 1, j, KH * P)
                    add_out(m * 2 + bank, bank)
            for j in range(2):
                split_lo(c, dve, u1 + KD - 1, j, KH * P)
            add_out(KD - 2, 0)
            add_out(KD - 1, 1)

        @block.tensor
        def _(pe):
            def up(i):
                for j in range(2):
                    wait_tile(c, pe, u0 + i, j)
                    if not (isinstance(i, int) and i == 0):
                        pe.wait_ge((gated, up_taken)[j], m0 + i)
                    w_hi, w_lo = w_tile(c, j, KD, 256)
                    for n in range(2):
                        col = slice(n * P, (n + 1) * P)
                        mm = products(c, ps[:, 2 * j + n, :], [
                            ((w_hi[:, k, col], w_lo[:, k, col]), (h[0][:, k, :], h[1][:, k, :])) for k in range(KD)])
                    mm.then_inc(c.tile_used, 1)

            up(0)
            with pe.Fori(1, n_up) as i:
                up(i)
            pe.wait_ge(a_lo_done, m0 + n_up)

            def down(n, bank, start_of_bank):
                if not start_of_bank:
                    pe.wait_ge(out_taken, n0 + n - 1)
                for j in range(2):
                    wait_tile(c, pe, u1 + n, j)
                    w_hi, w_lo = w_tile(c, j, KH, P)
                    for k in range(KH):
                        f = j * KH + k
                        first, final = j == 0 and k == 0, j == 1 and k == KH - 1
                        nc.tensor.matmul(ps[:, 4 + bank, :], w_hi[:, k, :], a_hi[:, f, :], start=first, stop=False)
                        nc.tensor.matmul(ps[:, 4 + bank, :], w_hi[:, k, :], a_lo[:, f, :], start=False, stop=False)
                        mm = nc.tensor.matmul(ps[:, 4 + bank, :], w_lo[:, k, :], a_hi[:, f, :], start=False,
                                              stop=final)
                    mm.then_inc(c.tile_used, 1)

            down(0, 0, True)
            down(1, 1, True)
            with pe.Fori(1, KD // 2) as m:
                down(m * 2, 0, False)
                down(m * 2 + 1, 1, False)
    c.use = u1 + KD


def store(c, out, src):
    nc = c.nc
    with ExitStack() as ph:
        rows = ph.enter_context(nc.sbuf_tensor("out_rows", [P, TC, D], F32))
        turned, taken, written = (sem(c, f"out_{n}") for n in ("turned", "taken", "written"))
        ps = c.psum
        block = ph.enter_context(nc.Block())

        @block.tensor
        def _(pe):
            for t in range(TC):
                for k in range(KD):
                    mm = nc.tensor.transpose(ps[:, 2 * t + k // 4, (k % 4) * P:(k % 4 + 1) * P],
                                             src[:, k, t * P:(t + 1) * P], c.ident[:, :])
                mm.then_inc(turned, 1)

        @block.vector
        def _(dve):
            for t in range(TC):
                dve.wait_ge(turned, t + 1)
                nc.vector.tensor_copy(rows[:, t, :].rearrange("p (b n) -> p b n", b=2),
                                      ps[:, 2 * t:2 * t + 2, :]).then_inc(taken, 1)

        @block.sync
        def _(sp):
            for t in range(TC):
                sp.wait_ge(taken, t + 1)
                sp.dma_start(out[0, t * P:(t + 1) * P, :], rows[:, t, :]).then_inc(written, 16)
            sp.wait_ge(written, 16 * TC)


def wide_first(c, w, use):
    def go(sp):
        for j in range(2):
            load_tile(c, sp, use, j, wide_parts(c, j, w, j * 256))
    return go


def split_acts(c, src, h, chunks):
    nc = c.nc
    with ExitStack() as ph:
        run, hi_done = shared(c, f"split{chunks}", ("hi_done",))
        block = ph.enter_context(nc.Block())

        @block.scalar
        def _(act):
            for k in range(0, chunks, 4):
                nc.scalar.copy(h[0][:, k:k + 4, :], src[:, k:k + 4, :]).then_inc(hi_done, 1)

        @block.vector
        def _(dve):
            for k in range(0, chunks, 4):
                dve.wait_ge(hi_done, run * (chunks // 4) + k // 4 + 1)
                nc.vector.tensor_tensor(h[1][:, k:k + 4, :], src[:, k:k + 4, :],
                                        h[0][:, k:k + 4, :].bitcast(F32), ALU.subtract)


def project(c, w, h, following, out=None):
    nc = c.nc
    pairs = D // 512
    u0 = c.use
    with ExitStack() as ph:
        run, added = shared(c, "project", ("added",))
        m0 = run * (2 * pairs + 2)
        ps = c.psum
        block = ph.enter_context(nc.Block())

        @block.sync
        def _(sp):
            with sp.Fori(1, pairs) as i:
                for j in range(2):
                    load_tile(c, sp, u0 + i, j, wide_parts(c, j, w, (i * 2 + j) * 256))
            following(sp)

        @block.scalar
        def _(act):
            with act.Fori(0, pairs) as i:
                for j in range(2):
                    split_hi(c, act, u0 + i, j)

        @block.vector
        def _(dve):
            dve.sem_inc(added, 2)
            for j in range(2):
                split_lo(c, dve, u0, j)

            def add(i, j):
                dve.wait_ge(c.tile_used, 2 * (u0 + i) + j + 3)
                place = bass.ds((i * 2 + j) * 2, 2)
                if out is None:
                    x = c.x_t[:, place, :]
                    nc.vector.tensor_tensor(x, x, ps[:, 2 * j:2 * j + 2, :], ALU.add).then_inc(added, 1)
                else:
                    nc.vector.tensor_copy(out[:, place, :], ps[:, 2 * j:2 * j + 2, :]).then_inc(added, 1)

            with dve.Fori(0, pairs - 1) as i:
                for j in range(2):
                    add(i, j)
                    split_lo(c, dve, u0 + i + 1, j)
            for j in range(2):
                add(pairs - 1, j)

        @block.tensor
        def _(pe):
            with pe.Fori(0, pairs) as i:
                for j in range(2):
                    wait_tile(c, pe, u0 + i, j)
                    pe.wait_ge(added, m0 + i * 2 + j + 1)
                    w_hi, w_lo = w_tile(c, j, KD, 256)
                    for n in range(2):
                        col = slice(n * P, (n + 1) * P)
                        mm = products(c, ps[:, 2 * j + n, :], [
                            ((w_hi[:, k, col], w_lo[:, k, col]), (h[0][:, k, :], h[1][:, k, :])) for k in range(KD)])
                    mm.then_inc(c.tile_used, 1)
    c.use = u0 + pairs


SB_GROUPS = D // 256
Z_OFF = {0: 0, 1: 512, 3: 896, 2: 1024}
Z_COLS = 1280


def z_cols(j, skip=0):
    return slice(Z_OFF[j] + skip, Z_OFF[j] + T - P * j)


def sb_attention(c, w_in, h, o_t, following):
    nc = c.nc
    u0 = c.use
    uq = u0 + 2
    with ExitStack() as ph:
        sb = lambda name, shape, dt=F32: ph.enter_context(nc.sbuf_tensor(f"sb_{name}", shape, dt))
        v = sb("v", [P, TC, D])
        v_group = sb("v_group", [P, TC, 256])
        qk = sb("qk", [P, 4, T])
        a = sb("a", [P, 2, Z_COLS])
        soft = sb("soft", [P, 2, Z_COLS])
        wt = sb("wt", [P, 2, Z_COLS])
        (v_taken, v_grouped, projected, qk_taken, z_done, abs_done, exp_done, ln_done, soft_done, soft_masked,
         sums_done, wt_done, wt_masked, pv_done, o_taken) = (sem(c, f"sb_{n}") for n in (
             "v_taken", "v_grouped", "projected", "qk_taken", "z_done", "abs_done", "exp_done", "ln_done",
             "soft_done", "soft_masked", "sums_done", "wt_done", "wt_masked", "pv_done", "o_taken"))
        ps = c.psum
        z = [ps[:, 3 * p:3 * p + 3, :].rearrange("p b n -> p (b n)") for p in range(2)]
        proj, pv = ps[:, 6, :], ps[:, 7, :]
        block = ph.enter_context(nc.Block())
        last = SB_GROUPS - 1

        @block.sync
        def _(sp):
            for j in range(2):
                load_tile(c, sp, u0 + 1, j, wide_parts(c, j, w_in, 2 * D + (2 + j) * 256))
            with sp.Fori(0, SB_GROUPS) as i:
                for j in range(2):
                    load_tile(c, sp, uq + i, j, wide_parts(c, j, w_in, i * 256 + j * D))
            following(sp)

        @block.gpsimd
        def _(pool):
            def group_v(i):
                pool.wait_ge(pv_done, i * 4 + 1)
                pool.tensor_copy(v_group[:, :, :], v[:, :, bass.ds(i * 256, 256)]).then_inc(v_grouped, 1)

            pool.wait_ge(v_taken, 4)
            with pool.Fori(0, SB_GROUPS) as i:
                group_v(i)

        @block.scalar
        def _(act):
            def exp_ln(n, p):
                act.wait_ge(z_done, n + 1)
                act.wait_ge(soft_done, n + 1 if isinstance(n, int) and n == 0 else n)
                nc.scalar.activation(a[:, p], z[p][:, 0:Z_COLS], ACT.Abs).then_inc(abs_done, 1)
                act.wait_ge(abs_done, n + 1)
                nc.scalar.activation(a[:, p], a[:, p], ACT.Exp, scale=-1.0).then_inc(exp_done, 1)
                act.wait_ge(exp_done, n + 1)
                nc.scalar.activation(a[:, p], a[:, p], ACT.Ln, bias=1.0).then_inc(ln_done, 1)

            def weights(n, p, credit=1):
                act.wait_ge(sums_done, n + 2)
                if credit:
                    act.wait_ge(pv_done, n + credit - 1)
                nc.scalar.activation(wt[:, p], z[p][:, 0:Z_COLS], ACT.Exp).then_inc(wt_done, 1)

            def take(i, m):
                act.wait_ge(projected, i * 4 + m + 1)
                act.wait_ge(z_done, i * 4 - (2 if m < 2 else 0))
                nc.scalar.mul(qk[:, m, :], proj, HEAD ** -0.5 if m % 2 == 0 else 1.0).then_inc(qk_taken, 1)

            act.preload_act_table_set("natural_log_exp_and_others")
            for j in range(2):
                split_hi(c, act, u0, j)
            for j in range(2):
                split_hi(c, act, u0 + 1, j)
            for j in range(2):
                split_hi(c, act, uq, j)
            for m in range(4):
                act.wait_ge(projected, m + 1)
                nc.scalar.mul(qk[:, m, :], proj, HEAD ** -0.5 if m % 2 == 0 else 1.0).then_inc(qk_taken, 1)
            exp_ln(0, 0)

            def body(i, more):
                for hh in range(4):
                    if more and hh:
                        for m in ((0,), (1,), (2, 3))[hh - 1]:
                            take(i + 1, m)
                    if hh < 3:
                        exp_ln(i * 4 + hh + 1, (hh + 1) % 2)
                    if more and hh == 0:
                        for j in range(2):
                            split_hi(c, act, uq + i + 1, j)
                    weights(i * 4 + hh, hh % 2, credit=2 if hh == 0 else 1)
                    if more and hh == 3:
                        exp_ln(i * 4 + 4, 0)

            with act.Fori(0, last) as i:
                body(i, True)
            body(last, False)

        @block.vector
        def _(dve):
            def causal(t, ready, done, n, credit=0):
                dve.wait_ge(ready, n + credit + 1)
                for j in range(TC):
                    blk = t[:, Z_OFF[j]:Z_OFF[j] + P]
                    nc.vector.tensor_tensor(blk, blk, c.causal_cap[:, :], ALU.min).then_inc(done, 1)

            def softplus(n, p):
                dve.wait_ge(ln_done, n + 1)
                dve.wait_ge(sums_done, n)
                nc.vector.scalar_tensor_tensor(soft[:, p], z[p][:, 0:Z_COLS], 0.0, a[:, p], ALU.max,
                                               ALU.add).then_inc(soft_done, 1)
                causal(soft[:, p], soft_done, soft_masked, n, 1)

            dve.sem_inc(soft_done, 1)

            def take_v(m, j):
                dve.wait_ge(c.tile_used, 2 * (u0 + m) + j + 3)
                nc.vector.tensor_copy(v[:, :, (2 * m + j) * 256:(2 * m + j + 1) * 256],
                                      ps[:, 2 * j:2 * j + 2, :].rearrange("p b (t n) -> p (b t) n", t=2)
                                      ).then_inc(v_taken, 1)

            for j in range(2):
                split_lo(c, dve, u0, j)
            for m in range(2):
                for j in range(2):
                    split_lo(c, dve, u0 + m + 1, j)
                    take_v(m, j)
            dve.sem_inc(o_taken, 1)
            dve.wait_ge(ln_done, 1)
            nc.vector.scalar_tensor_tensor(soft[:, 0], z[0][:, 0:Z_COLS], 0.0, a[:, 0], ALU.max,
                                           ALU.add).then_inc(soft_done, 1)
            causal(soft[:, 0], soft_done, soft_masked, 0, 1)

            def take_o(i, half):
                dve.wait_ge(pv_done, i * 4 + 2 * half + 3)
                nc.vector.tensor_copy(o_t[:, bass.ds(i * 2 + half, 1), :].rearrange("p k t -> p (k t)"),
                                      pv).then_inc(o_taken, 1)

            def body(i, more):
                for hh in range(4):
                    if more and hh == 0:
                        for j in range(2):
                            split_lo(c, dve, uq + i + 1, j)
                    if hh < 3:
                        softplus(i * 4 + hh + 1, (hh + 1) % 2)
                    if hh == 3:
                        take_o(i, 0)
                    causal(wt[:, hh % 2], wt_done, wt_masked, i * 4 + hh)
                    if hh == 3:
                        if more:
                            softplus(i * 4 + 4, 0)
                        take_o(i, 1)

            with dve.Fori(0, last) as i:
                body(i, True)
            body(last, False)

        @block.tensor
        def _(pe):
            def values(m):
                for j in range(2):
                    wait_tile(c, pe, u0 + m, j)
                    if m:
                        pe.wait_ge(v_taken, 2 * (m - 1) + j + 1)
                    w_hi, w_lo = w_tile(c, j, KD, 256)
                    for t in range(TC):
                        tok = slice(t * P, (t + 1) * P)
                        mm = products(c, ps[:, 2 * j + t // 2, (t % 2) * 256:(t % 2 + 1) * 256], [
                            ((h[0][:, k, tok], h[1][:, k, tok]), (w_hi[:, k, :], w_lo[:, k, :])) for k in range(KD)])
                    mm.then_inc(c.tile_used, 1)

            def project_chunk(i, m, first=False):
                j, n = m % 2, m // 2
                if n == 0:
                    wait_tile(c, pe, uq + i, j)
                if not (first and m == 0):
                    pe.wait_ge(qk_taken, i * 4 + m)
                w_hi, w_lo = w_tile(c, j, KD, 256)
                col = slice(n * P, (n + 1) * P)
                mm = products(c, proj, [((w_hi[:, k, col], w_lo[:, k, col]), (h[0][:, k, :], h[1][:, k, :]))
                                        for k in range(KD)])
                mm.then_inc(projected, 1)

            def scores(n, hh, first=False, frees=0):
                p, half = hh % 2, slice(HEAD * (hh % 2), HEAD * (hh % 2) + HEAD)
                q, k = qk[half, 2 * (hh // 2), :], qk[half, 2 * (hh // 2) + 1, :]
                if not first:
                    pe.wait_ge(wt_done, n - 1)
                for j in (0, 1, 3, 2):
                    mm = nc.tensor.matmul(z[p][:, z_cols(j)], k[:, j * P:(j + 1) * P], q[:, j * P:T],
                                          start=(j != 3), stop=False, skip_group_check=True)
                    if j < frees:
                        mm.then_inc(c.tile_used, 1)
                mm.then_inc(z_done, 1)

            def sums(n, hh, frees=0):
                p = hh % 2
                pe.wait_ge(soft_masked, n * 4 + 4)
                for j in (0, 1, 3, 2):
                    mm = nc.tensor.matmul(z[p][:, z_cols(j)], c.neg_tri[:, :], soft[:, p, z_cols(j)], start=False,
                                          stop=False, skip_group_check=True)
                    if j < frees:
                        mm.then_inc(c.tile_used, 1)
                for j in (0, 1, 2):
                    for later in range(j + 1, TC):
                        mm = nc.tensor.matmul(z[p][:, z_cols(j, (later - j) * P)], c.neg_ones[:, :],
                                              soft[:, p, z_cols(later)], start=False, stop=True,
                                              skip_group_check=True)
                mm.then_inc(sums_done, 1)

            def outputs(i, hh):
                p, half = hh % 2, slice(HEAD * (hh % 2), HEAD * (hh % 2) + HEAD)
                if hh == 0:
                    pe.wait_ge(v_grouped, i + 1)
                pe.wait_ge(wt_masked, (i * 4 + hh) * 4 + 4)
                if hh % 2 == 0:
                    pe.wait_ge(o_taken, i * 2 + hh // 2 + 1)
                for j in range(TC):
                    mm = nc.tensor.matmul(pv[half, j * P:T], v_group[:, j, hh * HEAD:(hh + 1) * HEAD],
                                          wt[:, p, z_cols(j)], start=(j == 0), stop=(j == TC - 1),
                                          skip_group_check=True)
                mm.then_inc(pv_done, 1)

            pe.sem_inc(pv_done, 1)
            pe.sem_inc(sums_done, 1)
            for m in range(2):
                values(m)
            for m in range(4):
                project_chunk(0, m, first=True)
            pe.wait_ge(v_taken, 4)
            pe.wait_ge(qk_taken, 2)
            scores(0, 0, first=True, frees=2)
            pe.wait_ge(qk_taken, 4)

            def body(i, more, first=False):
                n = i * 4
                scores(n + 1, 1, first)
                sums(n, 0)
                if more:
                    project_chunk(i + 1, 0)
                scores(n + 2, 2)
                sums(n + 1, 1)
                outputs(i, 0)
                if more:
                    project_chunk(i + 1, 1)
                scores(n + 3, 3)
                sums(n + 2, 2)
                outputs(i, 1)
                if more:
                    project_chunk(i + 1, 2)
                    project_chunk(i + 1, 3)
                sums(n + 3, 3, frees=2 if more else 0)
                outputs(i, 2)
                if more:
                    pe.wait_ge(qk_taken, i * 4 + 8)
                    scores(n + 4, 0)
                outputs(i, 3)

            body(0, True, first=True)
            with pe.Fori(1, last) as i:
                body(i, True)
            body(last, False)
    c.use = uq + SB_GROUPS


ROT = 16 // 2
INV_FREQ = [float(f) for f in np.float32(500000.0) ** (-np.arange(0, 16, 2, dtype=np.float32) / np.float32(16))]
TWO_PI = (6.28125, 0.0019350051879882812, 3.0198672e-07)
ROUND = 12582912.0
SW_HEADS = 16
SW_QK = SW_HEADS + 2


def sw_project(c, w_in, h, qk, v, following):
    nc = c.nc
    u0 = c.use
    with ExitStack() as ph:
        taken = sem(c, "sw_taken")
        ps = c.psum
        block = ph.enter_context(nc.Block())

        @block.sync
        def _(sp):
            for j in range(2):
                load_tile(c, sp, u0 + 1, j, wide_parts(c, j, w_in, (2 + j) * 256))
            for j in range(2):
                load_tile(c, sp, u0 + 2, j, wide_parts(c, j, w_in, D + j * P, P))
            following(sp)

        @block.scalar
        def _(act):
            for m in range(3):
                for j in range(2):
                    split_hi(c, act, u0 + m, j, TILE if m < 2 else KD * P)

        @block.vector
        def _(dve):
            for j in range(2):
                split_lo(c, dve, u0, j)
            for m in range(2):
                for j in range(2):
                    split_lo(c, dve, u0 + m + 1, j, TILE if m == 0 else KD * P)
                    dve.wait_ge(c.tile_used, 2 * (u0 + m) + j + 3)
                    nc.vector.tensor_copy(qk[:, :, (2 * m + j) * 256:(2 * m + j + 1) * 256],
                                          ps[:, 2 * j:2 * j + 2, :].rearrange("p b (t n) -> p (b t) n", t=2)
                                          ).then_inc(taken, 1)
            for j, dst in enumerate((qk[:, :, D:D + P], v[:, :, :])):
                dve.wait_ge(c.tile_used, 2 * (u0 + 2) + j + 3)
                nc.vector.tensor_copy(dst, ps[:, 4 + j, :].rearrange("p (t n) -> p t n", t=TC)).then_inc(taken, 1)

        @block.tensor
        def _(pe):
            for m in range(3):
                width = 256 if m < 2 else P
                for j in range(2):
                    wait_tile(c, pe, u0 + m, j)
                    if m == 1:
                        pe.wait_ge(taken, j + 1)
                    w_hi, w_lo = w_tile(c, j, KD, width)
                    for t in range(TC):
                        tok = slice(t * P, (t + 1) * P)
                        out = (ps[:, 2 * j + t // 2, (t % 2) * 256:(t % 2 + 1) * 256] if m < 2
                               else ps[:, 4 + j, t * P:(t + 1) * P])
                        mm = products(c, out, [
                            ((h[0][:, k, tok], h[1][:, k, tok]), (w_hi[:, k, :], w_lo[:, k, :])) for k in range(KD)])
                    mm.then_inc(c.tile_used, 1)
    c.use = u0 + 3


def sw_rotate(c, positions, qk):
    nc = c.nc
    with ExitStack() as ph:
        sb = lambda name, shape, dt=F32: ph.enter_context(nc.sbuf_tensor(f"sw_{name}", shape, dt))
        sq = sb("sq", [P, TC, SW_QK * HEAD])
        rstd = sb("rstd", [P, TC * SW_QK])
        gains = sb("gains", [P, 2, HEAD])
        pos_i = sb("pos_i", [TC, P], I32)
        pos_f = sb("pos_f", [TC, P])
        pos = sb("pos", [P, TC])
        ang = sb("ang", [P, TC, ROT])
        turns = sb("turns", [P, TC, ROT])
        cos = sb("cos", [P, TC, ROT])
        wrap = sb("wrap", [P, TC, ROT])
        prod = [sb(f"prod{n}", [P, TC, SW_QK, ROT]) for n in range(4)]
        pos_loaded, squared, rooted, sined, pos_turned, steps = (
            sem(c, f"sw_{n}") for n in ("pos_loaded", "squared", "rooted", "sined", "pos_turned", "steps"))
        ps = c.psum
        block = ph.enter_context(nc.Block())
        count = [0]

        def step(dve, ins):
            count[0] += 1
            ins.then_inc(steps, 1)
            dve.wait_ge(steps, count[0])

        POS_READY, MEAN_READY, ANGLES_READY = 1, 4, 4 + ROT + 10

        @block.sync
        def _(sp):
            sp.dma_start(pos_i[:, :], positions.rearrange("a (t p) -> (a t) p", p=P)).then_inc(pos_loaded, 16)

        @block.tensor
        def _(pe):
            pe.wait_ge(steps, POS_READY)
            nc.tensor.transpose(ps[:, 7, 0:TC], pos_f[:, :], c.ident[0:TC, 0:TC]).then_inc(pos_turned, 1)

        @block.scalar
        def _(act):
            for t in range(TC):
                nc.scalar.activation(sq[:, t, :], qk[:, t, :], ACT.Square).then_inc(squared, 1)
            act.wait_ge(steps, MEAN_READY)
            nc.scalar.activation(rstd[:, :], rstd[:, :], ACT.Sqrt).then_inc(rooted, 1)
            act.wait_ge(steps, ANGLES_READY)
            nc.scalar.activation(ang[:, :, :], ang[:, :, :], ACT.Sin).then_inc(sined, 1)
            nc.scalar.activation(cos[:, :, :], cos[:, :, :], ACT.Sin).then_inc(sined, 1)

        @block.vector
        def _(dve):
            v = nc.vector
            dve.wait_ge(pos_loaded, 16)
            step(dve, v.tensor_copy(pos_f[:, :], pos_i[:, :]))
            dve.wait_ge(squared, TC)
            step(dve, v.tensor_reduce(rstd[:, :], sq[:, :, :].rearrange("p t (h d) -> p (t h) d", d=HEAD), AX, ALU.add))
            step(dve, v.tensor_scalar(gains[:, 0, :], row_of(c, "sw_q_gain"), HEAD ** -0.5, None, ALU.mult))
            step(dve, v.tensor_scalar(rstd[:, :], rstd[:, :], 1.0 / HEAD, EPS, ALU.mult, ALU.add))
            dve.wait_ge(pos_turned, 1)
            step(dve, v.tensor_copy(pos[:, :], ps[:, 7, 0:TC]))
            for n, f in enumerate(INV_FREQ):
                step(dve, v.tensor_scalar(ang[:, :, n], pos[:, :], f, None, ALU.mult))
            step(dve, v.tensor_scalar(turns[:, :, :], ang[:, :, :], 1.0 / (2 * np.pi), ROUND, ALU.mult, ALU.add))
            step(dve, v.tensor_scalar(turns[:, :, :], turns[:, :, :], -ROUND, None, ALU.add))
            for part in TWO_PI:
                step(dve, v.scalar_tensor_tensor(ang[:, :, :], turns[:, :, :], -part, ang[:, :, :], ALU.mult, ALU.add))
            step(dve, v.tensor_scalar(wrap[:, :, :], ang[:, :, :], np.pi / 2, -2 * np.pi, ALU.is_gt, ALU.mult))
            step(dve, v.scalar_tensor_tensor(cos[:, :, :], ang[:, :, :], np.pi / 2, wrap[:, :, :], ALU.add, ALU.add))
            for t in (ang, cos):
                ins = v.tensor_scalar(t[:, :, :], t[:, :, :], 3.1415925, -3.1415925, ALU.min, ALU.max)
                if t is ang:
                    step(dve, ins)
            ins.then_inc(steps, 1)
            count[0] += 1
            assert count[0] == ANGLES_READY
            dve.wait_ge(rooted, 1)
            step(dve, v.reciprocal(rstd[:, :], rstd[:, :]))
            heads = qk[:, :, :].rearrange("p t (h d) -> p (t h) d", d=HEAD)
            step(dve, v.tensor_tensor(heads, heads, rstd[:, :].unsqueeze(2).broadcast_to([P, TC * SW_QK, HEAD]),
                                      ALU.mult))
            q = qk[:, :, 0:D].rearrange("p t (h d) -> p t h d", d=HEAD)
            k = qk[:, :, D:D + P].rearrange("p t (h d) -> p t h d", d=HEAD)
            for part, gain, n in ((q, gains[:, 0, :], SW_HEADS), (k, row_of(c, "sw_k_gain"), 2)):
                step(dve, v.tensor_tensor(part, part, gain.unsqueeze(1).unsqueeze(1).broadcast_to([P, TC, n, HEAD]),
                                          ALU.mult))
            dve.wait_ge(sined, 2)
            all_heads = qk[:, :, :].rearrange("p t (h d) -> p t h d", d=HEAD)
            x1, x2 = all_heads[:, :, :, 0:ROT], all_heads[:, :, :, ROT:2 * ROT]
            wide = lambda t: t[:, :, :].unsqueeze(2).broadcast_to([P, TC, SW_QK, ROT])
            for n, (x, y) in enumerate(((x1, cos), (x2, ang), (x2, cos), (x1, ang))):
                step(dve, v.tensor_tensor(prod[n][:, :, :, :], x, wide(y), ALU.mult))
            step(dve, v.tensor_tensor(x1, prod[0][:, :, :, :], prod[1][:, :, :, :], ALU.subtract))
            step(dve, v.tensor_tensor(x2, prod[2][:, :, :, :], prod[3][:, :, :, :], ALU.add))


def sw_attention(c, qk, v, o_t):
    nc = c.nc
    pairs = SW_HEADS // 4
    with ExitStack() as ph:
        sb = lambda name, shape, dt=F32: ph.enter_context(nc.sbuf_tensor(f"sw_{name}", shape, dt))
        k_twice = sb("k_twice", [P, 2, TC, 2, HEAD])
        k_t = sb("k_t", [P, 2, P + T])
        q_rows = sb("q_rows", [P, TC, P])
        q_t = sb("q_t", [P, T])
        s = sb("s", [P, 2, TC, 2 * P])
        probs_t = sb("probs_t", [P, 2, TC, 2, P])
        top = sb("top", [P, 2, TC])
        den = sb("den", [P, 2, TC])
        sink = sb("sink", [P, 2, TC])
        (k_copied, k_turned, k_taken, q_copied, q_turned, q_taken, scored, masked, maxed, topped, weighed, sunk, summed,
         inverted, normed, turned, probs_taken, pv_done, o_taken) = (sem(c, f"sw_{n}") for n in (
             "k_copied", "k_turned", "k_taken", "q_copied", "q_turned", "q_taken", "scored", "masked", "maxed",
             "topped", "weighed", "sunk", "summed", "inverted", "normed", "turned", "probs_taken", "pv_done",
             "o_taken"))
        ps = c.psum
        block = ph.enter_context(nc.Block())

        @block.gpsimd
        def _(pool):
            for kv in range(2):
                for r in range(2):
                    pool.tensor_copy(k_twice[:, kv, :, r, :], qk[:, :, D + kv * HEAD:D + (kv + 1) * HEAD]
                                     ).then_inc(k_copied, 1)
            pool.memset(k_t[:, :, 0:P], 0.0).then_inc(k_copied, 1)

            with pool.Fori(0, 2 * pairs) as pair:
                pool.wait_ge(q_turned, pair + 1)
                pool.tensor_copy(q_rows[:, :, :], qk[:, :, bass.ds(pair * P, P)]).then_inc(q_copied, 1)

        @block.scalar
        def _(act):
            for kv in range(2):
                act.wait_ge(k_turned, kv + 1)
                nc.scalar.copy(k_t[:, kv, P:P + T], ps[:, kv, :]).then_inc(k_taken, 1)

            with act.Fori(0, 2 * pairs) as pair:
                act.wait_ge(q_turned, pair + 2)
                nc.scalar.copy(q_t[:, :], ps[:, 0, :]).then_inc(q_taken, 1)
                for e in range(2):
                    n = pair * 2 + e
                    act.wait_ge(topped, n + 1)
                    for t in range(TC):
                        nc.scalar.activation(s[:, e, t, :], s[:, e, t, :], ACT.Exp, bias=top[:, e, t:t + 1],
                                             accum_out=den[:, e, t:t + 1]).then_inc(weighed, 1)
                    nc.scalar.activation(sink[:, e, :], top[:, e, :], ACT.Exp,
                                         bias=row_of(c, "sw_sinks")[:, bass.ds(n, 1)]).then_inc(sunk, 1)
                for e in range(2):
                    n = pair * 2 + e
                    act.wait_ge(turned, n + 1)
                    nc.scalar.copy(probs_t[:, e].rearrange("p t b n -> p (t b n)"),
                                   ps[:, 5:7, :].rearrange("p b n -> p (b n)")).then_inc(probs_taken, 1)

        @block.vector
        def _(dve):
            v_ = nc.vector
            sinks = row_of(c, "sw_sinks")

            def out(pair):
                dve.wait_ge(pv_done, pair * 2 + 2)
                v_.tensor_copy(o_t[:, bass.ds(pair, 1), :].rearrange("p k t -> p (k t)"), ps[:, 7, :]
                               ).then_inc(o_taken, 1)

            dve.sem_inc(o_taken, 1)
            with dve.Fori(0, 2 * pairs) as pair:
                for e in range(2):
                    n = pair * 2 + e
                    dve.wait_ge(scored, n + 1)
                    v_.tensor_tensor(s[:, e], ps[:, 1 + 2 * e:3 + 2 * e, :].rearrange("p b (t n) -> p (b t) n", t=2),
                                     c.swa_mask[:, :, :],
                                     ALU.add).then_inc(masked, 1)
                    dve.wait_ge(masked, n + 1)
                    v_.tensor_reduce(top[:, e, :], s[:, e], AX, ALU.max).then_inc(maxed, 1)
                    dve.wait_ge(maxed, n + 1)
                    v_.tensor_scalar(top[:, e, :], top[:, e, :], sinks[:, bass.ds(n, 1)], -1.0, ALU.max,
                                     ALU.mult).then_inc(topped, 1)
                for e in range(2):
                    n = pair * 2 + e
                    dve.wait_ge(weighed, n * TC + TC)
                    dve.wait_ge(sunk, n + 1)
                    v_.tensor_tensor(den[:, e, :], den[:, e, :], sink[:, e, :], ALU.add).then_inc(summed, 1)
                    dve.wait_ge(summed, n + 1)
                    v_.reciprocal(den[:, e, :], den[:, e, :]).then_inc(inverted, 1)
                    dve.wait_ge(inverted, n + 1)
                    v_.tensor_tensor(s[:, e], s[:, e], den[:, e, :].unsqueeze(2).broadcast_to([P, TC, 2 * P]),
                                     ALU.mult).then_inc(normed, 1)
                out(pair)

        @block.tensor
        def _(pe):
            pe.wait_ge(k_copied, 5)
            for kv in range(2):
                for t in range(TC):
                    mm = nc.tensor.transpose(ps[:, kv, t * P:(t + 1) * P],
                                             k_twice[:, kv, t].rearrange("p r d -> p (r d)"), c.ident[:, :])
                mm.then_inc(k_turned, 1)
            pe.wait_ge(k_taken, 2)
            pe.sem_inc(q_turned, 1)

            def body(pair, kv):
                pe.wait_ge(q_copied, pair + 1)
                if not (isinstance(pair, int) and pair == 0):
                    pe.wait_ge(q_taken, pair)
                for t in range(TC):
                    mm = nc.tensor.transpose(ps[:, 0, t * P:(t + 1) * P], q_rows[:, t, :], c.ident[:, :])
                mm.then_inc(q_turned, 1)
                pe.wait_ge(q_taken, pair + 1)
                for e in range(2):
                    half = slice(e * HEAD, (e + 1) * HEAD)
                    if not (isinstance(pair, int) and pair == 0):
                        pe.wait_ge(masked, pair * 2 + e - 1)
                    for t in range(TC):
                        mm = nc.tensor.matmul(ps[:, 1 + 2 * e + t // 2, (t % 2) * 256:(t % 2 + 1) * 256],
                                              q_t[half, t * P:(t + 1) * P], k_t[half, kv, t * P:(t + 2) * P],
                                              start=True, stop=True)
                    mm.then_inc(scored, 1)
                for e in range(2):
                    n = pair * 2 + e
                    pe.wait_ge(normed, n + 1)
                    if not (isinstance(pair, int) and n == 0):
                        pe.wait_ge(probs_taken, n)
                    for t in range(TC):
                        for b in range(2):
                            m = 2 * t + b
                            mm = nc.tensor.transpose(ps[:, 5 + m // 4, (m % 4) * P:(m % 4 + 1) * P],
                                                     s[:, e, t, b * P:(b + 1) * P], c.ident[:, :])
                    mm.then_inc(turned, 1)
                    pe.wait_ge(probs_taken, n + 1)
                    if e == 0:
                        pe.wait_ge(o_taken, pair + 1)
                    half = slice(e * HEAD, (e + 1) * HEAD)
                    for t in range(TC):
                        blocks = (0, 1) if t else (1,)
                        for b in blocks:
                            mm = nc.tensor.matmul(ps[half, 7, t * P:(t + 1) * P],
                                                  v[:, t - 1 + b, kv * HEAD:(kv + 1) * HEAD], probs_t[:, e, t, b, :],
                                                  start=(b == blocks[0]), stop=(b == 1))
                    mm.then_inc(pv_done, 1)

            body(0, 0)
            with pe.Fori(1, pairs) as pair:
                body(pair, 0)
            with pe.Fori(pairs, 2 * pairs) as pair:
                body(pair, 1)


SSD_IN = 2048
GROUPS = 8
G_COLS = SSD_IN // GROUPS
G_HEADS = 4
TAPS = 4
Z_AT, XS_AT, B_AT, C_AT, DT_AT, SB_AT, SC_AT, SX_AT, GATE_AT = 0, 2048, 4096, 5120, 6144, 6176, 7200, 8224, 9248
HALF_TM = TM // 2


def ssd_first(c, w_in, use, g=0):
    def go(sp):
        load_tile(c, sp, use, 0, wide_parts(c, 0, w_in, g * G_COLS + XS_AT))
        load_tile(c, sp, use, 1, pair_parts(c, 1, w_in, g * P + B_AT, g * P + C_AT))
    return go


def widen(c, meta, xm):
    nc = c.nc
    with ExitStack() as ph:
        rows = ph.enter_context(nc.sbuf_tensor("meta_rows", [META, D], F32))
        loaded, turned = sem(c, "meta_loaded"), sem(c, "meta_turned")
        ps = c.psum
        block = ph.enter_context(nc.Block())

        @block.sync
        def _(sp):
            sp.dma_start(rows[:, :], meta).then_inc(loaded, 16)

        @block.tensor
        def _(pe):
            pe.wait_ge(loaded, 16)
            for k in range(KD):
                mm = nc.tensor.transpose(ps[:, 0, k * META:(k + 1) * META], rows[:, k * P:(k + 1) * P],
                                         c.ident[0:META, 0:META])
            mm.then_inc(turned, 1)

        @block.scalar
        def _(act):
            nc.scalar.copy(xm[:, :, META:TM], c.x_t[:, :, :])

        @block.vector
        def _(dve):
            dve.wait_ge(turned, 1)
            nc.vector.tensor_copy(xm[:, :, 0:META], ps[:, 0, 0:KD * META].rearrange("p (k t) -> p k t", k=KD))


class Decay:
    pass


def ssd_times(c, w_in, h, dec, conv_w, conv_dst):
    nc = c.nc
    NH = 32
    with ExitStack() as ph:
        sb = lambda name, shape, dt=F32: ph.enter_context(nc.sbuf_tensor(f"dt_{name}", shape, dt))
        w_raw = sb("w_raw", [P, KD, NH])
        w_hi = sb("w_hi", [P, KD, NH], F32R)
        w_lo = sb("w_lo", [P, KD, NH], F32R)
        v = sb("v", [P, TC + 1, NH])
        e = sb("e", [P, TC + 1, NH])
        a = sb("a", [P, NH])
        total = sb("total", [P, TC + 1, NH])
        loaded, conv_loaded, acts, steps, pe_done = (sem(c, f"dt_{n}") for n in
                                                     ("loaded", "conv_loaded", "acts", "steps", "pe_done"))
        ps = c.psum
        dt_ps = ps[:, 0, 0:(TC + 1) * NH].rearrange("p (t n) -> p t n", n=NH)
        sum_ps = ps[:, 1, 0:(TC + 1) * NH].rearrange("p (t n) -> p t n", n=NH)
        tot_ps = ps[:, 2, 0:(TC + 1) * NH].rearrange("p (t n) -> p t n", n=NH)
        block = ph.enter_context(nc.Block())
        x_ = slice(0, TC)

        @block.sync
        def _(sp):
            sp.dma_start(w_raw[:, :, :], w_in.rearrange("(k p) n -> p k n", p=P)[:, :, DT_AT:DT_AT + NH]
                         ).then_inc(loaded, 16)
            sp.dma_start(conv_dst[0][:, :, :], conv_w[0].rearrange("(k p) n -> p k n", p=P)).then_inc(conv_loaded, 16)
            sp.dma_start(conv_dst[1][:, :, :], conv_w[1].rearrange("(k p) n -> p k n", p=P)).then_inc(conv_loaded, 16)
            sp.wait_ge(conv_loaded, 32)

        @block.scalar
        def _(act):
            acted = [0]

            def does(after, *args, **kw):
                if after:
                    act.wait_ge(steps, after)
                nc.scalar.activation(*args, **kw).then_inc(acts, 1)
                acted[0] += 1
                act.wait_ge(acts, acted[0])

            act.wait_ge(loaded, 16)
            nc.scalar.copy(w_hi[:, :, :], w_raw[:, :, :]).then_inc(acts, 1)
            acted[0] = 1
            act.preload_act_table_set("natural_log_exp_and_others")
            does(0, a[:, :], row_of(c, "ssd_a_log"), ACT.Exp)
            does(2, e[:, :, :], v[:, :, :], ACT.Abs)
            does(0, e[:, :, :], e[:, :, :], ACT.Exp, scale=-1.0)
            does(0, e[:, :, :], e[:, :, :], ACT.Ln, bias=1.0)
            does(11, dec.from_start[:, :, :], dec.sums[:, x_, :], ACT.Exp)
            does(0, total[:, :, :], total[:, :, :], ACT.Exp)
            does(0, dec.whole[:, :, :], dec.whole[:, :, :], ACT.Exp)

        @block.vector
        def _(dve):
            n = [0]

            def step(ins):
                n[0] += 1
                ins.then_inc(steps, 1)
                dve.wait_ge(steps, n[0])

            V = nc.vector
            dve.wait_ge(acts, 1)
            step(V.tensor_tensor(w_lo[:, :, :], w_raw[:, :, :], w_hi[:, :, :].bitcast(F32), ALU.subtract))
            dve.wait_ge(pe_done, 1)
            bias = row_of(c, "ssd_dt_bias").unsqueeze(1).broadcast_to([P, TC + 1, NH])
            step(V.tensor_tensor(v[:, :, :], dt_ps, bias, ALU.add))
            dve.wait_ge(acts, 5)
            step(V.scalar_tensor_tensor(dec.dt[:, :, :], v[:, :, :], 0.0, e[:, :, :], ALU.max, ALU.add))
            step(V.tensor_scalar(a[:, :], a[:, :], -1.0, None, ALU.mult))
            step(V.tensor_tensor(dec.adt[:, :, :], dec.dt[:, :, :],
                                 a[:, :].unsqueeze(1).broadcast_to([P, TC + 1, NH]), ALU.mult))
            dve.wait_ge(pe_done, 2)
            step(V.tensor_copy(dec.sums[:, x_, :], sum_ps[:, x_, :]))
            step(V.tensor_copy(dec.sums[0:META, TC, :], sum_ps[0:META, TC, :]))
            step(V.tensor_copy(dec.whole[:, :, :], tot_ps[:, x_, :]))
            step(V.tensor_tensor(total[:, x_, :], tot_ps[:, x_, :], dec.sums[:, x_, :], ALU.subtract))
            step(V.memset(total[:, TC, :], 0.0))
            step(V.tensor_tensor(total[0:META, TC, :], tot_ps[0:META, TC, :], dec.sums[0:META, TC, :], ALU.subtract))
            dve.wait_ge(acts, 8)
            step(V.tensor_tensor(dec.dt_end[:, :, :], dec.dt[:, :, :], total[:, :, :], ALU.mult))

        @block.tensor
        def _(pe):
            pe.wait_ge(steps, 1)
            for t in range(TC + 1):
                tok = slice(META + t * P, META + (t + 1) * P) if t < TC else slice(0, P)
                mm = products(c, dt_ps[:, t, :], [
                    ((h[0][:, k, tok], h[1][:, k, tok]), (w_hi[:, k, :], w_lo[:, k, :])) for k in range(KD)])
            mm.then_inc(pe_done, 1)
            pe.wait_ge(steps, 5)
            for lhs, out in ((c.tri_up, sum_ps), (c.ones, tot_ps)):
                nc.tensor.matmul(out[:, x_, :], lhs[:, :], dec.adt[:, x_, :], start=True, stop=True)
                mm = nc.tensor.matmul(out[:, TC, :], lhs[0:META, :], dec.adt[0:META, TC, :], start=True, stop=True)
            mm.then_inc(pe_done, 1)


def ssd(c, w_in, h, dec, conv_w, y_t, following):
    nc = c.nc
    u0 = c.use
    with ExitStack() as ph:
        sb = lambda name, shape, dt=F32: ph.enter_context(nc.sbuf_tensor(f"ssd_{name}", shape, dt))
        raw = sb("raw", [P, 4, TAPS - 1 + TM])
        xbc = sb("xbc", [P, 4, TM])
        rows = sb("rows", [P, 2, 4 * P])
        meta_rows = sb("meta_rows", [P, 4 * P])
        meta_in = sb("meta_in", [META, G_COLS])
        gate = sb("gate", [P, TC, G_COLS])
        spread = sb("spread", [P, 2, G_HEADS, P])
        seg = sb("seg", [P, 2, G_HEADS, P])
        cb = sb("cb", [P, 2, P])
        x_dt = sb("x_dt", [P, 2, G_COLS])
        x_end = sb("x_end", [P, 2, G_COLS])
        skip = sb("skip", [P, 2, G_COLS])
        state = sb("state", [P, G_COLS])
        y = sb("y", [P, TC, G_COLS])
        y_sq = sb("y_sq", [P, G_COLS])
        mean = sb("mean", [P, TC])
        rstd = sb("rstd", [P, TC])
        power = sb("power", [P, TC])
        names = ("half_done raw_taken zeroed conv_step conv_done silu_done gate_taken turned rows_taken spread_done "
                 "sums_ready seg_sub seg_min decayed x_dt_done cb_done m_done x_end_done skip_done advanced state_kept "
                 "state_new y_off_in y_in y_skipped y_gated squared mean_done rooted y_normed y_turned y_taken").split()
        (half_done, raw_taken, zeroed, conv_step, conv_done, silu_done, gate_taken, turned, rows_taken, spread_done,
         sums_ready, seg_sub, seg_min, decayed, x_dt_done, cb_done, m_done, x_end_done, skip_done, advanced, state_kept,
         state_new, y_off_in, y_in, y_skipped, y_gated, squared, mean_done, rooted, y_normed, y_turned, y_taken) = (
             sem(c, f"ssd_{n}") for n in names)
        ps = c.psum
        chan_ps = ps[:, 0:2, 0:HALF_TM]
        gate_ps = ps[:, 2:4, :].rearrange("p b (t n) -> p (b t) n", t=2)
        rows_ps, sums_ps, y_ps, state_ps = ps[:, 4, :], ps[:, 5, :], ps[:, 6, :], ps[:, 7, 0:G_COLS]
        block = ph.enter_context(nc.Block())
        last = GROUPS - 1
        UA = lambda g: u0 + g * 2
        UB = lambda g: u0 + g * 2 + 1
        heads = lambda t: t.rearrange("p (r d) -> p r d", r=G_HEADS)
        wide = lambda t, n: t.unsqueeze(2).broadcast_to([t.shape[0], G_HEADS, n])

        def of_group(t, i):
            return t[:, bass.ds(i * G_HEADS, G_HEADS)]

        @block.sync
        def _(sp):
            def gates(g):
                for j in range(2):
                    load_tile(c, sp, UB(g), j, wide_parts(c, j, w_in, (g * 2 + j) * P + Z_AT, P))

            gates(0)
            with sp.Fori(1, GROUPS) as g:
                ssd_first(c, w_in, UA(g), g)(sp)
                gates(g)
            following(sp)

        @block.gpsimd
        def _(pool):
            pool.memset(raw[:, :, 0:TAPS - 1], 0.0).then_inc(zeroed, 1)
            pool.memset(power[:, :], -0.5).then_inc(zeroed, 1)
            pool.wait_ge(zeroed, 2)

            def apart():
                pool.wait_ge(zeroed, 2)

            def spread_dt(i, t):
                apart()
                if t >= 2:
                    pool.wait_ge(sums_ready, i * TC + t - 1)
                elif not (isinstance(i, int) and i == 0):
                    pool.wait_ge(sums_ready, i * TC + t - 1)
                pool.tensor_tensor(spread[:, t % 2], c.tri_up[:, :].unsqueeze(1).broadcast_to([P, G_HEADS, P]),
                                   wide(of_group(dec.adt[:, t, :], i), P), ALU.mult).then_inc(spread_done, 1)

            def body(i):
                spread_dt(i, 0)
                spread_dt(i, 1)
                apart()
                pool.wait_ge(rows_taken, i * 5 + 1)
                pool.tensor_tensor(heads(meta_in[:, :]), heads(meta_rows[0:META, 0:G_COLS]),
                                   wide(of_group(dec.dt_end[0:META, TC, :], i), HEAD), ALU.mult).then_inc(x_end_done, 1)
                for t in range(TC):
                    apart()
                    pool.wait_ge(rows_taken, i * 5 + t + 2)
                    if t >= 2:
                        pool.wait_ge(advanced, i * 5 + t)
                    pool.tensor_tensor(heads(x_end[:, t % 2, :]), heads(rows[:, t % 2, 0:G_COLS]),
                                       wide(of_group(dec.dt_end[:, t, :], i), HEAD), ALU.mult).then_inc(x_end_done, 1)
                    apart()
                    if t >= 2:
                        pool.wait_ge(y_skipped, i * TC + t - 1)
                    pool.tensor_tensor(heads(skip[:, t % 2, :]), heads(rows[:, t % 2, 0:G_COLS]),
                                       wide(of_group(row_of(c, "ssd_d"), i), HEAD), ALU.mult).then_inc(skip_done, 1)
                    if t < 2:
                        spread_dt(i, t + 2)
                pool.wait_ge(mean_done, i + 1)
                pool.tensor_tensor(rstd[:, :], mean[:, :], power[:, :], ALU.pow).then_inc(rooted, 1)

            body(0)
            with pool.Fori(1, GROUPS) as i:
                body(i)

        @block.scalar
        def _(act):
            def take(i, m, first=False):
                if m % 2 == 0:
                    act.wait_ge(half_done, i * 2 + m // 2 + 1)
                else:
                    act.wait_ge(c.tile_used, 2 * UA(i) + 3 + m // 2)
                if not first:
                    act.wait_ge(conv_done, i * 4 + m - 3)
                nc.scalar.copy(raw[:, m, TAPS - 1:].rearrange("p (b n) -> p b n", b=2), chan_ps).then_inc(raw_taken, 1)

            def silu(i, m):
                chunk = (i * 2, i * 2 + 1, i + SSD_IN // P, i + (SSD_IN + D) // P)[m]
                act.wait_ge(conv_done, i * 4 + m + 1)
                at = vec_at("ssd_conv_b")
                nc.scalar.activation(xbc[:, m, :], xbc[:, m, :], ACT.Silu,
                                     bias=c.vec[:, bass.ds(chunk + at, 1)]).then_inc(silu_done, 1)

            def copy_rows(i, t):
                act.wait_ge(turned, i * 5 + t + 2)
                if t >= 2:
                    act.wait_ge(advanced, i * 5 + t)
                    act.wait_ge(skip_done, i * TC + t - 1)
                nc.scalar.copy(rows[:, t % 2, :], rows_ps).then_inc(rows_taken, 1)

            def decay(i, t):
                act.wait_ge(seg_min, i * TC + t + 1)
                nc.scalar.activation(seg[:, t % 2], seg[:, t % 2], ACT.Exp).then_inc(decayed, 1)

            def square(i, t):
                act.wait_ge(y_gated, i * TC + t + 1)
                if t or not (isinstance(i, int) and i == 0):
                    act.wait_ge(squared, i * TC + t)
                nc.scalar.activation(y_sq[:, :], y[:, t, :], ACT.Square, accum_out=mean[:, t:t + 1]
                                     ).then_inc(squared, 1)

            def body(i, more, more2):
                act.wait_ge(c.tile_used, 2 * UB(i) + 4)
                nc.scalar.activation(gate[:, :, :], gate_ps, ACT.Silu).then_inc(gate_taken, 1)
                silu(i, 0)
                if more:
                    take(i + 1, 0)
                silu(i, 1)
                silu(i, 2)
                if more:
                    take(i + 1, 1)
                    split_hi(c, act, UB(i + 1), 0, KD * P)
                silu(i, 3)
                act.wait_ge(turned, i * 5 + 1)
                nc.scalar.copy(meta_rows[:, :], rows_ps).then_inc(rows_taken, 1)
                copy_rows(i, 0)
                decay(i, 0)
                copy_rows(i, 1)
                decay(i, 1)
                square(i, 0)
                if more:
                    take(i + 1, 2)
                copy_rows(i, 2)
                decay(i, 2)
                square(i, 1)
                if more:
                    take(i + 1, 3)
                    split_hi(c, act, UB(i + 1), 1, KD * P)
                copy_rows(i, 3)
                decay(i, 3)
                square(i, 2)
                if more2:
                    split_hi(c, act, UA(i + 2), 0)
                square(i, 3)
                if more2:
                    split_hi(c, act, UA(i + 2), 1)

            act.wait_ge(zeroed, 2)
            for j in range(2):
                split_hi(c, act, UA(0), j)
            take(0, 0, True)
            take(0, 1, True)
            split_hi(c, act, UB(0), 0, KD * P)
            take(0, 2, True)
            take(0, 3, True)
            split_hi(c, act, UB(0), 1, KD * P)
            for j in range(2):
                split_hi(c, act, UA(1), j)
            body(0, True, True)
            with act.Fori(1, last - 1) as i:
                body(i, True, True)
            body(last - 1, True, False)
            body(last, False, False)

        @block.vector
        def _(dve):
            V = nc.vector

            def conv(i, m):
                chunk = (i * 2, i * 2 + 1, i + SSD_IN // P, i + (SSD_IN + D) // P)[m]
                tap = lambda k: conv_w[:, bass.ds(chunk, 1), k]
                dve.wait_ge(raw_taken, i * 4 + m + 1)
                V.tensor_scalar(xbc[:, m, :], raw[:, m, 0:TM], tap(0), None, ALU.mult).then_inc(conv_step, 1)
                for k in range(1, TAPS):
                    dve.wait_ge(conv_step, i * 12 + m * 3 + k)
                    V.scalar_tensor_tensor(xbc[:, m, :], raw[:, m, k:k + TM], tap(k), xbc[:, m, :], ALU.mult,
                                           ALU.add).then_inc(conv_step if k < TAPS - 1 else conv_done, 1)

            def pre(i, t):
                p, n = t % 2, i * TC + t
                later = not (isinstance(i, int) and i == 0 and t < 2)
                dve.wait_ge(sums_ready, n + 1)
                if later:
                    dve.wait_ge(advanced, i * 5 + (t if t >= 2 else t - 1))
                V.tensor_tensor(seg[:, p], sums_ps.rearrange("p (r l) -> p r l", r=G_HEADS),
                                wide(of_group(dec.sums[:, t, :], i), P), ALU.subtract).then_inc(seg_sub, 1)
                dve.wait_ge(seg_sub, n + 1)
                V.tensor_scalar(seg[:, p], seg[:, p], 0.0, None, ALU.min).then_inc(seg_min, 1)
                dve.wait_ge(rows_taken, i * 5 + t + 2)
                V.tensor_tensor(heads(x_dt[:, p, :]), heads(rows[:, p, 0:G_COLS]),
                                wide(of_group(dec.dt[:, t, :], i), HEAD), ALU.mult).then_inc(x_dt_done, 1)
                V.tensor_tensor(cb[:, p, :], rows[:, p, 3 * P:4 * P], c.tri_up[:, :], ALU.mult).then_inc(cb_done, 1)
                dve.wait_ge(cb_done, n + 1)
                dve.wait_ge(decayed, n + 1)
                V.tensor_tensor(seg[:, p], seg[:, p], cb[:, p, :].unsqueeze(1).broadcast_to([P, G_HEADS, P]),
                                ALU.mult).then_inc(m_done, 1)

            def post(i, t):
                p, n = t % 2, i * TC + t
                dve.wait_ge(advanced, i * 5 + t + 2)
                V.tensor_tensor(heads(state[:, :]), heads(state[:, :]), wide(of_group(dec.whole[:, t, :], i), HEAD),
                                ALU.mult).then_inc(state_kept, 1)
                V.tensor_tensor(heads(y[:, t, :]), heads(y_ps[:, G_COLS:]),
                                wide(of_group(dec.from_start[:, t, :], i), HEAD), ALU.mult).then_inc(y_off_in, 1)
                dve.wait_ge(state_kept, n + 1)
                V.tensor_tensor(state[:, :], state[:, :], state_ps, ALU.add).then_inc(state_new, 1)
                dve.wait_ge(y_off_in, n + 1)
                V.tensor_tensor(y[:, t, :], y[:, t, :], y_ps[:, 0:G_COLS], ALU.add).then_inc(y_in, 1)
                dve.wait_ge(skip_done, n + 1)
                dve.wait_ge(y_in, n + 1)
                V.tensor_tensor(y[:, t, :], y[:, t, :], skip[:, p, :], ALU.add).then_inc(y_skipped, 1)
                dve.wait_ge(y_skipped, n + 1)
                dve.wait_ge(gate_taken, i + 1)
                V.tensor_tensor(y[:, t, :], y[:, t, :], gate[:, t, :], ALU.mult).then_inc(y_gated, 1)

            def body(i, more, more2):
                for m in range(4):
                    conv(i, m)
                if more:
                    split_lo(c, dve, UB(i + 1), 0, KD * P)
                dve.wait_ge(advanced, i * 5 + 1)
                V.tensor_copy(state[:, :], state_ps).then_inc(state_new, 1)
                pre(i, 0)
                pre(i, 1)
                post(i, 0)
                pre(i, 2)
                post(i, 1)
                if more:
                    split_lo(c, dve, UB(i + 1), 1, KD * P)
                pre(i, 3)
                post(i, 2)
                if more2:
                    split_lo(c, dve, UA(i + 2), 0)
                post(i, 3)
                dve.wait_ge(squared, i * TC + TC)
                V.tensor_scalar(mean[:, :], mean[:, :], 1.0 / G_COLS, EPS, ALU.mult, ALU.add).then_inc(mean_done, 1)
                if more2:
                    split_lo(c, dve, UA(i + 2), 1)
                dve.wait_ge(rooted, i + 1)
                dve.wait_ge(y_gated, i * TC + TC)
                V.tensor_tensor(y[:, :, :], y[:, :, :], rstd[:, :].unsqueeze(2).broadcast_to([P, TC, G_COLS]),
                                ALU.mult).then_inc(y_normed, 1)
                dve.wait_ge(y_turned, i + 1)
                for j in range(2):
                    V.tensor_scalar(y_t[:, bass.ds(i * 2 + j, 1), :].rearrange("p k t -> p (k t)"), ps[:, 6 + j, :],
                                    c.vec[:, bass.ds(i * 2 + j + vec_at("ssd_norm"), 1)], None, ALU.mult).then_inc(y_taken, 1)

            for u, j, cols in ((UA(0), 0, TILE), (UA(0), 1, TILE), (UB(0), 0, KD * P), (UB(0), 1, KD * P),
                               (UA(1), 0, TILE), (UA(1), 1, TILE)):
                split_lo(c, dve, u, j, cols)
            body(0, True, True)
            with dve.Fori(1, last - 1) as i:
                body(i, True, True)
            body(last - 1, True, False)
            body(last, False, False)

        @block.tensor
        def _(pe):
            def channels(i, m):
                j = m // 2
                if m % 2 == 0:
                    wait_tile(c, pe, UA(i), j)
                if not (isinstance(i, int) and i == 0 and m == 0):
                    pe.wait_ge(raw_taken, i * 4 + m)
                if j == 0:
                    w_hi, w_lo = (t[:, :, (m % 2) * P:(m % 2 + 1) * P] for t in w_tile(c, 0, KD, 256))
                else:
                    w_hi, w_lo = (part[:, 1, :].rearrange("p (j k n) -> p j k n", j=2, k=KD)[:, m % 2]
                                  for part in (c.hi, c.lo))
                for b in range(2):
                    tok = slice(b * HALF_TM, (b + 1) * HALF_TM)
                    mm = products(c, chan_ps[:, b, :], [
                        ((w_hi[:, k, :], w_lo[:, k, :]), (h[0][:, k, tok], h[1][:, k, tok])) for k in range(KD)])
                mm.then_inc(c.tile_used if m % 2 else half_done, 1)

            def gates(i, j):
                wait_tile(c, pe, UB(i), j)
                if not (isinstance(i, int) and i == 0):
                    pe.wait_ge(gate_taken, i)
                w_hi, w_lo = w_tile(c, j, KD, P)
                for t in range(TC):
                    tok = slice(META + t * P, META + (t + 1) * P)
                    mm = products(c, gate_ps[:, t, j * P:(j + 1) * P], [
                        ((h[0][:, k, tok], h[1][:, k, tok]), (w_hi[:, k, :], w_lo[:, k, :])) for k in range(KD)])
                mm.then_inc(c.tile_used, 1)

            def turn(tok, score):
                for m in range(3):
                    mm = nc.tensor.transpose(rows_ps[:, m * P:(m + 1) * P], xbc[:, m, tok], c.ident[:, :])
                return nc.tensor.matmul(rows_ps[:, 3 * P:4 * P], xbc[:, 2, tok], xbc[:, 3, tok], start=True, stop=True)

            def first_half(i, t):
                pe.wait_ge(rows_taken, i * 5 + t + 1)
                turn(slice(META + t * P, META + (t + 1) * P), True).then_inc(turned, 1)
                pe.wait_ge(spread_done, i * TC + t + 1)
                if not (isinstance(i, int) and i == 0 and t == 0):
                    pe.wait_ge(seg_sub, i * TC + t)
                nc.tensor.matmul(sums_ps, c.ones[:, :], spread[:, t % 2].rearrange("p r l -> p (r l)"), start=True,
                                 stop=True).then_inc(sums_ready, 1)

            def second_half(i, t):
                p = t % 2
                pe.wait_ge(x_end_done, i * 5 + t + 2)
                pe.wait_ge(m_done, i * TC + t + 1)
                pe.wait_ge(state_new, i * 5 + t + 1)
                if t:
                    pe.wait_ge(y_in, i * TC + t)
                for r in range(G_HEADS):
                    nc.tensor.matmul(y_ps[:, r * HEAD:(r + 1) * HEAD], seg[:, p, r, :],
                                     x_dt[:, p, r * HEAD:(r + 1) * HEAD], start=True, stop=True)
                nc.tensor.matmul(y_ps[:, G_COLS:], xbc[:, 3, META + t * P:META + (t + 1) * P], state[:, :], start=True,
                                 stop=True)
                nc.tensor.matmul(state_ps, rows[:, p, 2 * P:3 * P], x_end[:, p, :], start=True,
                                 stop=True).then_inc(advanced, 1)

            def body(i, more):
                if more:
                    channels(i + 1, 0)
                    channels(i + 1, 1)
                pe.wait_ge(silu_done, i * 4 + 4)
                if not (isinstance(i, int) and i == 0):
                    pe.wait_ge(rows_taken, i * 5)
                turn(slice(0, P), False).then_inc(turned, 1)
                pe.wait_ge(x_end_done, i * 5 + 1)
                if not (isinstance(i, int) and i == 0):
                    pe.wait_ge(y_taken, i * 2)
                nc.tensor.matmul(state_ps, meta_rows[0:META, 2 * P:3 * P], meta_in[:, :], start=True,
                                 stop=True).then_inc(advanced, 1)
                first_half(i, 0)
                first_half(i, 1)
                second_half(i, 0)
                if more:
                    channels(i + 1, 2)
                first_half(i, 2)
                second_half(i, 1)
                if more:
                    channels(i + 1, 3)
                first_half(i, 3)
                second_half(i, 2)
                if more:
                    gates(i + 1, 0)
                second_half(i, 3)
                if more:
                    gates(i + 1, 1)
                pe.wait_ge(y_normed, i + 1)
                for j in range(2):
                    for t in range(TC):
                        mm = nc.tensor.transpose(ps[:, 6 + j, t * P:(t + 1) * P], y[:, t, j * P:(j + 1) * P],
                                                 c.ident[:, :])
                mm.then_inc(y_turned, 1)

            for m in range(4):
                channels(0, m)
            for j in range(2):
                gates(0, j)
            body(0, True)
            with pe.Fori(1, last) as i:
                body(i, True)
            body(last, False)
    c.use = u0 + 2 * GROUPS


def rows_first(c, w, use):
    def go(sp):
        for j in range(2):
            load_tile(c, sp, use, j, tall_parts(c, j, w, 0, 16, j * P))
    return go


def ssd_out(c, w, y, out, following):
    nc = c.nc
    u0 = c.use
    pairs = KD // 2
    with ExitStack() as ph:
        taken = sem(c, "so_taken")
        ps = c.psum
        block = ph.enter_context(nc.Block())

        @block.sync
        def _(sp):
            with sp.Fori(1, pairs) as i:
                for j in range(2):
                    load_tile(c, sp, u0 + i, j, tall_parts(c, j, w, 0, 16, (i * 2 + j) * P))
            following(sp)

        @block.scalar
        def _(act):
            with act.Fori(0, pairs) as i:
                for j in range(2):
                    split_hi(c, act, u0 + i, j)

        @block.vector
        def _(dve):
            dve.sem_inc(taken, 2)
            for j in range(2):
                split_lo(c, dve, u0, j)

            def take(i, j):
                dve.wait_ge(c.tile_used, 2 * (u0 + i) + j + 3)
                nc.vector.tensor_copy(out[:, bass.ds(i * 2 + j, 1), :].rearrange("p k t -> p (k t)"), ps[:, j, :]
                                      ).then_inc(taken, 1)

            with dve.Fori(0, pairs - 1) as i:
                for j in range(2):
                    take(i, j)
                    split_lo(c, dve, u0 + i + 1, j)
            for j in range(2):
                take(pairs - 1, j)

        @block.tensor
        def _(pe):
            with pe.Fori(0, pairs) as i:
                for j in range(2):
                    wait_tile(c, pe, u0 + i, j)
                    pe.wait_ge(taken, i * 2 + j + 1)
                    w_hi, w_lo = w_tile(c, j, 16, P)
                    products(c, ps[:, j, :], [((w_hi[:, k, :], w_lo[:, k, :]), (y[0][:, k, :], y[1][:, k, :]))
                                              for k in range(16)]).then_inc(c.tile_used, 1)
    c.use = u0 + pairs


def sc_parts(c, w_in, slot, n):
    if slot == 0:
        return pair_parts(c, 0, w_in, n * P + SC_AT, n * P + SX_AT)
    return wide_parts(c, 1, w_in, n * P + SB_AT, P)


def sc_first(c, w_in, use):
    def go(sp):
        for j in range(2):
            load_tile(c, sp, use, j, sc_parts(c, w_in, j, 0))
    return go


def short_conv(c, w_in, h, conv_w, out, following):
    nc = c.nc
    u0 = c.use
    taps = 3
    with ExitStack() as ph:
        sb = lambda name, shape, dt=F32: ph.enter_context(nc.sbuf_tensor(f"sc_{name}", shape, dt))
        x = sb("x", [P, TM])
        prod = sb("prod", [P, taps - 1 + TM])
        conv = sb("conv", [P, T])
        zeroed, c_done, x_done, x_taken, prod_done, conv_step, out_done = (sem(c, f"sc_{n}") for n in (
            "zeroed", "c_done", "x_done", "x_taken", "prod_done", "conv_step", "out_done"))
        ps = c.psum
        block = ph.enter_context(nc.Block())

        @block.gpsimd
        def _(pool):
            pool.memset(prod[:, 0:taps - 1], 0.0).then_inc(zeroed, 1)

        @block.sync
        def _(sp):
            with sp.Fori(1, KD) as n:
                for j in range(2):
                    load_tile(c, sp, u0 + n, j, sc_parts(c, w_in, j, n))
            following(sp)

        @block.scalar
        def _(act):
            def split(n):
                split_hi(c, act, u0 + n, 0)
                split_hi(c, act, u0 + n, 1, KD * P)

            def take(n):
                act.wait_ge(c.tile_used, 2 * (u0 + n) + 3)
                act.wait_ge(prod_done, n + 1)
                nc.scalar.copy(x[:, :].rearrange("p (b n) -> p b n", b=2), ps[:, 2:4, 0:HALF_TM]).then_inc(x_taken, 1)

            split(0)
            with act.Fori(0, KD - 1) as n:
                take(n)
                split(n + 1)
            take(KD - 1)

        @block.vector
        def _(dve):
            def split(n):
                split_lo(c, dve, u0 + n, 0)
                split_lo(c, dve, u0 + n, 1, KD * P)

            def convolve(n, more):
                tap = lambda k: conv_w[:, bass.ds(n, 1), k]
                dve.wait_ge(x_taken, n + 1)
                nc.vector.tensor_tensor(prod[:, taps - 1:].rearrange("p (b n) -> p b n", b=2),
                                        x[:, :].rearrange("p (b n) -> p b n", b=2), ps[:, 0:2, 0:HALF_TM],
                                        ALU.mult).then_inc(prod_done, 1)
                if more:
                    split(n + 1)
                dve.wait_ge(prod_done, n + 2)
                nc.vector.tensor_scalar(conv[:, :], prod[:, META:META + T], tap(0), None, ALU.mult
                                        ).then_inc(conv_step, 1)
                for k in range(1, taps):
                    dve.wait_ge(conv_step, n * 3 + k)
                    nc.vector.scalar_tensor_tensor(conv[:, :], prod[:, META + k:META + k + T], tap(k), conv[:, :],
                                                   ALU.mult, ALU.add).then_inc(conv_step, 1)
                dve.wait_ge(conv_step, n * 3 + 3)
                dve.wait_ge(c.tile_used, 2 * (u0 + n) + 4)
                nc.vector.tensor_tensor(out[:, bass.ds(n, 1), :].rearrange("p k t -> p (k t)"), conv[:, :],
                                        ps[:, 4, :], ALU.mult).then_inc(out_done, 1)

            dve.sem_inc(prod_done, 1)
            dve.sem_inc(out_done, 1)
            split(0)
            dve.wait_ge(zeroed, 1)
            with dve.Fori(0, KD - 1) as n:
                convolve(n, True)
            convolve(KD - 1, False)

        @block.tensor
        def _(pe):
            with pe.Fori(0, KD) as n:
                wait_tile(c, pe, u0 + n, 0)
                pe.wait_ge(prod_done, n + 1)
                for m in range(2):
                    w_hi, w_lo = (part[:, 0, :].rearrange("p (j k n) -> p j k n", j=2, k=KD)[:, m]
                                  for part in (c.hi, c.lo))
                    for b in range(2):
                        tok = slice(b * HALF_TM, (b + 1) * HALF_TM)
                        mm = products(c, ps[:, 2 * m + b, 0:HALF_TM], [
                            ((w_hi[:, k, :], w_lo[:, k, :]), (h[0][:, k, tok], h[1][:, k, tok])) for k in range(KD)])
                mm.then_inc(c.tile_used, 1)
                wait_tile(c, pe, u0 + n, 1)
                pe.wait_ge(out_done, n + 1)
                w_hi, w_lo = w_tile(c, 1, KD, P)
                products(c, ps[:, 4, :], [((w_hi[:, k, :], w_lo[:, k, :]), (h[0][:, k, META:TM], h[1][:, k, META:TM]))
                                          for k in range(KD)]).then_inc(c.tile_used, 1)
    c.use = u0 + KD


def gate_parts(c, w_in, slot, i):
    return wide_parts(c, slot, w_in, i * 256 + GATE_AT + slot * D)


def gate_first(c, w_in, use):
    def go(sp):
        for j in range(2):
            load_tile(c, sp, use, j, gate_parts(c, w_in, j, 0))
    return go


def merge(c, w_in, h, branches, following):
    nc = c.nc
    u0 = c.use
    pairs = D // 256
    with ExitStack() as ph:
        gate = ph.enter_context(nc.sbuf_tensor("mg_gate", [P, 2, 2, T], F32))
        gate_done, gated, merged = (sem(c, f"mg_{n}") for n in ("gate_done", "gated", "merged"))
        ps = c.psum
        block = ph.enter_context(nc.Block())

        @block.sync
        def _(sp):
            with sp.Fori(1, pairs) as i:
                for j in range(2):
                    load_tile(c, sp, u0 + i, j, gate_parts(c, w_in, j, i))
            following(sp)

        @block.scalar
        def _(act):
            def sigmoid(i, j):
                act.wait_ge(c.tile_used, 2 * (u0 + i) + j + 3)
                act.wait_ge(gated, i * 2 + j + 1)
                nc.scalar.activation(gate[:, j], ps[:, 2 * j:2 * j + 2, :], ACT.Sigmoid).then_inc(gate_done, 1)

            for j in range(2):
                split_hi(c, act, u0, j)
            with act.Fori(0, pairs - 1) as i:
                for j in range(2):
                    sigmoid(i, j)
                    split_hi(c, act, u0 + i + 1, j)
            for j in range(2):
                sigmoid(pairs - 1, j)

        @block.vector
        def _(dve):
            def apply(i, j):
                part = branches[j][:, bass.ds(i * 2, 2), :]
                dve.wait_ge(gate_done, i * 2 + j + 1)
                nc.vector.tensor_tensor(part, part, gate[:, j], ALU.mult).then_inc(gated, 1)

            def add(i):
                first, second = (t[:, bass.ds(i * 2, 2), :] for t in branches)
                dve.wait_ge(gated, i * 2 + 4)
                nc.vector.tensor_tensor(first, first, second, ALU.add).then_inc(merged, 1)

            dve.sem_inc(gated, 2)
            for j in range(2):
                split_lo(c, dve, u0, j)
            with dve.Fori(0, pairs - 1) as i:
                for j in range(2):
                    apply(i, j)
                    split_lo(c, dve, u0 + i + 1, j)
                add(i)
            for j in range(2):
                apply(pairs - 1, j)
            add(pairs - 1)

        @block.tensor
        def _(pe):
            with pe.Fori(0, pairs) as i:
                for j in range(2):
                    wait_tile(c, pe, u0 + i, j)
                    pe.wait_ge(gated, i * 2 + j + 1)
                    w_hi, w_lo = w_tile(c, j, KD, 256)
                    for n in range(2):
                        col = slice(n * P, (n + 1) * P)
                        mm = products(c, ps[:, 2 * j + n, :], [
                            ((w_hi[:, k, col], w_lo[:, k, col]), (h[0][:, k, META:TM], h[1][:, k, META:TM]))
                            for k in range(KD)])
                    mm.then_inc(c.tile_used, 1)
    c.use = u0 + pairs


NH = 8
KEYS = 128
TOP = 16
SLOTS = NH * TOP
LOW = -3e38
TG = 64
N_TG = T // TG
PART = 16
N_PARTS = KEYS // PART


class Steps:

    def __init__(self, eng, handle, turn, per):
        self.eng, self.handle, self.turn, self.per, self.n = eng, handle, turn, per, 0

    def __call__(self, ins):
        self.n += 1
        ins.then_inc(self.handle, 1)
        self.eng.wait_ge(self.handle, self.turn * self.per + self.n)


def peer_queries(c, w_q, sub_keys, h, values, places, following):
    nc = c.nc
    u0 = c.use
    units = 2 * TC
    with ExitStack() as ph:
        sb = lambda name, shape, dt=F32: ph.enter_context(nc.sbuf_tensor(f"pq_{name}", shape, dt))
        keys = sb("keys", [P, 2, 2, P])
        keys_t = sb("keys_t", [P, 2, 2, P])
        q = sb("q", [P, 2, 2, T])
        s = sb("s", [P, 2, units, KEYS])
        rest = sb("rest", [P, units, KEYS])
        val = sb("val", [P, 2, units, TOP])
        idx = sb("idx", [P, 2, units, TOP], U32)
        pad = sb("pad", [P, 1])
        keys_loaded = [sem(c, f"pq_keys_loaded{j}") for j in range(2)]
        q_taken, keys_turned, keys_taken, scored, s_taken, topped, indexed, cut, stored = (
            sem(c, f"pq_{n}") for n in ("q_taken", "keys_turned", "keys_taken", "scored", "s_taken",
                                        "topped", "indexed", "cut", "stored"))
        ps = c.psum
        keys_ps = ps[:, 4, 0:2 * P]
        s_ps = ps[:, 5:7, :].rearrange("p b n -> p (b n)")
        block = ph.enter_context(nc.Block())

        @block.sync
        def _(sp):
            def keys_of(i, j):
                sp.wait_ge(c.begun, 1)
                sp.wait_ge(keys_turned, i * 2 + j + 1)
                sp.dma_start(keys[:, j], sub_keys[bass.ds((i * 2 + j), 1)].rearrange("h j k d -> k (h j) d")
                             ).then_inc(keys_loaded[j], 16)

            for j in range(2):
                keys_of(0, j)
            with sp.Fori(1, NH // 2) as i:
                for j in range(2):
                    load_tile(c, sp, u0 + i, j, wide_parts(c, j, w_q, (i * 2 + j) * 256))
                    keys_of(i, j)
            following(sp)

        @block.scalar
        def _(act):
            def head(i, j):
                n = i * 2 + j
                act.wait_ge(c.tile_used, 2 * (u0 + i) + j + 3)
                act.wait_ge(scored, n + 1)
                nc.scalar.copy(q[:, j], ps[:, 2 * j:2 * j + 2, :]).then_inc(q_taken, 1)
                act.wait_ge(keys_turned, n + 3)
                nc.scalar.copy(keys_t[:, j].rearrange("p j k -> p (j k)"), keys_ps).then_inc(keys_taken, 1)

            def scores(i, j):
                n = i * 2 + j
                act.wait_ge(scored, n + 3)
                act.wait_ge(stored, n + 1)
                nc.scalar.copy(s[:, j].rearrange("p u k -> p (u k)"), s_ps).then_inc(s_taken, 1)

            for j in range(2):
                split_hi(c, act, u0, j)
            with act.Fori(0, NH // 2 - 1) as i:
                for j in range(2):
                    head(i, j)
                    split_hi(c, act, u0 + i + 1, j)
                    scores(i, j)
            for j in range(2):
                head(NH // 2 - 1, j)
                scores(NH // 2 - 1, j)

        @block.vector
        def _(dve):
            V = nc.vector

            def rank(i, j):
                n = i * 2 + j

                def wait(handle, value):
                    dve.wait_ge(handle, value)
                    V.memset(pad[:, :], 0.0)

                wait(s_taken, n + 1)
                for half in range(2):
                    src = s[:, j] if half == 0 else rest
                    part = slice(half * 8, half * 8 + 8)
                    if half:
                        wait(cut, (n + 1) * units)
                    for u in range(units):
                        V.max(val[:, j, u, part], src[:, u, :]).then_inc(topped, 1)
                    wait(topped, (n * 2 + half + 1) * units)
                    for u in range(units):
                        V.max_index(idx[:, j, u, part], val[:, j, u, part], src[:, u, :]).then_inc(indexed, 1)
                    if half == 0:
                        for u in range(units):
                            V.match_replace(rest[:, u, :], val[:, j, u, part], src[:, u, :], LOW).then_inc(cut, 1)
                V.tensor_copy(values[:, bass.ds(n, 1)].rearrange("p h u k -> p (h u k)"),
                              val[:, j].rearrange("p u k -> p (u k)"))
                dve.wait_ge(indexed, (n * 2 + 2) * units)
                V.tensor_copy(places[:, bass.ds(n, 1)].rearrange("p h u k -> p (h u k)"),
                              idx[:, j].rearrange("p u k -> p (u k)")).then_inc(stored, 1)

            dve.sem_inc(stored, 2)
            for j in range(2):
                split_lo(c, dve, u0, j)
            with dve.Fori(0, NH // 2 - 1) as i:
                for j in range(2):
                    split_lo(c, dve, u0 + i + 1, j)
                    rank(i, j)
            for j in range(2):
                rank(NH // 2 - 1, j)

        @block.tensor
        def _(pe):
            def queries(i, j):
                n = i * 2 + j
                wait_tile(c, pe, u0 + i, j)
                if not (isinstance(i, int) and i == 0):
                    pe.wait_ge(q_taken, n - 1)
                w_hi, w_lo = w_tile(c, j, KD, 256)
                for m in range(2):
                    col = slice(m * P, (m + 1) * P)
                    mm = products(c, ps[:, 2 * j + m, :], [
                        ((w_hi[:, k, col], w_lo[:, k, col]), (h[0][:, k, :], h[1][:, k, :])) for k in range(KD)])
                mm.then_inc(c.tile_used, 1)
                pe.wait_ge(keys_loaded[j], i * 16 + 16)
                if not (isinstance(i, int) and i == 0 and j == 0):
                    pe.wait_ge(keys_taken, n)
                for m in range(2):
                    mm = nc.tensor.transpose(keys_ps[:, m * P:(m + 1) * P], keys[:, j, m, :], c.ident[:, :])
                mm.then_inc(keys_turned, 1)

            def scores(n, j):
                pe.wait_ge(q_taken, n + 1)
                pe.wait_ge(keys_taken, n + 1)
                if not (isinstance(n, int) and n == 0):
                    pe.wait_ge(s_taken, n)
                for m in range(2):
                    for t in range(TC):
                        u = m * TC + t
                        mm = nc.tensor.matmul(s_ps[:, u * KEYS:(u + 1) * KEYS], q[:, j, m, t * P:(t + 1) * P],
                                              keys_t[:, j, m, :], start=True, stop=True)
                mm.then_inc(scored, 1)

            pe.sem_inc(keys_turned, 2)
            pe.sem_inc(scored, 2)
            queries(0, 0)
            queries(0, 1)
            scores(0, 0)
            with pe.Fori(1, NH // 2) as i:
                queries(i, 0)
                scores(i * 2 - 1, 1)
                queries(i, 1)
                scores(i * 2, 0)
            scores(NH - 1, 1)
    c.use = u0 + NH // 2


def peer_choose(c, values, places, chosen):
    nc = c.nc
    with ExitStack() as ph:
        sb = lambda name, shape, dt=F32: ph.enter_context(nc.sbuf_tensor(f"pc_{name}", shape, dt))
        pad = sb("pad", [P, 1])
        cand = sb("cand", [P, NH, TOP * TOP])
        rest = sb("rest", [P, NH, TOP * TOP])
        hot = sb("hot", [P, SLOTS, TOP])
        val = sb("val", [P, NH, TOP])
        idx = sb("idx", [P, NH, TOP], U32)
        digit = sb("digit", [P, 2, SLOTS], U32)
        digit_f = sb("digit_f", [P, 2, SLOTS])
        total = sb("total", [P, NH])
        rows = sb("rows", [P, 3, SLOTS])
        steps, shifted, weighed, chosen_done, turned, taken = (
            sem(c, f"pc_{n}") for n in ("steps", "shifted", "weighed", "chosen_done", "turned", "taken"))
        ps = c.psum
        block = ph.enter_context(nc.Block())
        PER = 6 + 4 + 6

        @block.vector
        def _(dve):
            V = nc.vector
            with dve.Fori(0, TC) as t:
                step = Steps(dve, steps, t, PER)

                def settle(ins):
                    step(ins)
                    V.memset(pad[:, :], 0.0)

                of = lambda x, half: x[:, :, bass.ds(t + half * TC, 1), :].rearrange("p h u k -> p h (u k)")
                first = of(values, 0).unsqueeze(3).broadcast_to([P, NH, TOP, TOP])
                second = of(values, 1).unsqueeze(2).broadcast_to([P, NH, TOP, TOP])
                settle(V.tensor_tensor(cand[:, :, :].rearrange("p h (a b) -> p h a b", a=TOP), first, second, ALU.add))
                for half in range(2):
                    src, part = (cand, rest)[half], slice(half * 8, half * 8 + 8)
                    for n in range(NH):
                        ins = V.max(val[:, n, part], src[:, n, :])
                    settle(ins)
                    for n in range(NH):
                        ins = V.max_index(idx[:, n, part], val[:, n, part], src[:, n, :])
                    settle(ins)
                    if half == 0:
                        for n in range(NH):
                            ins = V.match_replace(rest[:, n, :], val[:, n, part], src[:, n, :], LOW)
                        settle(ins)
                weight = rows[:, 2, :].rearrange("p (h k) -> p h k", h=NH)
                dve.wait_ge(turned, t + 1)
                V.tensor_tensor(weight, val[:, :, :], val[:, :, 0:1].broadcast_to([P, NH, TOP]), ALU.subtract
                                ).then_inc(shifted, 1)
                flat = idx[:, :, :].rearrange("p h k -> p (h k)")
                V.tensor_scalar(digit[:, 0, :], flat, 4, None, ALU.logical_shift_right)
                step(V.tensor_scalar(digit[:, 1, :], flat, 15, None, ALU.bitwise_and))
                step(V.tensor_copy(digit_f[:, :, :], digit[:, :, :]))
                dve.wait_ge(weighed, t + 1)
                step(V.tensor_reduce(total[:, :], weight, AX, ALU.add))
                step(V.reciprocal(total[:, :], total[:, :]))
                for half in range(2):
                    step(V.tensor_tensor(hot[:, :, :], digit_f[:, half, :].unsqueeze(2).broadcast_to([P, SLOTS, TOP]),
                                         c.iota[:, 0:TOP].unsqueeze(1).broadcast_to([P, SLOTS, TOP]), ALU.is_equal))
                    hot4 = hot[:, :, :].rearrange("p (h k) a -> p h k a", h=NH)
                    step(V.tensor_tensor(hot4, hot4, of(places, half).unsqueeze(2).broadcast_to([P, NH, TOP, TOP]),
                                         ALU.mult))
                    step(V.tensor_reduce(rows[:, half, :], hot[:, :, :], AX, ALU.add))
                V.tensor_tensor(weight, weight, total[:, :].unsqueeze(2).broadcast_to([P, NH, TOP]), ALU.mult
                                ).then_inc(chosen_done, 1)
                dve.wait_ge(turned, t + 2)
                V.tensor_copy(chosen[:, :, bass.ds(t * P, P)], ps[:, 0, 0:3 * P].rearrange("p (r t) -> p r t", r=3)
                              ).then_inc(taken, 1)
                assert step.n == PER

        @block.scalar
        def _(act):
            with act.Fori(0, TC) as t:
                act.wait_ge(shifted, t + 1)
                nc.scalar.activation(rows[:, 2, :], rows[:, 2, :], ACT.Exp).then_inc(weighed, 1)

        @block.tensor
        def _(pe):
            pe.sem_inc(turned, 1)
            with pe.Fori(0, TC) as t:
                pe.wait_ge(chosen_done, t + 1)
                for r in range(3):
                    mm = nc.tensor.transpose(ps[:, 0, r * P:(r + 1) * P], rows[:, r, :], c.ident[:, :])
                mm.then_inc(turned, 1)


def peer_spread(c, chosen, gates, following):
    nc = c.nc
    QUADS = 4
    with ExitStack() as ph:
        sb = lambda name, shape, dt=F32: ph.enter_context(nc.sbuf_tensor(f"pg_{name}", shape, dt))
        cols = sb("cols", [P, 3, 4 * QUADS])
        second = sb("second", [P, QUADS, 4, KEYS])
        first = sb("first", [P, QUADS, 4, KEYS])
        staged = sb("staged", [P, 2, KEYS, TG])
        colled, built, spread, taken = (sem(c, f"pg_{n}") for n in ("colled", "built", "spread", "taken"))
        written = [sem(c, f"pg_written{p}") for p in range(2)]
        ps = c.psum
        inner = TG // (4 * QUADS)
        block = ph.enter_context(nc.Block())

        def turns(eng, body):
            with eng.Fori(0, N_TG // 2) as o:
                for p in range(2):
                    with eng.Fori(0, inner) as n:
                        body((o * 2 + p) * inner + n, n, o, p)

        @block.vector
        def _(dve):
            V = nc.vector

            def body(m, n, o, p):
                dve.wait_ge(built, m * QUADS + 1)
                V.tensor_copy(cols[:, :, :], chosen[:, :, bass.ds(m * 4 * QUADS, 4 * QUADS)]).then_inc(colled, 1)
                dve.wait_ge(colled, m + 1)
                for q in range(QUADS):
                    dve.wait_ge(spread, m * QUADS + q + 1)
                    for j in range(4):
                        at = q * 4 + j
                        V.tensor_scalar(second[:, q, j, :], c.iota[:, :], cols[:, 1, at:at + 1], None, ALU.is_equal)
                        ins = V.tensor_scalar(first[:, q, j, :], c.iota[:, :], cols[:, 0, at:at + 1],
                                              cols[:, 2, at:at + 1], ALU.is_equal, ALU.mult)
                    ins.then_inc(built, 1)

            dve.sem_inc(built, 1)
            turns(dve, body)

        @block.tensor
        def _(pe):
            def body(m, n, o, p):
                for q in range(QUADS):
                    pe.wait_ge(built, m * QUADS + q + 2)
                    pe.wait_ge(taken, m * QUADS + q + 1)
                    for j in range(4):
                        mm = nc.tensor.matmul(ps[:, q, j * KEYS:(j + 1) * KEYS], second[:, q, j, :],
                                              first[:, q, j, :], start=True, stop=True)
                    mm.then_inc(spread, 1)

            pe.sem_inc(spread, QUADS)
            turns(pe, body)

        @block.scalar
        def _(act):
            def body(m, n, o, p):
                act.wait_ge(written[p], o * 16 + 16)
                for q in range(QUADS):
                    act.wait_ge(spread, m * QUADS + q + QUADS + 1)
                    nc.scalar.copy(staged[:, p, :, bass.ds(n * (4 * QUADS) + q * 4, 4)],
                                   ps[:, q, :].rearrange("p (t k) -> p k t", t=4)).then_inc(taken, 1)

            act.sem_inc(taken, QUADS)
            turns(act, body)

        @block.sync
        def _(sp):
            for p in range(2):
                sp.sem_inc(written[p], 16)
            with sp.Fori(0, N_TG // 2) as o:
                for p in range(2):
                    sp.wait_ge(c.begun, 1)
                    sp.wait_ge(taken, (o * 2 + p + 1) * (inner * QUADS) + QUADS)
                    sp.dma_start(gates[bass.ds(o * 2 + p, 1)].rearrange("g p k t -> p (g k) t"), staged[:, p]
                                 ).then_inc(written[p], 16)
            for p in range(2):
                sp.wait_ge(written[p], 16 * (N_TG // 2) + 16)
            following(sp)


def u_parts(c, slot, u, first):
    v = u.rearrange("(a b) d -> b a d", b=KEYS)
    dst = raw_tile(c, slot, 2, D)
    return [(dst[:, a:a + 1, :], v[:, bass.ds(first + a, 1), :]) for a in range(2)]


def v_parts(c, slot, w, first, half):
    v = w.rearrange("(a b) d -> b a d", b=KEYS)
    dst = raw_tile(c, slot, 4, D // 2)
    return [(dst[:, a:a + 2, :], v[:, bass.ds(first + a, 2), half * 512:half * 512 + 512]) for a in (0, 2)]


def u_first(c, u, use):
    def go(sp):
        for j in range(2):
            load_tile(c, sp, use, j, u_parts(c, j, u, 2 * j))
    return go


def peer_experts(c, u, v, h, gates, following):
    nc = c.nc
    u0 = c.use
    N_U = PART // 2
    PER = N_U
    with ExitStack() as ph:
        sb = lambda name, shape, dt=F32: ph.enter_context(nc.sbuf_tensor(f"pe_{name}", shape, dt))
        act_hi = sb("act_hi", [P, PART, T], F32R)
        act_lo = sb("act_lo", [P, PART, T], F32R)
        gate = sb("gate", [P, 2, N_TG, 2, TG])
        gelu = sb("gelu", [P, 2, T])
        prod = sb("prod", [P, 2, T])
        gate_loaded = [sem(c, f"pe_gate_loaded{j}") for j in range(2)]
        turned, hidden, gelued, gated, hi_done, lo_done, out_done, added = (sem(c, f"pe_{n}") for n in (
            "turned", "hidden", "gelued", "gated", "hi_done", "lo_done", "out_done", "added"))
        ps = c.psum
        turn_ps = ps[:, 0:4, :].rearrange("p b n -> p (b n)")
        block = ph.enter_context(nc.Block())

        @block.sync
        def _(sp):
            def gate_tile(q, i, j):
                sp.wait_ge(c.begun, 1)
                sp.wait_ge(gated, q * N_U + i * 2 + j + 1)
                src = gates[:, :, bass.ds(q * PART + i * 4 + j * 2, 2), :].rearrange("g p a t -> p g a t")
                sp.dma_start(gate[:, j], src).then_inc(gate_loaded[j], 16)

            def part(q, begun):
                use = u0 + q * PER
                for j in range(2):
                    if not begun:
                        load_tile(c, sp, use, j, u_parts(c, j, u, q * PART + j * 2))
                    gate_tile(q, 0, j)
                with sp.Fori(1, N_U // 2) as i:
                    for j in range(2):
                        load_tile(c, sp, use + i, j, u_parts(c, j, u, q * PART + i * 4 + j * 2))
                        gate_tile(q, i, j)
                for half in range(2):
                    for m in range(PART // 4):
                        load_tile(c, sp, use + N_U // 2 + half * 2 + m // 2, m % 2,
                                  v_parts(c, m % 2, v, q * PART + m * 4, half))

            part(0, True)
            with sp.Fori(1, N_PARTS) as q:
                part(q, False)
            following(sp)

        @block.tensor
        def _(pe):
            def turn(q, i, j):
                use = u0 + q * PER + i
                pe.wait_ge(c.tile_loaded[j], 32 * use + 32)
                pe.wait_ge(c.lo_ready, 2 * use + j + 2)
                rows = raw_tile(c, j, 2, D)
                for a in range(2):
                    for k in range(KD):
                        at = (a * KD + k) * P
                        mm = nc.tensor.transpose(turn_ps[:, at:at + P], rows[:, a, k * P:(k + 1) * P], c.ident[:, :])
                mm.then_inc(turned, 1)

            def hide(q, i, j):
                n = q * N_U + i * 2 + j
                wait_tile(c, pe, u0 + q * PER + i, j)
                pe.wait_ge(gelued, n + 1)
                w_hi, w_lo = (t[:, j, :].rearrange("p (a k n) -> p a k n", a=2, k=KD) for t in (c.hi, c.lo))
                for a in range(2):
                    mm = products(c, ps[:, 4 + a, :], [
                        ((w_hi[:, a, k, :], w_lo[:, a, k, :]), (h[0][:, k, :], h[1][:, k, :])) for k in range(KD)])
                mm.then_inc(c.tile_used, 1)

            def outputs(q, half):
                if half == 1:
                    pe.wait_ge(gelued, q * N_U + N_U + 1)
                for m in range(PART // 4):
                    j = m % 2
                    wait_tile(c, pe, u0 + q * PER + N_U // 2 + half * 2 + m // 2, j)
                    pe.wait_ge(lo_done, q * N_U + 2 * m + 3)
                    w_hi, w_lo = w_tile(c, j, 4, D // 2)
                    for a in range(4):
                        e = m * 4 + a
                        for d in range(4):
                            out, col = ps[:, 4 * half + d, :], slice(d * P, (d + 1) * P)
                            start, stop = e == 0, e == PART - 1
                            nc.tensor.matmul(out, w_hi[:, a, col], act_hi[:, e, :], start=start, stop=False)
                            nc.tensor.matmul(out, w_hi[:, a, col], act_lo[:, e, :], start=False, stop=False)
                            mm = nc.tensor.matmul(out, w_lo[:, a, col], act_hi[:, e, :], start=False, stop=stop)
                    mm.then_inc(c.tile_used, 1)

            with pe.Fori(0, N_PARTS) as q:
                pe.wait_ge(added, q * 2 + 2)
                turn(q, 0, 0)
                with pe.Fori(0, N_U // 2 - 1) as i:
                    turn(q, i, 1)
                    hide(q, i, 0)
                    turn(q, i + 1, 0)
                    hide(q, i, 1)
                i = N_U // 2 - 1
                turn(q, i, 1)
                hide(q, i, 0)
                hide(q, i, 1)
                for half in range(2):
                    outputs(q, half)

        @block.scalar
        def _(act):
            def turned_hi(q, i, j):
                use = u0 + q * PER + i
                act.wait_ge(turned, q * N_U + i * 2 + j + 1)
                act.wait_ge(c.tile_used, 2 * use + j + 1)
                nc.scalar.copy(c.hi[:, j, :], turn_ps).then_inc(c.hi_ready, 1)

            def activate(q, i, j):
                n = q * N_U + i * 2 + j
                act.wait_ge(c.tile_used, 2 * (u0 + q * PER + i) + j + 3)
                act.wait_ge(gated, n + 2)
                nc.scalar.activation(gelu[:, :, :], ps[:, 4:6, :], ACT.Gelu).then_inc(gelued, 1)

            def high(q, i, j):
                n = q * N_U + i * 2 + j
                act.wait_ge(gated, n + 3)
                nc.scalar.copy(act_hi[:, bass.ds(i * 4 + j * 2, 2), :], prod[:, :, :]).then_inc(hi_done, 1)

            act.sem_inc(gelued, 1)
            with act.Fori(0, N_PARTS) as q:
                turned_hi(q, 0, 0)
                with act.Fori(0, N_U // 2 - 1) as i:
                    turned_hi(q, i, 1)
                    activate(q, i, 0)
                    high(q, i, 0)
                    turned_hi(q, i + 1, 0)
                    activate(q, i, 1)
                    high(q, i, 1)
                i = N_U // 2 - 1
                turned_hi(q, i, 1)
                activate(q, i, 0)
                high(q, i, 0)
                split_hi(c, act, u0 + q * PER + N_U // 2, 0)
                activate(q, i, 1)
                high(q, i, 1)
                for m in range(1, N_U):
                    split_hi(c, act, u0 + q * PER + N_U // 2 + m // 2, m % 2)

        @block.gpsimd
        def _(pool):
            pool.sem_inc(gated, 2)
            with pool.Fori(0, N_PARTS * N_U // 2) as m:
                for j in range(2):
                    n = m * 2 + j
                    pool.wait_ge(c.begun, 1)
                    pool.wait_ge(gelued, n + 2)
                    pool.wait_ge(gate_loaded[j], m * 16 + 16)
                    pool.wait_ge(lo_done, n + 1)
                    pool.tensor_tensor(prod[:, :, :].rearrange("p a (g t) -> p a g t", g=N_TG),
                                       gelu[:, :, :].rearrange("p a (g t) -> p a g t", g=N_TG),
                                       gate[:, j].rearrange("p g a t -> p a g t"), ALU.mult).then_inc(gated, 1)

        @block.vector
        def _(dve):
            V = nc.vector

            def turned_lo(q, i, j):
                dve.wait_ge(c.hi_ready, 2 * (u0 + q * PER + i) + j + 1)
                V.tensor_tensor(c.lo[:, j, :], turn_ps, c.hi[:, j, :].bitcast(F32), ALU.subtract
                                ).then_inc(c.lo_ready, 1)

            def low(q, i, j):
                place = bass.ds(i * 4 + j * 2, 2)
                dve.wait_ge(hi_done, q * N_U + i * 2 + j + 1)
                V.tensor_tensor(act_lo[:, place, :], prod[:, :, :], act_hi[:, place, :].bitcast(F32),
                                ALU.subtract).then_inc(lo_done, 1)

            def add(q, half):
                dve.wait_ge(c.tile_used, 2 * (u0 + q * PER + N_U // 2 + half * 2 + 2) + 2)
                x = c.x_t[:, 4 * half:4 * half + 4, :]
                V.tensor_tensor(x, x, ps[:, 4 * half:4 * half + 4, :], ALU.add).then_inc(added, 1)

            dve.sem_inc(added, 2)
            dve.sem_inc(lo_done, 1)
            with dve.Fori(0, N_PARTS) as q:
                turned_lo(q, 0, 0)
                with dve.Fori(0, N_U // 2 - 1) as i:
                    turned_lo(q, i, 1)
                    low(q, i, 0)
                    turned_lo(q, i + 1, 0)
                    low(q, i, 1)
                i = N_U // 2 - 1
                turned_lo(q, i, 1)
                low(q, i, 0)
                split_lo(c, dve, u0 + q * PER + N_U // 2, 0)
                low(q, i, 1)
                for m in range(1, N_U):
                    split_lo(c, dve, u0 + q * PER + N_U // 2 + m // 2, m % 2)
                    if m == PART // 4 + 1:
                        add(q, 0)
                add(q, 1)
    c.use = u0 + N_PARTS * PER


class Layer:

    def __init__(self, name, first, uses, run):
        self.name, self.first, self.uses, self.run = name, first, uses, run


def splits(c, ph, tag, width=T):
    return [ph.enter_context(c.nc.sbuf_tensor(f"h_{n}_{tag}", [P, KD, width], F32R)) for n in ("hi", "lo")]


def ffn_layer(c, w, layer, which):
    tag = f"ffn{layer}{which}"
    w_gu, w_down = w["ffn_w_gate_up"][layer, which], w["ffn_w_down"][layer, which]

    def run(following):
        with ExitStack() as ph:
            h = splits(c, ph, tag)
            norm(c, tag, gain_of(c, layer, 2 * which), h)
            ffn(c, tag, w_gu, w_down, h, following)

    return Layer(tag, lambda use: ffn_first(c, w_gu, use), F_FF // 256 + KD, run)


def gain_of(c, layer, which):
    return lambda k: vec_col(c, "norm_gains", (3 * layer + which) * KD + k)


def sb_layer(c, w):
    w_in, w_out = w["sb_w_in"][0], w["sb_w_out"][0]

    def first(use):
        def go(sp):
            for j in range(2):
                load_tile(c, sp, use, j, wide_parts(c, j, w_in, 2 * D + j * 256))
        return go

    def run(following):
        with ExitStack() as ph:
            h = splits(c, ph, "sb")
            o_t = ph.enter_context(c.nc.sbuf_tensor("sb_o_t", [P, KD, T], F32))
            norm(c, "sb", gain_of(c, 0, 1), h)
            sb_attention(c, w_in, h, o_t, wide_first(c, w_out, c.use + 2 + SB_GROUPS))
            split_acts(c, o_t, h, KD)
            project(c, w_out, h, following)

    return Layer("sb", first, 2 + SB_GROUPS + 2, run)


def sw_layer(c, w):
    w_in, w_out = w["sw_w_in"][0], w["sw_w_out"][0]

    def run(following):
        with ExitStack() as ph:
            h = splits(c, ph, "sw")
            o_t = ph.enter_context(c.nc.sbuf_tensor("sw_o_t", [P, KD, T], F32))
            qk = ph.enter_context(c.nc.sbuf_tensor("sw_qk", [P, TC, SW_QK * HEAD], F32))
            v = ph.enter_context(c.nc.sbuf_tensor("sw_v", [P, TC, P], F32))
            norm(c, "sw", gain_of(c, 1, 1), h)
            sw_project(c, w_in, h, qk, v, wide_first(c, w_out, c.use + 3))
            sw_rotate(c, w["positions"], qk)
            sw_attention(c, qk, v, o_t)
            split_acts(c, o_t, h, KD)
            project(c, w_out, h, following)

    return Layer("sw", lambda use: wide_first(c, w_in, use), 3 + 2, run)


def move(c, dst, src):
    with ExitStack() as ph:
        block = ph.enter_context(c.nc.Block())

        @block.scalar
        def _(act):
            c.nc.scalar.copy(dst[:, 0:KD // 2, :], src[:, 0:KD // 2, :])

        @block.vector
        def _(dve):
            c.nc.vector.tensor_copy(dst[:, KD // 2:, :], src[:, KD // 2:, :])


def mixer_layer(c, w):
    nc = c.nc
    w_in, ssd_w_out, sc_w_out, w_o = w["w_in"][0], w["ssd_w_out"][0], w["sc_w_out"][0], w["w_o"][0]

    def run(following):
        with ExitStack() as ph:
            sb = lambda name, shape, dt=F32, on=ph: on.enter_context(nc.sbuf_tensor(f"mix_{name}", shape, dt))
            h = [sb(f"h_{n}", [P, KD, TM], F32R) for n in ("hi", "lo")]
            conv_w = [sb("conv_w", [P, 32, 4]), sb("sc_conv_w", [P, KD, 3])]
            with ExitStack() as pre:
                xm = sb("xm", [P, KD, TM], on=pre)
                widen(c, w["meta_tokens"], xm)
                norm(c, "mix", lambda k: vec_col(c, "ln_mix", k), h, src=xm, width=TM)
            with ExitStack() as pre:
                dec = Decay()
                dec.dt, dec.adt, dec.sums, dec.dt_end = (sb(n, [P, TC + 1, 32], on=pre)
                                                         for n in ("dt", "adt", "sums", "dt_end"))
                dec.from_start, dec.whole = (sb(n, [P, TC, 32], on=pre) for n in ("from_start", "whole"))
                with ExitStack() as last:
                    ssd_times(c, w_in, h, dec, (w["ssd_conv_w"][0], w["sc_conv_w"][0]), conv_w)
                    y_t = sb("y_t", [P, 16, T], on=last)
                    ssd(c, w_in, h, dec, conv_w[0], y_t, rows_first(c, ssd_w_out, c.use + 16))
                y_lo, y_hi = (sb(n, [P, 16, T], F32R, on=pre) for n in ("y_lo", "y_hi"))
                branch = sb("branch0", [P, KD, T], on=pre)
                split_acts(c, y_t, (y_hi, y_lo), 16)
                ssd_out(c, ssd_w_out, (y_hi, y_lo), branch, sc_first(c, w_in, c.use + 4))
            with ExitStack() as pre:
                ys = sb("branch_ssd", [P, KD, T], on=pre)
                move(c, ys, branch)
                s_t = sb("s_t", [P, KD, T], on=pre)
                short_conv(c, w_in, h, conv_w[1], s_t, wide_first(c, sc_w_out, c.use + KD))
                s_hi, s_lo = (sb(f"s_{n}", [P, KD, T], F32R, on=pre) for n in ("hi", "lo"))
                split_acts(c, s_t, (s_hi, s_lo), KD)
                project(c, sc_w_out, (s_hi, s_lo), gate_first(c, w_in, c.use + 2), out=s_t)
                merge(c, w_in, h, (ys, s_t), wide_first(c, w_o, c.use + 4))
                split_acts(c, ys, (s_hi, s_lo), KD)
                project(c, w_o, (s_hi, s_lo), following)

    return Layer("mixer", lambda use: ssd_first(c, w_in, use), 16 + 4 + KD + 2 + 4 + 2, run)


def peer_layer(c, w):
    nc = c.nc
    gates = nc.dram_tensor("peer_gates", [N_TG, P, KEYS, TG], F32).ap()
    w_q, keys, u, v = w["peer_w_q"][0], w["peer_sub_keys"][0], w["peer_u"][0], w["peer_v"][0]

    def run(following):
        with ExitStack() as ph:
            h = splits(c, ph, "peer")
            norm(c, "peer", lambda k: vec_col(c, "ln_ffn", k), h)
            with ExitStack() as pre:
                chosen = pre.enter_context(nc.sbuf_tensor("chosen", [P, 3, T], F32))
                with ExitStack() as top:
                    values, places = (top.enter_context(nc.sbuf_tensor(n, [P, NH, 2 * TC, TOP], F32))
                                      for n in ("top_values", "top_places"))
                    peer_queries(c, w_q, keys, h, values, places, lambda sp: None)
                    peer_choose(c, values, places, chosen)
                peer_spread(c, chosen, gates, u_first(c, u, c.use))
            peer_experts(c, u, v, h, gates, following)

    return Layer("peer", lambda use: wide_first(c, w_q, use), NH // 2 + N_PARTS * PART // 2, run)


def final_layer(c, out):
    def run(following):
        with ExitStack() as ph:
            y = ph.enter_context(c.nc.sbuf_tensor("final", [P, KD, T], F32))
            norm(c, "final", lambda k: vec_col(c, "ln_final", k), None, out_f32=y)
            store(c, out, y)

    return Layer("final", lambda use: (lambda sp: None), 0, run)


def build(nc, args, out):
    w = {n.removesuffix("_2"): a for n, a in args.items()}
    with ExitStack() as ctx:
        c = Chip()
        c.nc, c.ctx, c.use, c.stages = nc, ctx, 0, {}
        sb = lambda name, shape, dt=F32: ctx.enter_context(nc.sbuf_tensor(name, shape, dt))
        c.x_t = sb("x_t", [P, KD, T])
        c.raw = sb("w_raw", [P, 2, TILE])
        c.hi = sb("w_hi", [P, 2, TILE], F32R)
        c.lo = sb("w_lo", [P, 2, TILE], F32R)
        c.ones = sb("ones", [P, P])
        c.neg_ones = sb("neg_ones", [P, P])
        c.ident = sb("ident", [P, P])
        c.tri_up = sb("tri_up", [P, P])
        c.neg_tri = sb("neg_tri", [P, P])
        c.swa_mask = sb("swa_mask", [P, TC, 2 * P])
        c.causal_cap = sb("causal_cap", [P, P])
        c.iota = sb("iota", [P, P])
        c.vec = sb("vec", [P, sum(n for _, n in VECTORS)])
        c.rows = sb("rows", [P, sum(n for _, n in ROWS)])
        c.psum = ctx.enter_context(nc.psum_tensor("psum", [P, 8, BANK], F32))
        c.tile_loaded = [sem(c, f"tile_loaded{j}") for j in range(2)]
        c.begun = sem(c, "begun")
        c.hi_ready, c.lo_ready, c.tile_used = (sem(c, n) for n in ("hi_ready", "lo_ready", "tile_used"))

        plan = [ffn_layer(c, w, 0, 0), sb_layer(c, w), ffn_layer(c, w, 0, 1),
                ffn_layer(c, w, 1, 0), sw_layer(c, w), ffn_layer(c, w, 1, 1),
                mixer_layer(c, w), peer_layer(c, w), final_layer(c, out)]
        following, at = [], 0
        for layer in plan:
            following.append(layer.first(at))
            at += layer.uses
        following.append(lambda sp: None)
        setup(c, w, following[0])
        for n, layer in enumerate(plan):
            layer.run(following[n + 1])
            assert c.use == sum(done.uses for done in plan[:n + 1]), layer.name


_INS = ["x", "positions", "norm_gains", "ffn_w_gate_up", "ffn_w_down", "sb_w_in", "sb_w_out", "sw_w_in", "sw_w_out",
        "sw_q_gain", "sw_k_gain", "sw_sinks", "meta_tokens_2", "ln_mix_2", "w_in_2", "ssd_conv_w_2", "ssd_conv_b_2",
        "ssd_dt_bias_2", "ssd_a_log_2", "ssd_d_2", "ssd_norm_2", "ssd_w_out_2", "sc_conv_w_2", "sc_w_out_2",
        "w_o_2", "ln_ffn_2", "peer_w_q_2", "peer_sub_keys_2", "peer_u_2", "peer_v_2", "ln_final_2"]
_OUTS = [((1, T, D), "float32")]


def kernel(**inputs):
    import numpy as _np
    import concourse.bacc as _bacc
    from concourse import mybir as _mybir
    from concourse.bass_utils import run_bass_kernel_spmd as _run

    nc = _bacc.Bacc("TRN2", target_bir_lowering=False, num_devices=1)
    arrays, args = {}, {}
    for name in _INS:
        a = _np.ascontiguousarray(inputs[name])
        arrays[f"in_{name}_dram"] = a
        args[name] = nc.dram_tensor(f"in_{name}_dram", a.shape, _mybir.dt.from_np(a.dtype), kind="ExternalInput").ap()
    out = nc.dram_tensor("out_0_dram", _OUTS[0][0], F32, kind="ExternalOutput").ap()
    build(nc, args, out)
    r = _run(nc, [arrays], core_ids=[0])
    return r.results[0]["out_0_dram"]
```

```python
from contextlib import ExitStack

import numpy as np

import concourse.bass as bass
from concourse import mybir

F32 = mybir.dt.float32
F32R = mybir.dt.float32r
I32 = mybir.dt.int32
U32 = mybir.dt.uint32
ALU = mybir.AluOpType
ACT = mybir.ActivationFunctionType
AX = mybir.AxisListType.X

P = 128
T = 512
D = 1024
KD = D // P
TC = T // P
BANK = 512
TILE = 2048
HEAD = 64
EPS = 1e-6

F_FF = 2816
KF = F_FF // P
KH = KF // 2

META = 16
TM = META + T


class Chip:
    pass


def sem(c, name):
    return c.ctx.enter_context(c.nc.semaphore(name))


def shared(c, kind, names, steps=1):
    if kind not in c.stages:
        c.stages[kind] = [0, [sem(c, f"{kind}_{n}") for n in names]]
    stage = c.stages[kind]
    stage[0] += steps
    return [stage[0] - steps] + stage[1]


def load_tile(c, sp, use, slot, parts):
    sp.wait_ge(c.begun, 1)
    sp.wait_ge(c.lo_ready, 2 * use + slot + 1)
    for dst, src in parts:
        sp.dma_start(dst, src).then_inc(c.tile_loaded[slot], 16)


def split_hi(c, act, use, slot, cols=TILE):
    act.wait_ge(c.tile_loaded[slot], 32 * use + 32)
    act.wait_ge(c.tile_used, 2 * use + slot + 1)
    c.nc.scalar.copy(c.hi[:, slot, :cols], c.raw[:, slot, :cols]).then_inc(c.hi_ready, 1)


def split_lo(c, dve, use, slot, cols=TILE):
    dve.wait_ge(c.hi_ready, 2 * use + slot + 1)
    c.nc.vector.tensor_tensor(c.lo[:, slot, :cols], c.raw[:, slot, :cols],
                              c.hi[:, slot, :cols].bitcast(F32), ALU.subtract).then_inc(c.lo_ready, 1)


def wait_tile(c, pe, use, slot):
    pe.wait_ge(c.lo_ready, 2 * use + slot + 3)


def products(c, out, pairs, before=None):
    last = len(pairs) - 1
    for n, ((w_hi, w_lo), (x_hi, x_lo)) in enumerate(pairs):
        if before is not None:
            before(n)
        c.nc.tensor.matmul(out, w_hi, x_hi, start=(n == 0), stop=False)
        c.nc.tensor.matmul(out, w_hi, x_lo, start=False, stop=False)
        mm = c.nc.tensor.matmul(out, w_lo, x_hi, start=False, stop=(n == last))
    return mm


def products_as_ready(c, pe, acts, jobs):
    for k in range(acts.chunks):
        acts.wait(pe, k)
        first, last = k == 0, k == acts.chunks - 1
        for out, pair, done in jobs:
            (w_hi, w_lo), (x_hi, x_lo) = pair(k)
            c.nc.tensor.matmul(out, w_hi, x_hi, start=first, stop=False)
            c.nc.tensor.matmul(out, w_hi, x_lo, start=False, stop=False)
            mm = c.nc.tensor.matmul(out, w_lo, x_hi, start=False, stop=last)
            if last and done is not None:
                mm.then_inc(done, 1)


def wide_jobs(c, h, j):
    w_hi, w_lo = w_tile(c, j, KD, 256)
    jobs = []
    for n in range(2):
        def pair(k, col=slice(n * P, (n + 1) * P)):
            return (w_hi[:, k, col], w_lo[:, k, col]), (h[0][:, k, :], h[1][:, k, :])
        jobs.append((c.psum[:, 2 * j + n, :], pair, c.tile_used if n else None))
    return jobs


def w_tile(c, slot, k, width):
    return [part[:, slot, :k * width].rearrange("p (k n) -> p k n", k=k) for part in (c.hi, c.lo)]


def raw_tile(c, slot, k, width):
    return c.raw[:, slot, :k * width].rearrange("p (k n) -> p k n", k=k)


def wide_parts(c, slot, w, col, width=256):
    v = w.rearrange("(k p) n -> p k n", p=P)
    dst = raw_tile(c, slot, KD, width)
    return [(dst[:, k:k + KD // 2, :], v[:, k:k + KD // 2, bass.ds(col, width)]) for k in (0, KD // 2)]


def pair_parts(c, slot, w, col_a, col_b):
    v = w.rearrange("(k p) n -> p k n", p=P)
    dst = c.raw[:, slot, :].rearrange("p (j k n) -> p j k n", j=2, k=KD)
    return [(dst[:, j], v[:, :, bass.ds(col, P)]) for j, col in enumerate((col_a, col_b))]


def tall_parts(c, slot, w, row, k, col):
    v = w.rearrange("(k p) n -> p k n", p=P)
    dst = raw_tile(c, slot, k, P)
    a = k // 2
    return [(dst[:, lo:hi, :], v[:, row + lo:row + hi, bass.ds(col, P)]) for lo, hi in ((0, a), (a, k))]


VECTORS = (("norm_gains", 48), ("ln_mix", 8), ("ssd_conv_b", 32), ("ssd_norm", 16), ("ln_ffn", 8), ("ln_final", 8))
ROWS = (("sw_q_gain", HEAD), ("sw_k_gain", HEAD), ("sw_sinks", 16), ("ssd_dt_bias", 32), ("ssd_a_log", 32), ("ssd_d", 32))


def setup(c, w, first):
    nc = c.nc
    n_vec = sum(n for _, n in VECTORS)
    n_row = sum(n for _, n in ROWS)
    with ExitStack() as ph:
        vec_rows = ph.enter_context(nc.sbuf_tensor("vec_rows", [n_vec, P], F32))
        row = ph.enter_context(nc.sbuf_tensor("row", [1, n_row], F32))
        x_rows = ph.enter_context(nc.sbuf_tensor("x_rows", [P, TC, D], F32))
        made, vec_loaded = (sem(c, n) for n in ("const_made", "vec_loaded"))
        _, turned, taken = shared(c, "rows", ("turned", "taken"), 2 + TC)
        loaded = [sem(c, f"in_loaded{t}") for t in range(TC)]
        ps = c.psum
        block = ph.enter_context(nc.Block())

        @block.sync
        def _(sp):
            at = 0
            for name, n in VECTORS:
                src = w[name]
                flat = src.rearrange("a b d -> (a b d)") if len(src.shape) == 3 else (
                    src.rearrange("a d -> (a d)") if len(src.shape) == 2 else src)
                sp.dma_start(vec_rows[at:at + n, :], flat.rearrange("(r p) -> r p", p=P)).then_inc(vec_loaded, 16)
                at += n
            at = 0
            for name, n in ROWS:
                src = w[name]
                sp.dma_start(row[0:1, at:at + n], src[0:1, :]).then_inc(vec_loaded, 16)
                at += n
            for t in range(TC):
                sp.dma_start(x_rows[:, t, :], w["x"][0, t * P:(t + 1) * P, :]).then_inc(loaded[t], 16)
            first(sp)

        @block.gpsimd
        def _(pool):
            pool.memset(c.ones[:, :], 1.0).then_inc(made, 1)
            pool.memset(c.neg_ones[:, :], -1.0).then_inc(made, 1)
            pool.memset(c.ident[:, :], 0.0).then_inc(made, 1)
            pool.memset(c.swa_mask[:, :, :], 0.0).then_inc(made, 1)
            pool.memset(c.causal_cap[:, :], 3e38).then_inc(made, 1)
            pool.wait_ge(made, 5)
            pool.affine_select(out=c.ident[:, :], in_=c.ident[:, :], compare_op=ALU.not_equal, fill=1.0,
                               base=0, pattern=[[-1, P]], channel_multiplier=1).then_inc(made, 1)
            pool.affine_select(out=c.tri_up[:, :], in_=c.ones[:, :], compare_op=ALU.is_ge, fill=0.0,
                               base=0, pattern=[[1, P]], channel_multiplier=-1).then_inc(made, 1)
            pool.affine_select(out=c.neg_tri[:, :], in_=c.neg_ones[:, :], compare_op=ALU.is_ge, fill=0.0,
                               base=0, pattern=[[-1, P]], channel_multiplier=1).then_inc(made, 1)
            pool.affine_select(out=c.causal_cap[:, :], in_=c.causal_cap[:, :], compare_op=ALU.is_gt, fill=0.0,
                               base=0, pattern=[[1, P]], channel_multiplier=-1).then_inc(made, 1)
            pool.affine_select(out=c.swa_mask[:, :, 0:P], in_=c.swa_mask[:, :, 0:P], compare_op=ALU.is_gt, fill=-3e38,
                               base=0, pattern=[[0, TC], [1, P]], channel_multiplier=-1).then_inc(made, 1)
            pool.affine_select(out=c.swa_mask[:, :, P:2 * P], in_=c.swa_mask[:, :, P:2 * P], compare_op=ALU.is_ge,
                               fill=-3e38, base=0, pattern=[[0, TC], [-1, P]], channel_multiplier=1).then_inc(made, 1)
            pool.wait_ge(made, 11)
            pool.memset(c.swa_mask[:, 0, 0:P], -3e38).then_inc(made, 1)
            pool.iota(c.iota[:, :], pattern=[[1, P]], base=0, channel_multiplier=0,
                      allow_small_or_imprecise_dtypes=True).then_inc(made, 1)

        @block.tensor
        def _(pe):
            pe.sem_inc(c.begun, 1)
            pe.sem_inc(c.tile_used, 2)
            pe.sem_inc(c.lo_ready, 2)
            pe.wait_ge(made, 13)
            pe.wait_ge(vec_loaded, 16 * (len(VECTORS) + len(ROWS)))
            nc.tensor.transpose(ps[:, 4, 0:n_vec], vec_rows[:, :], c.ident[0:n_vec, 0:n_vec]).then_inc(turned, 1)
            nc.tensor.matmul(ps[:, 5, 0:n_row], c.ones[0:1, :], row[0:1, :], start=True, stop=True).then_inc(turned, 1)
            for t in range(TC):
                pe.wait_ge(loaded[t], 16)
                if t >= 2:
                    pe.wait_ge(taken, 4 + t - 2 - 1)
                for k in range(KD):
                    b = 2 * (t % 2) + k // 4
                    mm = nc.tensor.transpose(ps[:, b, (k % 4) * P:(k % 4 + 1) * P], x_rows[:, t, k * P:(k + 1) * P],
                                             c.ident[:, :])
                mm.then_inc(turned, 1)

        @block.vector
        def _(dve):
            dve.wait_ge(turned, 2)
            nc.vector.tensor_copy(c.vec[:, 0:n_vec], ps[:, 4, 0:n_vec]).then_inc(taken, 1)
            nc.vector.tensor_copy(c.rows[:, 0:n_row], ps[:, 5, 0:n_row]).then_inc(taken, 1)
            for t in range(TC):
                dve.wait_ge(turned, 3 + t)
                src = ps[:, 2 * (t % 2):2 * (t % 2) + 2, :].rearrange("p b (k n) -> p (b k) n", n=P)
                nc.vector.tensor_copy(c.x_t[:, :, t * P:(t + 1) * P], src).then_inc(taken, 1)


def vec_at(name):
    at = 0
    for n, size in VECTORS:
        if n == name:
            return at
        at += size


def vec_col(c, name, i):
    at = vec_at(name) + i
    return c.vec[:, at:at + 1]


def row_of(c, name):
    at = 0
    for n, size in ROWS:
        if n == name:
            return c.rows[:, at:at + size]
        at += size


class Norm:
    STEPS = 6

    def __init__(self, c, ph, tag, gain, h, src=None, width=T, sq=None, out_f32=None, bank=7):
        sb = lambda name, shape: ph.enter_context(c.nc.sbuf_tensor(f"{name}_{tag}", shape, F32))
        self.c, self.gain, self.h, self.out, self.chunks = c, gain, h, out_f32, KD
        self.src = c.x_t if src is None else src
        self.banks = [(0, width)] if width <= BANK else [(0, width // 2), (width // 2, width)]
        self.sq = sb("sq", [P, KD, width]) if sq is None else sq
        self.rstd = sb("rstd", [P, width])
        self.ps = c.psum[:, bank + 1 - len(self.banks):bank + 1, 0:self.banks[0][1]]
        (self.run, self.squared, self.summed, self.rooted, self.steps, self.scaled, self.hi_done,
         self.lo_done) = shared(c, "norm", ("squared", "summed", "rooted", "steps", "scaled", "hi_done", "lo_done"))

    def wait(self, pe, k):
        pe.wait_ge(self.lo_done, self.run * KD + k + 1)

    def scalar(self, act, meanwhile=lambda: None):
        nc, sq, rstd = self.c.nc, self.sq, self.rstd
        act.preload_act_table_set("sqrt_and_others")
        for n in range(4):
            part = slice(n * KD // 4, (n + 1) * KD // 4)
            nc.scalar.activation(sq[:, part], self.src[:, part], ACT.Square).then_inc(self.squared, 1)
        meanwhile()
        act.wait_ge(self.steps, self.run * self.STEPS + 5)
        nc.scalar.activation(rstd[:, :], rstd[:, :], ACT.Sqrt).then_inc(self.rooted, 1)
        if self.h is not None:
            for k in range(KD):
                act.wait_ge(self.scaled, self.run * KD + k + 1)
                nc.scalar.copy(self.h[0][:, k, :], sq[:, k, :]).then_inc(self.hi_done, 1)

    def vector(self, dve, meanwhile=lambda: None):
        nc, sq, rstd, run = self.c.nc, self.sq, self.rstd, self.run
        for n in range(1, 4):
            dve.wait_ge(self.squared, run * 4 + n + 1)
            nc.vector.tensor_tensor(sq[:, 0:2], sq[:, 0:2], sq[:, 2 * n:2 * n + 2], ALU.add).then_inc(self.steps, 1)
            dve.wait_ge(self.steps, run * self.STEPS + n)
        nc.vector.tensor_tensor(sq[:, 0], sq[:, 0], sq[:, 1], ALU.add).then_inc(self.steps, 1)
        meanwhile()
        dve.wait_ge(self.summed, run + 1)
        nc.vector.tensor_scalar(rstd[:, :].rearrange("p (b n) -> p b n", b=len(self.banks)), self.ps,
                                1.0 / D, EPS, ALU.mult, ALU.add).then_inc(self.steps, 1)
        dve.wait_ge(self.rooted, run + 1)
        nc.vector.reciprocal(rstd[:, :], rstd[:, :]).then_inc(self.steps, 1)
        dve.wait_ge(self.steps, run * self.STEPS + self.STEPS)
        dst = sq if self.out is None else self.out

        def scale(k):
            nc.vector.scalar_tensor_tensor(dst[:, k, :], self.src[:, k, :], self.gain(k), rstd[:, :], ALU.mult,
                                           ALU.mult).then_inc(self.scaled, 1)

        scale(0)
        for k in range(KD):
            if k + 1 < KD:
                scale(k + 1)
            if self.h is not None:
                dve.wait_ge(self.hi_done, run * KD + k + 1)
                nc.vector.tensor_tensor(self.h[1][:, k, :], sq[:, k, :], self.h[0][:, k, :].bitcast(F32),
                                        ALU.subtract).then_inc(self.lo_done, 1)

    def tensor(self, pe):
        pe.wait_ge(self.steps, self.run * self.STEPS + 4)
        for b, (lo, hi) in enumerate(self.banks):
            mm = self.c.nc.tensor.matmul(self.ps[:, b, :], self.c.ones[:, :], self.sq[:, 0, lo:hi], start=True,
                                         stop=True)
        mm.then_inc(self.summed, 1)


def norm(c, tag, gain, h, src=None, width=T, out_f32=None):
    with ExitStack() as ph:
        pre = Norm(c, ph, tag, gain, h, src, width, out_f32=out_f32)
        block = ph.enter_context(c.nc.Block())

        @block.scalar
        def _(act):
            pre.scalar(act)

        @block.vector
        def _(dve):
            pre.vector(dve)

        @block.tensor
        def _(pe):
            pre.tensor(pe)


def ffn_first(c, w_gu, use):
    def go(sp):
        load_tile(c, sp, use, 0, wide_parts(c, 0, w_gu, 0))
        load_tile(c, sp, use, 1, wide_parts(c, 1, w_gu, F_FF))
    return go


def ffn(c, tag, gain, w_gu, w_down, h, following):
    nc = c.nc
    n_up = F_FF // 256
    u0 = c.use
    u1 = u0 + n_up
    with ExitStack() as ph:
        with nc.sbuf_tensor(f"sq_{tag}", [P, KD, T], F32) as squares:
            pass
        a_hi = ph.enter_context(nc.sbuf_tensor(f"a_hi_{tag}", [P, KF, T], F32R))
        a_lo = ph.enter_context(nc.sbuf_tensor(f"a_lo_{tag}", [P, KF, T], F32R))
        a = ph.enter_context(nc.sbuf_tensor(f"a_{tag}", [P, 2, T], F32))
        silu = ph.enter_context(nc.sbuf_tensor(f"silu_{tag}", [P, 2, T], F32))
        run, gated, up_taken, a_hi_done, a_lo_done, out_taken = shared(
            c, "ffn", ("gated", "up_taken", "a_hi_done", "a_lo_done", "out_taken"))
        m0, n0 = run * n_up, run * KD
        pre = Norm(c, ph, tag, gain, h, sq=squares)
        ps = c.psum
        block = ph.enter_context(nc.Block())

        @block.sync
        def _(sp):
            with sp.Fori(1, n_up) as i:
                load_tile(c, sp, u0 + i, 0, wide_parts(c, 0, w_gu, i * 256))
                load_tile(c, sp, u0 + i, 1, wide_parts(c, 1, w_gu, i * 256 + F_FF))
            with sp.Fori(0, KD) as n:
                for j in range(2):
                    load_tile(c, sp, u1 + n, j, tall_parts(c, j, w_down, j * KH, KH, n * P))
            following(sp)

        @block.scalar
        def _(act):
            def body(i, cols):
                act.wait_ge(c.tile_used, 2 * (u0 + i) + 3)
                if not (isinstance(i, int) and i == 0):
                    act.wait_ge(up_taken, m0 + i)
                nc.scalar.activation(silu[:, :, :], ps[:, 0:2, :], ACT.Silu).then_inc(gated, 1)
                split_hi(c, act, u0 + i + 1, 0, cols)
                act.wait_ge(up_taken, m0 + i + 1)
                nc.scalar.copy(a_hi[:, bass.ds(i * 2, 2), :], a[:, :, :]).then_inc(a_hi_done, 1)
                split_hi(c, act, u0 + i + 1, 1, cols)

            def splits():
                split_hi(c, act, u0, 0)
                split_hi(c, act, u0, 1)

            pre.scalar(act, splits)
            body(0, TILE)
            with act.Fori(1, n_up - 1) as i:
                body(i, TILE)
            body(n_up - 1, KH * P)
            with act.Fori(1, KD) as n:
                split_hi(c, act, u1 + n, 0, KH * P)
                split_hi(c, act, u1 + n, 1, KH * P)

        @block.vector
        def _(dve):
            def body(i, cols):
                split_lo(c, dve, u0 + i + 1, 0, cols)
                dve.wait_ge(gated, m0 + i + 1)
                dve.wait_ge(c.tile_used, 2 * (u0 + i) + 4)
                if not (isinstance(i, int) and i == 0):
                    dve.wait_ge(a_lo_done, m0 + i)
                nc.vector.tensor_tensor(a[:, :, :], silu[:, :, :], ps[:, 2:4, :], ALU.mult).then_inc(up_taken, 1)
                split_lo(c, dve, u0 + i + 1, 1, cols)
                dve.wait_ge(a_hi_done, m0 + i + 1)
                nc.vector.tensor_tensor(a_lo[:, bass.ds(i * 2, 2), :], a[:, :, :],
                                        a_hi[:, bass.ds(i * 2, 2), :].bitcast(F32),
                                        ALU.subtract).then_inc(a_lo_done, 1)

            pre.vector(dve, lambda: split_lo(c, dve, u0, 0))
            split_lo(c, dve, u0, 1)
            body(0, TILE)
            with dve.Fori(1, n_up - 1) as i:
                body(i, TILE)
            body(n_up - 1, KH * P)

            def add_out(n, bank):
                dve.wait_ge(c.tile_used, 2 * (u1 + n) + 4)
                nc.vector.scalar_tensor_tensor(c.x_t[:, n, :] if isinstance(n, int) else
                                               c.x_t[:, bass.ds(n, 1), :].rearrange("p k t -> p (k t)"),
                                               ps[:, 4 + bank, :], 0.5,
                                               c.x_t[:, n, :] if isinstance(n, int) else
                                               c.x_t[:, bass.ds(n, 1), :].rearrange("p k t -> p (k t)"),
                                               ALU.mult, ALU.add).then_inc(out_taken, 1)

            with dve.Fori(0, KD // 2 - 1) as m:
                for bank in range(2):
                    for j in range(2):
                        split_lo(c, dve, u1 + m * 2 + bank + 1, j, KH * P)
                    add_out(m * 2 + bank, bank)
            for j in range(2):
                split_lo(c, dve, u1 + KD - 1, j, KH * P)
            add_out(KD - 2, 0)
            add_out(KD - 1, 1)

        @block.tensor
        def _(pe):
            def up(i):
                for j in range(2):
                    wait_tile(c, pe, u0 + i, j)
                    pe.wait_ge((gated, up_taken)[j], m0 + i)
                    w_hi, w_lo = w_tile(c, j, KD, 256)
                    for n in range(2):
                        col = slice(n * P, (n + 1) * P)
                        mm = products(c, ps[:, 2 * j + n, :], [
                            ((w_hi[:, k, col], w_lo[:, k, col]), (h[0][:, k, :], h[1][:, k, :])) for k in range(KD)])
                    mm.then_inc(c.tile_used, 1)

            pre.tensor(pe)
            for j in range(2):
                wait_tile(c, pe, u0, j)
                products_as_ready(c, pe, pre, wide_jobs(c, h, j))
            with pe.Fori(1, n_up) as i:
                up(i)

            def down(n, bank, start_of_bank):
                if not start_of_bank:
                    pe.wait_ge(out_taken, n0 + n - 1)
                for j in range(2):
                    wait_tile(c, pe, u1 + n, j)
                    if start_of_bank and n == 0:
                        pe.wait_ge(a_lo_done, m0 + ((KH + 1) // 2, n_up)[j])
                    w_hi, w_lo = w_tile(c, j, KH, P)
                    for k in range(KH):
                        f = j * KH + k
                        first, final = j == 0 and k == 0, j == 1 and k == KH - 1
                        nc.tensor.matmul(ps[:, 4 + bank, :], w_hi[:, k, :], a_hi[:, f, :], start=first, stop=False)
                        nc.tensor.matmul(ps[:, 4 + bank, :], w_hi[:, k, :], a_lo[:, f, :], start=False, stop=False)
                        mm = nc.tensor.matmul(ps[:, 4 + bank, :], w_lo[:, k, :], a_hi[:, f, :], start=False,
                                              stop=final)
                    mm.then_inc(c.tile_used, 1)

            down(0, 0, True)
            down(1, 1, True)
            with pe.Fori(1, KD // 2) as m:
                down(m * 2, 0, False)
                down(m * 2 + 1, 1, False)
    c.use = u1 + KD


def store(c, out, src):
    nc = c.nc
    with ExitStack() as ph:
        rows = ph.enter_context(nc.sbuf_tensor("out_rows", [P, TC, D], F32))
        base, turned, taken = shared(c, "rows", ("turned", "taken"), TC)
        written = sem(c, "out_written")
        ps = c.psum
        block = ph.enter_context(nc.Block())

        @block.tensor
        def _(pe):
            for t in range(TC):
                for k in range(KD):
                    mm = nc.tensor.transpose(ps[:, 2 * t + k // 4, (k % 4) * P:(k % 4 + 1) * P],
                                             src[:, k, t * P:(t + 1) * P], c.ident[:, :])
                mm.then_inc(turned, 1)

        @block.vector
        def _(dve):
            for t in range(TC):
                dve.wait_ge(turned, base + t + 1)
                nc.vector.tensor_copy(rows[:, t, :].rearrange("p (b n) -> p b n", b=2),
                                      ps[:, 2 * t:2 * t + 2, :]).then_inc(taken, 1)

        @block.sync
        def _(sp):
            for t in range(TC):
                sp.wait_ge(taken, base + t + 1)
                sp.dma_start(out[0, t * P:(t + 1) * P, :], rows[:, t, :]).then_inc(written, 16)
            sp.wait_ge(written, 16 * TC)


def wide_first(c, w, use):
    def go(sp):
        for j in range(2):
            load_tile(c, sp, use, j, wide_parts(c, j, w, j * 256))
    return go


class Split:

    def __init__(self, c, src, h, chunks):
        self.c, self.src, self.h, self.chunks = c, src, h, chunks
        self.base, self.hi_done, self.lo_done = shared(c, "split", ("hi_done", "lo_done"), chunks // 2)

    def wait(self, pe, k):
        pe.wait_ge(self.lo_done, self.base + k // 2 + 1)

    def scalar(self, first, last):
        for k in range(first, last, 2):
            self.c.nc.scalar.copy(self.h[0][:, k:k + 2, :], self.src[:, k:k + 2, :]).then_inc(self.hi_done, 1)

    def vector(self, dve, first, last):
        for k in range(first, last, 2):
            dve.wait_ge(self.hi_done, self.base + k // 2 + 1)
            self.c.nc.vector.tensor_tensor(self.h[1][:, k:k + 2, :], self.src[:, k:k + 2, :],
                                           self.h[0][:, k:k + 2, :].bitcast(F32), ALU.subtract
                                           ).then_inc(self.lo_done, 1)


def project(c, w, src, h, following, out=None):
    nc = c.nc
    pairs = D // 512
    u0 = c.use
    with ExitStack() as ph:
        pre = Split(c, src, h, KD)
        run, added = shared(c, "project", ("added",))
        m0 = run * (2 * pairs)
        ps = c.psum
        block = ph.enter_context(nc.Block())

        @block.sync
        def _(sp):
            with sp.Fori(1, pairs) as i:
                for j in range(2):
                    load_tile(c, sp, u0 + i, j, wide_parts(c, j, w, (i * 2 + j) * 256))
            following(sp)

        @block.scalar
        def _(act):
            split_hi(c, act, u0, 0)
            pre.scalar(0, KD)
            split_hi(c, act, u0, 1)
            with act.Fori(1, pairs) as i:
                for j in range(2):
                    split_hi(c, act, u0 + i, j)

        @block.vector
        def _(dve):
            split_lo(c, dve, u0, 0)
            pre.vector(dve, 0, KD)
            split_lo(c, dve, u0, 1)

            def add(i, j):
                dve.wait_ge(c.tile_used, 2 * (u0 + i) + j + 3)
                place = bass.ds((i * 2 + j) * 2, 2)
                if out is None:
                    x = c.x_t[:, place, :]
                    nc.vector.tensor_tensor(x, x, ps[:, 2 * j:2 * j + 2, :], ALU.add).then_inc(added, 1)
                else:
                    nc.vector.tensor_copy(out[:, place, :], ps[:, 2 * j:2 * j + 2, :]).then_inc(added, 1)

            with dve.Fori(0, pairs - 1) as i:
                for j in range(2):
                    add(i, j)
                    split_lo(c, dve, u0 + i + 1, j)
            for j in range(2):
                add(pairs - 1, j)

        @block.tensor
        def _(pe):
            for j in range(2):
                wait_tile(c, pe, u0, j)
                products_as_ready(c, pe, pre, wide_jobs(c, h, j))
            with pe.Fori(1, pairs) as i:
                for j in range(2):
                    wait_tile(c, pe, u0 + i, j)
                    pe.wait_ge(added, m0 + i * 2 + j - 1)
                    w_hi, w_lo = w_tile(c, j, KD, 256)
                    for n in range(2):
                        col = slice(n * P, (n + 1) * P)
                        mm = products(c, ps[:, 2 * j + n, :], [
                            ((w_hi[:, k, col], w_lo[:, k, col]), (h[0][:, k, :], h[1][:, k, :])) for k in range(KD)])
                    mm.then_inc(c.tile_used, 1)
    c.use = u0 + pairs


SB_GROUPS = D // 256
Z_OFF = {0: 0, 1: 512, 3: 896, 2: 1024}
Z_COLS = 1280


def z_cols(j, skip=0):
    return slice(Z_OFF[j] + skip, Z_OFF[j] + T - P * j)


def sb_attention(c, gain, w_in, h, o_t, following):
    nc = c.nc
    u0 = c.use
    uq = u0 + 2
    with ExitStack() as ph:
        sb = lambda name, shape, dt=F32: ph.enter_context(nc.sbuf_tensor(f"sb_{name}", shape, dt))
        v = sb("v", [P, TC, D])
        v_group = sb("v_group", [P, TC, 256])
        qk = sb("qk", [P, 4, T])
        a = sb("a", [P, 2, Z_COLS])
        soft = sb("soft", [P, 2, Z_COLS])
        wt = sb("wt", [P, 2, Z_COLS])
        (v_taken, v_grouped, projected, qk_taken, z_done, abs_done, exp_done, ln_done, soft_done, soft_masked,
         sums_done, wt_done, wt_masked, pv_done, o_taken) = (sem(c, f"sb_{n}") for n in (
             "v_taken", "v_grouped", "projected", "qk_taken", "z_done", "abs_done", "exp_done", "ln_done",
             "soft_done", "soft_masked", "sums_done", "wt_done", "wt_masked", "pv_done", "o_taken"))
        ps = c.psum
        pre = Norm(c, ph, "sb", gain, h)
        z = [ps[:, 3 * p:3 * p + 3, :].rearrange("p b n -> p (b n)") for p in range(2)]
        proj, pv = ps[:, 6, :], ps[:, 7, :]
        block = ph.enter_context(nc.Block())
        last = SB_GROUPS - 1

        @block.sync
        def _(sp):
            for j in range(2):
                load_tile(c, sp, u0 + 1, j, wide_parts(c, j, w_in, 2 * D + (2 + j) * 256))
            with sp.Fori(0, SB_GROUPS) as i:
                for j in range(2):
                    load_tile(c, sp, uq + i, j, wide_parts(c, j, w_in, i * 256 + j * D))
            following(sp)

        @block.gpsimd
        def _(pool):
            def group_v(i):
                pool.wait_ge(pv_done, i * 4 + 1)
                pool.tensor_copy(v_group[:, :, :], v[:, :, bass.ds(i * 256, 256)]).then_inc(v_grouped, 1)

            pool.wait_ge(v_taken, 4)
            with pool.Fori(0, SB_GROUPS) as i:
                group_v(i)

        @block.scalar
        def _(act):
            def exp_ln(n, p):
                act.wait_ge(z_done, n + 1)
                act.wait_ge(soft_done, n + 1 if isinstance(n, int) and n == 0 else n)
                nc.scalar.activation(a[:, p], z[p][:, 0:Z_COLS], ACT.Abs).then_inc(abs_done, 1)
                act.wait_ge(abs_done, n + 1)
                nc.scalar.activation(a[:, p], a[:, p], ACT.Exp, scale=-1.0).then_inc(exp_done, 1)
                act.wait_ge(exp_done, n + 1)
                nc.scalar.activation(a[:, p], a[:, p], ACT.Ln, bias=1.0).then_inc(ln_done, 1)

            def weights(n, p, credit=1):
                act.wait_ge(sums_done, n + 2)
                if credit:
                    act.wait_ge(pv_done, n + credit - 1)
                nc.scalar.activation(wt[:, p], z[p][:, 0:Z_COLS], ACT.Exp).then_inc(wt_done, 1)

            def take(i, m):
                act.wait_ge(projected, i * 4 + m + 1)
                act.wait_ge(z_done, i * 4 - (2 if m < 2 else 0))
                nc.scalar.mul(qk[:, m, :], proj, HEAD ** -0.5 if m % 2 == 0 else 1.0).then_inc(qk_taken, 1)

            def splits():
                for j in range(2):
                    split_hi(c, act, u0, j)

            pre.scalar(act, splits)
            act.preload_act_table_set("natural_log_exp_and_others")
            for j in range(2):
                split_hi(c, act, u0 + 1, j)
            for j in range(2):
                split_hi(c, act, uq, j)
            for m in range(4):
                act.wait_ge(projected, m + 1)
                nc.scalar.mul(qk[:, m, :], proj, HEAD ** -0.5 if m % 2 == 0 else 1.0).then_inc(qk_taken, 1)
            exp_ln(0, 0)

            def body(i, more):
                for hh in range(4):
                    if more and hh:
                        for m in ((0,), (1,), (2, 3))[hh - 1]:
                            take(i + 1, m)
                    if hh < 3:
                        exp_ln(i * 4 + hh + 1, (hh + 1) % 2)
                    if more and hh == 0:
                        for j in range(2):
                            split_hi(c, act, uq + i + 1, j)
                    weights(i * 4 + hh, hh % 2, credit=2 if hh == 0 else 1)
                    if more and hh == 3:
                        exp_ln(i * 4 + 4, 0)

            with act.Fori(0, last) as i:
                body(i, True)
            body(last, False)

        @block.vector
        def _(dve):
            def causal(t, ready, done, n, credit=0):
                dve.wait_ge(ready, n + credit + 1)
                for j in range(TC):
                    blk = t[:, Z_OFF[j]:Z_OFF[j] + P]
                    nc.vector.tensor_tensor(blk, blk, c.causal_cap[:, :], ALU.min).then_inc(done, 1)

            def softplus(n, p):
                dve.wait_ge(ln_done, n + 1)
                dve.wait_ge(sums_done, n)
                nc.vector.scalar_tensor_tensor(soft[:, p], z[p][:, 0:Z_COLS], 0.0, a[:, p], ALU.max,
                                               ALU.add).then_inc(soft_done, 1)
                causal(soft[:, p], soft_done, soft_masked, n, 1)

            dve.sem_inc(soft_done, 1)

            def take_v(m, j):
                dve.wait_ge(c.tile_used, 2 * (u0 + m) + j + 3)
                nc.vector.tensor_copy(v[:, :, (2 * m + j) * 256:(2 * m + j + 1) * 256],
                                      ps[:, 2 * j:2 * j + 2, :].rearrange("p b (t n) -> p (b t) n", t=2)
                                      ).then_inc(v_taken, 1)

            pre.vector(dve, lambda: split_lo(c, dve, u0, 0))
            split_lo(c, dve, u0, 1)
            for m in range(2):
                for j in range(2):
                    split_lo(c, dve, u0 + m + 1, j)
                    take_v(m, j)
            dve.sem_inc(o_taken, 1)
            dve.wait_ge(ln_done, 1)
            nc.vector.scalar_tensor_tensor(soft[:, 0], z[0][:, 0:Z_COLS], 0.0, a[:, 0], ALU.max,
                                           ALU.add).then_inc(soft_done, 1)
            causal(soft[:, 0], soft_done, soft_masked, 0, 1)

            def take_o(i, half):
                dve.wait_ge(pv_done, i * 4 + 2 * half + 3)
                nc.vector.tensor_copy(o_t[:, bass.ds(i * 2 + half, 1), :].rearrange("p k t -> p (k t)"),
                                      pv).then_inc(o_taken, 1)

            def body(i, more):
                for hh in range(4):
                    if more and hh == 0:
                        for j in range(2):
                            split_lo(c, dve, uq + i + 1, j)
                    if hh < 3:
                        softplus(i * 4 + hh + 1, (hh + 1) % 2)
                    if hh == 3:
                        take_o(i, 0)
                    causal(wt[:, hh % 2], wt_done, wt_masked, i * 4 + hh)
                    if hh == 3:
                        if more:
                            softplus(i * 4 + 4, 0)
                        take_o(i, 1)

            with dve.Fori(0, last) as i:
                body(i, True)
            body(last, False)

        @block.tensor
        def _(pe):
            def values(m):
                for j in range(2):
                    wait_tile(c, pe, u0 + m, j)
                    if m:
                        pe.wait_ge(v_taken, 2 * (m - 1) + j + 1)
                    w_hi, w_lo = w_tile(c, j, KD, 256)
                    for t in range(TC):
                        tok = slice(t * P, (t + 1) * P)
                        mm = products(c, ps[:, 2 * j + t // 2, (t % 2) * 256:(t % 2 + 1) * 256], [
                            ((h[0][:, k, tok], h[1][:, k, tok]), (w_hi[:, k, :], w_lo[:, k, :])) for k in range(KD)],
                            (lambda k: pre.wait(pe, k)) if m == 0 and j == 0 and t == 0 else None)
                    mm.then_inc(c.tile_used, 1)

            def project_chunk(i, m, first=False):
                j, n = m % 2, m // 2
                if n == 0:
                    wait_tile(c, pe, uq + i, j)
                if not (first and m == 0):
                    pe.wait_ge(qk_taken, i * 4 + m)
                w_hi, w_lo = w_tile(c, j, KD, 256)
                col = slice(n * P, (n + 1) * P)
                mm = products(c, proj, [((w_hi[:, k, col], w_lo[:, k, col]), (h[0][:, k, :], h[1][:, k, :]))
                                        for k in range(KD)])
                mm.then_inc(projected, 1)

            def scores(n, hh, first=False, frees=0):
                p, half = hh % 2, slice(HEAD * (hh % 2), HEAD * (hh % 2) + HEAD)
                q, k = qk[half, 2 * (hh // 2), :], qk[half, 2 * (hh // 2) + 1, :]
                if not first:
                    pe.wait_ge(wt_done, n - 1)
                for j in (0, 1, 3, 2):
                    mm = nc.tensor.matmul(z[p][:, z_cols(j)], k[:, j * P:(j + 1) * P], q[:, j * P:T],
                                          start=(j != 3), stop=False, skip_group_check=True)
                    if j < frees:
                        mm.then_inc(c.tile_used, 1)
                mm.then_inc(z_done, 1)

            def sums(n, hh, frees=0):
                p = hh % 2
                pe.wait_ge(soft_masked, n * 4 + 4)
                for j in (0, 1, 3, 2):
                    mm = nc.tensor.matmul(z[p][:, z_cols(j)], c.neg_tri[:, :], soft[:, p, z_cols(j)], start=False,
                                          stop=False, skip_group_check=True)
                    if j < frees:
                        mm.then_inc(c.tile_used, 1)
                for j in (0, 1, 2):
                    for later in range(j + 1, TC):
                        mm = nc.tensor.matmul(z[p][:, z_cols(j, (later - j) * P)], c.neg_ones[:, :],
                                              soft[:, p, z_cols(later)], start=False, stop=True,
                                              skip_group_check=True)
                mm.then_inc(sums_done, 1)

            def outputs(i, hh):
                p, half = hh % 2, slice(HEAD * (hh % 2), HEAD * (hh % 2) + HEAD)
                if hh == 0:
                    pe.wait_ge(v_grouped, i + 1)
                pe.wait_ge(wt_masked, (i * 4 + hh) * 4 + 4)
                if hh % 2 == 0:
                    pe.wait_ge(o_taken, i * 2 + hh // 2 + 1)
                for j in range(TC):
                    mm = nc.tensor.matmul(pv[half, j * P:T], v_group[:, j, hh * HEAD:(hh + 1) * HEAD],
                                          wt[:, p, z_cols(j)], start=(j == 0), stop=(j == TC - 1),
                                          skip_group_check=True)
                mm.then_inc(pv_done, 1)

            pre.tensor(pe)
            pe.sem_inc(pv_done, 1)
            pe.sem_inc(sums_done, 1)
            for m in range(2):
                values(m)
            for m in range(4):
                project_chunk(0, m, first=True)
            pe.wait_ge(v_taken, 4)
            pe.wait_ge(qk_taken, 2)
            scores(0, 0, first=True, frees=2)
            pe.wait_ge(qk_taken, 4)

            def body(i, more, first=False):
                n = i * 4
                scores(n + 1, 1, first)
                sums(n, 0)
                if more:
                    project_chunk(i + 1, 0)
                scores(n + 2, 2)
                sums(n + 1, 1)
                outputs(i, 0)
                if more:
                    project_chunk(i + 1, 1)
                scores(n + 3, 3)
                sums(n + 2, 2)
                outputs(i, 1)
                if more:
                    project_chunk(i + 1, 2)
                    project_chunk(i + 1, 3)
                sums(n + 3, 3, frees=2 if more else 0)
                outputs(i, 2)
                if more:
                    pe.wait_ge(qk_taken, i * 4 + 8)
                    scores(n + 4, 0)
                outputs(i, 3)

            body(0, True, first=True)
            with pe.Fori(1, last) as i:
                body(i, True)
            body(last, False)
    c.use = uq + SB_GROUPS


ROT = 16 // 2
INV_FREQ = [float(f) for f in np.float32(500000.0) ** (-np.arange(0, 16, 2, dtype=np.float32) / np.float32(16))]
TWO_PI = (6.28125, 0.0019350051879882812, 3.0198672e-07)
ROUND = 12582912.0
SW_HEADS = 16
SW_QK = SW_HEADS + 2


def sw_project(c, gain, w_in, h, qk, v, following):
    nc = c.nc
    u0 = c.use
    with ExitStack() as ph:
        taken = sem(c, "sw_taken")
        ps = c.psum
        pre = Norm(c, ph, "sw", gain, h)
        block = ph.enter_context(nc.Block())

        @block.sync
        def _(sp):
            for j in range(2):
                load_tile(c, sp, u0 + 1, j, wide_parts(c, j, w_in, (2 + j) * 256))
            for j in range(2):
                load_tile(c, sp, u0 + 2, j, wide_parts(c, j, w_in, D + j * P, P))
            following(sp)

        @block.scalar
        def _(act):
            def splits():
                for j in range(2):
                    split_hi(c, act, u0, j)

            pre.scalar(act, splits)
            for m in range(1, 3):
                for j in range(2):
                    split_hi(c, act, u0 + m, j, TILE if m < 2 else KD * P)

        @block.vector
        def _(dve):
            pre.vector(dve, lambda: split_lo(c, dve, u0, 0))
            split_lo(c, dve, u0, 1)
            for m in range(2):
                for j in range(2):
                    split_lo(c, dve, u0 + m + 1, j, TILE if m == 0 else KD * P)
                    dve.wait_ge(c.tile_used, 2 * (u0 + m) + j + 3)
                    nc.vector.tensor_copy(qk[:, :, (2 * m + j) * 256:(2 * m + j + 1) * 256],
                                          ps[:, 2 * j:2 * j + 2, :].rearrange("p b (t n) -> p (b t) n", t=2)
                                          ).then_inc(taken, 1)
            for j, dst in enumerate((qk[:, :, D:D + P], v[:, :, :])):
                dve.wait_ge(c.tile_used, 2 * (u0 + 2) + j + 3)
                nc.vector.tensor_copy(dst, ps[:, 4 + j, :].rearrange("p (t n) -> p t n", t=TC)).then_inc(taken, 1)

        @block.tensor
        def _(pe):
            pre.tensor(pe)
            for m in range(3):
                width = 256 if m < 2 else P
                for j in range(2):
                    wait_tile(c, pe, u0 + m, j)
                    if m == 1:
                        pe.wait_ge(taken, j + 1)
                    w_hi, w_lo = w_tile(c, j, KD, width)
                    for t in range(TC):
                        tok = slice(t * P, (t + 1) * P)
                        out = (ps[:, 2 * j + t // 2, (t % 2) * 256:(t % 2 + 1) * 256] if m < 2
                               else ps[:, 4 + j, t * P:(t + 1) * P])
                        mm = products(c, out, [
                            ((h[0][:, k, tok], h[1][:, k, tok]), (w_hi[:, k, :], w_lo[:, k, :])) for k in range(KD)],
                            (lambda k: pre.wait(pe, k)) if m == 0 and j == 0 and t == 0 else None)
                    mm.then_inc(c.tile_used, 1)
    c.use = u0 + 3


def sw_rotate(c, positions, qk):
    nc = c.nc
    with ExitStack() as ph:
        sb = lambda name, shape, dt=F32: ph.enter_context(nc.sbuf_tensor(f"sw_{name}", shape, dt))
        sq = sb("sq", [P, TC, SW_QK * HEAD])
        rstd = sb("rstd", [P, TC * SW_QK])
        gains = sb("gains", [P, 2, HEAD])
        pos_i = sb("pos_i", [TC, P], I32)
        pos_f = sb("pos_f", [TC, P])
        pos = sb("pos", [P, TC])
        ang = sb("ang", [P, TC, ROT])
        turns = sb("turns", [P, TC, ROT])
        cos = sb("cos", [P, TC, ROT])
        wrap = sb("wrap", [P, TC, ROT])
        prod = [sb(f"prod{n}", [P, TC, SW_QK, ROT]) for n in range(4)]
        pos_loaded, squared, rooted, sined, pos_turned, steps = (
            sem(c, f"sw_{n}") for n in ("pos_loaded", "squared", "rooted", "sined", "pos_turned", "steps"))
        ps = c.psum
        block = ph.enter_context(nc.Block())
        count = [0]

        def step(dve, ins):
            count[0] += 1
            ins.then_inc(steps, 1)
            dve.wait_ge(steps, count[0])

        POS_READY, MEAN_READY, ANGLES_READY = 1, 4, 4 + ROT + 10

        @block.sync
        def _(sp):
            sp.dma_start(pos_i[:, :], positions.rearrange("a (t p) -> (a t) p", p=P)).then_inc(pos_loaded, 16)

        @block.tensor
        def _(pe):
            pe.wait_ge(steps, POS_READY)
            nc.tensor.transpose(ps[:, 7, 0:TC], pos_f[:, :], c.ident[0:TC, 0:TC]).then_inc(pos_turned, 1)

        @block.scalar
        def _(act):
            for t in range(TC):
                nc.scalar.activation(sq[:, t, :], qk[:, t, :], ACT.Square).then_inc(squared, 1)
            act.wait_ge(steps, MEAN_READY)
            nc.scalar.activation(rstd[:, :], rstd[:, :], ACT.Sqrt).then_inc(rooted, 1)
            act.wait_ge(steps, ANGLES_READY)
            nc.scalar.activation(ang[:, :, :], ang[:, :, :], ACT.Sin).then_inc(sined, 1)
            nc.scalar.activation(cos[:, :, :], cos[:, :, :], ACT.Sin).then_inc(sined, 1)

        @block.vector
        def _(dve):
            v = nc.vector
            dve.wait_ge(pos_loaded, 16)
            step(dve, v.tensor_copy(pos_f[:, :], pos_i[:, :]))
            dve.wait_ge(squared, TC)
            step(dve, v.tensor_reduce(rstd[:, :], sq[:, :, :].rearrange("p t (h d) -> p (t h) d", d=HEAD), AX, ALU.add))
            step(dve, v.tensor_scalar(gains[:, 0, :], row_of(c, "sw_q_gain"), HEAD ** -0.5, None, ALU.mult))
            step(dve, v.tensor_scalar(rstd[:, :], rstd[:, :], 1.0 / HEAD, EPS, ALU.mult, ALU.add))
            dve.wait_ge(pos_turned, 1)
            step(dve, v.tensor_copy(pos[:, :], ps[:, 7, 0:TC]))
            for n, f in enumerate(INV_FREQ):
                step(dve, v.tensor_scalar(ang[:, :, n], pos[:, :], f, None, ALU.mult))
            step(dve, v.tensor_scalar(turns[:, :, :], ang[:, :, :], 1.0 / (2 * np.pi), ROUND, ALU.mult, ALU.add))
            step(dve, v.tensor_scalar(turns[:, :, :], turns[:, :, :], -ROUND, None, ALU.add))
            for part in TWO_PI:
                step(dve, v.scalar_tensor_tensor(ang[:, :, :], turns[:, :, :], -part, ang[:, :, :], ALU.mult, ALU.add))
            step(dve, v.tensor_scalar(wrap[:, :, :], ang[:, :, :], np.pi / 2, -2 * np.pi, ALU.is_gt, ALU.mult))
            step(dve, v.scalar_tensor_tensor(cos[:, :, :], ang[:, :, :], np.pi / 2, wrap[:, :, :], ALU.add, ALU.add))
            for t in (ang, cos):
                ins = v.tensor_scalar(t[:, :, :], t[:, :, :], 3.1415925, -3.1415925, ALU.min, ALU.max)
                if t is ang:
                    step(dve, ins)
            ins.then_inc(steps, 1)
            count[0] += 1
            assert count[0] == ANGLES_READY
            dve.wait_ge(rooted, 1)
            step(dve, v.reciprocal(rstd[:, :], rstd[:, :]))
            heads = qk[:, :, :].rearrange("p t (h d) -> p (t h) d", d=HEAD)
            step(dve, v.tensor_tensor(heads, heads, rstd[:, :].unsqueeze(2).broadcast_to([P, TC * SW_QK, HEAD]),
                                      ALU.mult))
            q = qk[:, :, 0:D].rearrange("p t (h d) -> p t h d", d=HEAD)
            k = qk[:, :, D:D + P].rearrange("p t (h d) -> p t h d", d=HEAD)
            for part, gain, n in ((q, gains[:, 0, :], SW_HEADS), (k, row_of(c, "sw_k_gain"), 2)):
                step(dve, v.tensor_tensor(part, part, gain.unsqueeze(1).unsqueeze(1).broadcast_to([P, TC, n, HEAD]),
                                          ALU.mult))
            dve.wait_ge(sined, 2)
            all_heads = qk[:, :, :].rearrange("p t (h d) -> p t h d", d=HEAD)
            x1, x2 = all_heads[:, :, :, 0:ROT], all_heads[:, :, :, ROT:2 * ROT]
            wide = lambda t: t[:, :, :].unsqueeze(2).broadcast_to([P, TC, SW_QK, ROT])
            for n, (x, y) in enumerate(((x1, cos), (x2, ang), (x2, cos), (x1, ang))):
                step(dve, v.tensor_tensor(prod[n][:, :, :, :], x, wide(y), ALU.mult))
            step(dve, v.tensor_tensor(x1, prod[0][:, :, :, :], prod[1][:, :, :, :], ALU.subtract))
            step(dve, v.tensor_tensor(x2, prod[2][:, :, :, :], prod[3][:, :, :, :], ALU.add))


def sw_attention(c, qk, v, o_t):
    nc = c.nc
    pairs = SW_HEADS // 4
    with ExitStack() as ph:
        sb = lambda name, shape, dt=F32: ph.enter_context(nc.sbuf_tensor(f"sw_{name}", shape, dt))
        k_twice = sb("k_twice", [P, 2, TC, 2, HEAD])
        k_t = sb("k_t", [P, 2, P + T])
        q_rows = sb("q_rows", [P, TC, P])
        q_t = sb("q_t", [P, T])
        s = sb("s", [P, 2, 2, TC, 2 * P])
        probs_t = sb("probs_t", [P, 2, TC, 2, P])
        top = sb("top", [P, 2, 2, TC])
        den = sb("den", [P, 2, 2, TC])
        sink = sb("sink", [P, 2, 2, TC])
        (k_copied, k_turned, k_taken, q_copied, q_turned, q_taken, scored, masked, maxed, topped, weighed, sunk, summed,
         inverted, normed, turned, probs_taken, pv_done, o_taken) = (sem(c, f"sw_{n}") for n in (
             "k_copied", "k_turned", "k_taken", "q_copied", "q_turned", "q_taken", "scored", "masked", "maxed",
             "topped", "weighed", "sunk", "summed", "inverted", "normed", "turned", "probs_taken", "pv_done",
             "o_taken"))
        ps = c.psum
        block = ph.enter_context(nc.Block())

        @block.gpsimd
        def _(pool):
            for kv in range(2):
                for r in range(2):
                    pool.tensor_copy(k_twice[:, kv, :, r, :], qk[:, :, D + kv * HEAD:D + (kv + 1) * HEAD]
                                     ).then_inc(k_copied, 1)
            pool.memset(k_t[:, :, 0:P], 0.0).then_inc(k_copied, 1)

            with pool.Fori(0, pairs) as i:
                for kv in range(2):
                    pool.wait_ge(q_turned, i * 2 + kv + 1)
                    pool.tensor_copy(q_rows[:, :, :], qk[:, :, bass.ds(i * P + kv * (pairs * P), P)]
                                     ).then_inc(q_copied, 1)

        @block.scalar
        def _(act):
            def take_q(i, kv):
                act.wait_ge(q_turned, i * 2 + kv + 2)
                nc.scalar.copy(q_t[:, :], ps[:, 0, :]).then_inc(q_taken, 1)

            def weigh(i, kv, e):
                act.wait_ge(topped, i * 4 + kv * 2 + e + 1)
                for t in range(TC):
                    nc.scalar.activation(s[:, kv, e, t, :], s[:, kv, e, t, :], ACT.Exp, bias=top[:, kv, e, t:t + 1],
                                         accum_out=den[:, kv, e, t:t + 1]).then_inc(weighed, 1)
                head = i * 2 + kv * (2 * pairs) + e
                nc.scalar.activation(sink[:, kv, e, :], top[:, kv, e, :], ACT.Exp,
                                     bias=row_of(c, "sw_sinks")[:, bass.ds(head, 1)]).then_inc(sunk, 1)

            def take_probs(i, kv, e):
                act.wait_ge(turned, i * 4 + kv * 2 + e + 1)
                nc.scalar.copy(probs_t[:, e].rearrange("p t b n -> p (t b n)"),
                               ps[:, 5:7, :].rearrange("p b n -> p (b n)")).then_inc(probs_taken, 1)

            for kv in range(2):
                act.wait_ge(k_turned, kv + 1)
                nc.scalar.copy(k_t[:, kv, P:P + T], ps[:, kv, :]).then_inc(k_taken, 1)
            take_q(0, 0)
            for e in range(2):
                weigh(0, 0, e)

            def turn(i, kv):
                take_q(i + kv, 1 - kv)
                for e in range(2):
                    take_probs(i, kv, e)
                    weigh(i + kv, 1 - kv, e)

            with act.Fori(0, pairs - 1) as i:
                turn(i, 0)
                turn(i, 1)
            turn(pairs - 1, 0)
            for e in range(2):
                take_probs(pairs - 1, 1, e)

        @block.vector
        def _(dve):
            v_ = nc.vector
            sinks = row_of(c, "sw_sinks")

            def mask(i, kv, e):
                n = i * 4 + kv * 2 + e
                dve.wait_ge(scored, n + 1)
                v_.tensor_tensor(s[:, kv, e], ps[:, 1 + 2 * e:3 + 2 * e, :].rearrange("p b (t n) -> p (b t) n", t=2),
                                 c.swa_mask[:, :, :], ALU.add).then_inc(masked, 1)
                dve.wait_ge(masked, n + 1)
                v_.tensor_reduce(top[:, kv, e, :], s[:, kv, e], AX, ALU.max).then_inc(maxed, 1)
                dve.wait_ge(maxed, n + 1)
                head = i * 2 + kv * (2 * pairs) + e
                v_.tensor_scalar(top[:, kv, e, :], top[:, kv, e, :], sinks[:, bass.ds(head, 1)], -1.0, ALU.max,
                                 ALU.mult).then_inc(topped, 1)

            def norm_weights(i, kv, e):
                n = i * 4 + kv * 2 + e
                dve.wait_ge(weighed, n * TC + TC)
                dve.wait_ge(sunk, n + 1)
                v_.tensor_tensor(den[:, kv, e, :], den[:, kv, e, :], sink[:, kv, e, :], ALU.add).then_inc(summed, 1)
                dve.wait_ge(summed, n + 1)
                v_.reciprocal(den[:, kv, e, :], den[:, kv, e, :]).then_inc(inverted, 1)
                dve.wait_ge(inverted, n + 1)
                v_.tensor_tensor(s[:, kv, e], s[:, kv, e],
                                 den[:, kv, e, :].unsqueeze(2).broadcast_to([P, TC, 2 * P]),
                                 ALU.mult).then_inc(normed, 1)

            def take_out(i, kv):
                dve.wait_ge(pv_done, i * 4 + kv * 2 + 2)
                v_.tensor_copy(o_t[:, bass.ds(i + kv * pairs, 1), :].rearrange("p k t -> p (k t)"), ps[:, 7, :]
                               ).then_inc(o_taken, 1)

            def turn(i, kv):
                norm_weights(i, kv, 1)
                for e in range(2):
                    mask(i + kv, 1 - kv, e)
                norm_weights(i + kv, 1 - kv, 0)
                take_out(i, kv)

            dve.sem_inc(o_taken, 1)
            for e in range(2):
                mask(0, 0, e)
            norm_weights(0, 0, 0)
            with dve.Fori(0, pairs - 1) as i:
                turn(i, 0)
                turn(i, 1)
            turn(pairs - 1, 0)
            norm_weights(pairs - 1, 1, 1)
            take_out(pairs - 1, 1)

        @block.tensor
        def _(pe):
            pe.wait_ge(k_copied, 5)
            for kv in range(2):
                for t in range(TC):
                    mm = nc.tensor.transpose(ps[:, kv, t * P:(t + 1) * P],
                                             k_twice[:, kv, t].rearrange("p r d -> p (r d)"), c.ident[:, :])
                mm.then_inc(k_turned, 1)
            pe.wait_ge(k_taken, 2)
            pe.sem_inc(q_turned, 1)

            def turn_q(i, kv, first=False):
                n = i * 2 + kv
                pe.wait_ge(q_copied, n + 1)
                if not first:
                    pe.wait_ge(q_taken, n)
                for t in range(TC):
                    mm = nc.tensor.transpose(ps[:, 0, t * P:(t + 1) * P], q_rows[:, t, :], c.ident[:, :])
                mm.then_inc(q_turned, 1)

            def scores(i, kv, e, first=False):
                n = i * 2 + kv
                half = slice(e * HEAD, (e + 1) * HEAD)
                pe.wait_ge(q_taken, n + 1)
                if not first:
                    pe.wait_ge(masked, n * 2 + e - 1)
                for t in range(TC):
                    mm = nc.tensor.matmul(ps[:, 1 + 2 * e + t // 2, (t % 2) * 256:(t % 2 + 1) * 256],
                                          q_t[half, t * P:(t + 1) * P], k_t[half, kv, t * P:(t + 2) * P],
                                          start=True, stop=True)
                mm.then_inc(scored, 1)

            def turn_weights(i, kv, e):
                pe.wait_ge(normed, i * 4 + kv * 2 + e + 1)
                for t in range(TC):
                    for b in range(2):
                        m = 2 * t + b
                        mm = nc.tensor.transpose(ps[:, 5 + m // 4, (m % 4) * P:(m % 4 + 1) * P],
                                                 s[:, kv, e, t, b * P:(b + 1) * P], c.ident[:, :])
                mm.then_inc(turned, 1)

            def outputs(i, kv, e):
                half = slice(e * HEAD, (e + 1) * HEAD)
                pe.wait_ge(probs_taken, i * 4 + kv * 2 + e + 1)
                if e == 0:
                    pe.wait_ge(o_taken, i * 2 + kv + 1)
                for t in range(TC):
                    blocks = (0, 1) if t else (1,)
                    for b in blocks:
                        mm = nc.tensor.matmul(ps[half, 7, t * P:(t + 1) * P],
                                              v[:, t - 1 + b, kv * HEAD:(kv + 1) * HEAD], probs_t[:, e, t, b, :],
                                              start=(b == blocks[0]), stop=(b == 1))
                mm.then_inc(pv_done, 1)

            def turn(i, kv, more=True):
                if more:
                    turn_q(i + kv, 1 - kv)
                for e in range(2):
                    turn_weights(i, kv, e)
                    if more:
                        scores(i + kv, 1 - kv, e)
                    outputs(i, kv, e)

            turn_q(0, 0, first=True)
            for e in range(2):
                scores(0, 0, e, first=True)
            with pe.Fori(0, pairs - 1) as i:
                turn(i, 0)
                turn(i, 1)
            turn(pairs - 1, 0)
            turn(pairs - 1, 1, more=False)


SSD_IN = 2048
GROUPS = 8
G_COLS = SSD_IN // GROUPS
G_HEADS = 4
TAPS = 4
Z_AT, XS_AT, B_AT, C_AT, DT_AT, SB_AT, SC_AT, SX_AT, GATE_AT = 0, 2048, 4096, 5120, 6144, 6176, 7200, 8224, 9248
HALF_TM = TM // 2


def gate_rows(c, slot, w, col):
    v = w.rearrange("(k p) n -> p k n", p=P)
    dst = raw_tile(c, slot, KD // 2, G_COLS)
    at, n = slot * KD // 2, KD // 4
    return [(dst[:, k:k + n, :], v[:, at + k:at + k + n, bass.ds(col, G_COLS)]) for k in (0, n)]


def ssd_first(c, w_in, use, g=0):
    def go(sp):
        load_tile(c, sp, use, 0, wide_parts(c, 0, w_in, g * G_COLS + XS_AT))
        load_tile(c, sp, use, 1, pair_parts(c, 1, w_in, g * P + B_AT, g * P + C_AT))
    return go


def widen(c, meta, xm):
    nc = c.nc
    with ExitStack() as ph:
        rows = ph.enter_context(nc.sbuf_tensor("meta_rows", [META, D], F32))
        loaded, turned = sem(c, "meta_loaded"), sem(c, "meta_turned")
        ps = c.psum
        block = ph.enter_context(nc.Block())

        @block.sync
        def _(sp):
            sp.dma_start(rows[:, :], meta).then_inc(loaded, 16)

        @block.tensor
        def _(pe):
            pe.wait_ge(loaded, 16)
            for k in range(KD):
                mm = nc.tensor.transpose(ps[:, 0, k * META:(k + 1) * META], rows[:, k * P:(k + 1) * P],
                                         c.ident[0:META, 0:META])
            mm.then_inc(turned, 1)

        @block.scalar
        def _(act):
            nc.scalar.copy(xm[:, :, META:TM], c.x_t[:, :, :])

        @block.vector
        def _(dve):
            dve.wait_ge(turned, 1)
            nc.vector.tensor_copy(xm[:, :, 0:META], ps[:, 0, 0:KD * META].rearrange("p (k t) -> p k t", k=KD))


class Decay:
    pass


def ssd_times(c, w_in, h, dec, conv_w, conv_dst):
    nc = c.nc
    NH = 32
    with ExitStack() as ph:
        sb = lambda name, shape, dt=F32: ph.enter_context(nc.sbuf_tensor(f"dt_{name}", shape, dt))
        w_raw = sb("w_raw", [P, KD, NH])
        w_hi = sb("w_hi", [P, KD, NH], F32R)
        w_lo = sb("w_lo", [P, KD, NH], F32R)
        v = sb("v", [P, TC + 1, NH])
        e = sb("e", [P, TC + 1, NH])
        a = sb("a", [P, NH])
        total = sb("total", [P, TC + 1, NH])
        loaded, conv_loaded, acts, steps, pe_done = (sem(c, f"dt_{n}") for n in
                                                     ("loaded", "conv_loaded", "acts", "steps", "pe_done"))
        ps = c.psum
        dt_ps = ps[:, 0, 0:(TC + 1) * NH].rearrange("p (t n) -> p t n", n=NH)
        sum_ps = ps[:, 1, 0:(TC + 1) * NH].rearrange("p (t n) -> p t n", n=NH)
        tot_ps = ps[:, 2, 0:(TC + 1) * NH].rearrange("p (t n) -> p t n", n=NH)
        block = ph.enter_context(nc.Block())
        x_ = slice(0, TC)

        @block.sync
        def _(sp):
            sp.dma_start(w_raw[:, :, :], w_in.rearrange("(k p) n -> p k n", p=P)[:, :, DT_AT:DT_AT + NH]
                         ).then_inc(loaded, 16)
            sp.dma_start(conv_dst[0][:, :, :], conv_w[0].rearrange("(k p) n -> p k n", p=P)).then_inc(conv_loaded, 16)
            sp.dma_start(conv_dst[1][:, :, :], conv_w[1].rearrange("(k p) n -> p k n", p=P)).then_inc(conv_loaded, 16)
            sp.wait_ge(conv_loaded, 32)

        @block.scalar
        def _(act):
            acted = [0]

            def does(after, *args, **kw):
                if after:
                    act.wait_ge(steps, after)
                nc.scalar.activation(*args, **kw).then_inc(acts, 1)
                acted[0] += 1
                act.wait_ge(acts, acted[0])

            act.wait_ge(loaded, 16)
            nc.scalar.copy(w_hi[:, :, :], w_raw[:, :, :]).then_inc(acts, 1)
            acted[0] = 1
            act.preload_act_table_set("natural_log_exp_and_others")
            does(0, a[:, :], row_of(c, "ssd_a_log"), ACT.Exp)
            does(2, e[:, :, :], v[:, :, :], ACT.Abs)
            does(0, e[:, :, :], e[:, :, :], ACT.Exp, scale=-1.0)
            does(0, e[:, :, :], e[:, :, :], ACT.Ln, bias=1.0)
            does(11, dec.from_start[:, :, :], dec.sums[:, x_, :], ACT.Exp)
            does(0, total[:, :, :], total[:, :, :], ACT.Exp)
            does(0, dec.whole[:, :, :], dec.whole[:, :, :], ACT.Exp)

        @block.vector
        def _(dve):
            n = [0]

            def step(ins):
                n[0] += 1
                ins.then_inc(steps, 1)
                dve.wait_ge(steps, n[0])

            V = nc.vector
            dve.wait_ge(acts, 1)
            step(V.tensor_tensor(w_lo[:, :, :], w_raw[:, :, :], w_hi[:, :, :].bitcast(F32), ALU.subtract))
            dve.wait_ge(pe_done, 1)
            bias = row_of(c, "ssd_dt_bias").unsqueeze(1).broadcast_to([P, TC + 1, NH])
            step(V.tensor_tensor(v[:, :, :], dt_ps, bias, ALU.add))
            dve.wait_ge(acts, 5)
            step(V.scalar_tensor_tensor(dec.dt[:, :, :], v[:, :, :], 0.0, e[:, :, :], ALU.max, ALU.add))
            step(V.tensor_scalar(a[:, :], a[:, :], -1.0, None, ALU.mult))
            step(V.tensor_tensor(dec.adt[:, :, :], dec.dt[:, :, :],
                                 a[:, :].unsqueeze(1).broadcast_to([P, TC + 1, NH]), ALU.mult))
            dve.wait_ge(pe_done, 2)
            step(V.tensor_copy(dec.sums[:, x_, :], sum_ps[:, x_, :]))
            step(V.tensor_copy(dec.sums[0:META, TC, :], sum_ps[0:META, TC, :]))
            step(V.tensor_copy(dec.whole[:, :, :], tot_ps[:, x_, :]))
            step(V.tensor_tensor(total[:, x_, :], tot_ps[:, x_, :], dec.sums[:, x_, :], ALU.subtract))
            step(V.memset(total[:, TC, :], 0.0))
            step(V.tensor_tensor(total[0:META, TC, :], tot_ps[0:META, TC, :], dec.sums[0:META, TC, :], ALU.subtract))
            dve.wait_ge(acts, 8)
            step(V.tensor_tensor(dec.dt_end[:, :, :], dec.dt[:, :, :], total[:, :, :], ALU.mult))

        @block.tensor
        def _(pe):
            pe.wait_ge(steps, 1)
            for t in range(TC + 1):
                tok = slice(META + t * P, META + (t + 1) * P) if t < TC else slice(0, P)
                mm = products(c, dt_ps[:, t, :], [
                    ((h[0][:, k, tok], h[1][:, k, tok]), (w_hi[:, k, :], w_lo[:, k, :])) for k in range(KD)])
            mm.then_inc(pe_done, 1)
            pe.wait_ge(steps, 5)
            for lhs, out in ((c.tri_up, sum_ps), (c.ones, tot_ps)):
                nc.tensor.matmul(out[:, x_, :], lhs[:, :], dec.adt[:, x_, :], start=True, stop=True)
                mm = nc.tensor.matmul(out[:, TC, :], lhs[0:META, :], dec.adt[0:META, TC, :], start=True, stop=True)
            mm.then_inc(pe_done, 1)


def ssd(c, w_in, h, dec, conv_w, y_t, following):
    nc = c.nc
    u0 = c.use
    with ExitStack() as ph:
        sb = lambda name, shape, dt=F32: ph.enter_context(nc.sbuf_tensor(f"ssd_{name}", shape, dt))
        raw = sb("raw", [P, 4, TAPS - 1 + TM])
        xbc = sb("xbc", [P, 4, TM])
        rows = sb("rows", [P, 2, 4 * P])
        meta_rows = sb("meta_rows", [P, 4 * P])
        meta_in = sb("meta_in", [META, G_COLS])
        gate = sb("gate", [P, TC, G_COLS])
        spread = sb("spread", [P, 2, G_HEADS, P])
        seg = sb("seg", [P, 2, G_HEADS, P])
        cb = sb("cb", [P, 2, P])
        x_dt = sb("x_dt", [P, 2, G_COLS])
        x_end = sb("x_end", [P, 2, G_COLS])
        skip = sb("skip", [P, 2, G_COLS])
        state = sb("state", [P, G_COLS])
        y = sb("y", [P, TC, G_COLS])
        y_sq = sb("y_sq", [P, G_COLS])
        mean = sb("mean", [P, TC])
        rstd = sb("rstd", [P, TC])
        power = sb("power", [P, TC])
        names = ("half_done raw_taken zeroed conv_step conv_done silu_done gate_taken turned rows_taken spread_done "
                 "sums_ready seg_sub seg_min decayed cb_done m_done x_end_done skip_done advanced state_kept "
                 "state_new y_off_in y_in y_skipped y_gated squared mean_done rooted y_normed y_turned y_taken").split()
        (half_done, raw_taken, zeroed, conv_step, conv_done, silu_done, gate_taken, turned, rows_taken, spread_done,
         sums_ready, seg_sub, seg_min, decayed, cb_done, m_done, x_end_done, skip_done, advanced, state_kept,
         state_new, y_off_in, y_in, y_skipped, y_gated, squared, mean_done, rooted, y_normed, y_turned, y_taken) = (
             sem(c, f"ssd_{n}") for n in names)
        ps = c.psum
        chan_ps = ps[:, 0:2, 0:HALF_TM]
        gate_ps = ps[:, 2:4, :].rearrange("p b (t n) -> p (b t) n", t=2)
        rows_ps, sums_ps, y_ps, state_ps = ps[:, 4, :], ps[:, 5, :], ps[:, 6, :], ps[:, 7, 0:G_COLS]
        block = ph.enter_context(nc.Block())
        last = GROUPS - 1
        UA = lambda g: u0 + g * 2
        UB = lambda g: u0 + g * 2 + 1
        heads = lambda t: t.rearrange("p (r d) -> p r d", r=G_HEADS)
        wide = lambda t, n: t.unsqueeze(2).broadcast_to([t.shape[0], G_HEADS, n])

        def of_group(t, i):
            return t[:, bass.ds(i * G_HEADS, G_HEADS)]

        @block.sync
        def _(sp):
            def gates(g):
                for j in range(2):
                    load_tile(c, sp, UB(g), j, gate_rows(c, j, w_in, (g * 2) * P + Z_AT))

            gates(0)
            with sp.Fori(1, GROUPS) as g:
                ssd_first(c, w_in, UA(g), g)(sp)
                gates(g)
            following(sp)

        @block.gpsimd
        def _(pool):
            pool.memset(raw[:, :, 0:TAPS - 1], 0.0).then_inc(zeroed, 1)
            pool.memset(power[:, :], -0.5).then_inc(zeroed, 1)
            pool.wait_ge(zeroed, 2)

            def apart():
                pool.wait_ge(zeroed, 2)

            def spread_dt(i, t):
                apart()
                if t >= 2:
                    pool.wait_ge(sums_ready, i * TC + t - 1)
                elif not (isinstance(i, int) and i == 0):
                    pool.wait_ge(sums_ready, i * TC + t - 1)
                pool.tensor_tensor(spread[:, t % 2], c.tri_up[:, :].unsqueeze(1).broadcast_to([P, G_HEADS, P]),
                                   wide(of_group(dec.adt[:, t, :], i), P), ALU.mult).then_inc(spread_done, 1)

            def body(i):
                spread_dt(i, 0)
                spread_dt(i, 1)
                apart()
                pool.wait_ge(rows_taken, i * 5 + 1)
                pool.tensor_tensor(heads(meta_in[:, :]), heads(meta_rows[0:META, 0:G_COLS]),
                                   wide(of_group(dec.dt_end[0:META, TC, :], i), HEAD), ALU.mult).then_inc(x_end_done, 1)
                for t in range(TC):
                    apart()
                    pool.wait_ge(rows_taken, i * 5 + t + 2)
                    if t >= 2:
                        pool.wait_ge(advanced, i * 5 + t)
                    pool.tensor_tensor(heads(x_end[:, t % 2, :]), heads(rows[:, t % 2, 0:G_COLS]),
                                       wide(of_group(dec.dt_end[:, t, :], i), HEAD), ALU.mult).then_inc(x_end_done, 1)
                    apart()
                    if t >= 2:
                        pool.wait_ge(y_skipped, i * TC + t - 1)
                    pool.tensor_tensor(heads(skip[:, t % 2, :]), heads(rows[:, t % 2, 0:G_COLS]),
                                       wide(of_group(row_of(c, "ssd_d"), i), HEAD), ALU.mult).then_inc(skip_done, 1)
                    if t < 2:
                        spread_dt(i, t + 2)
                pool.wait_ge(mean_done, i + 1)
                pool.tensor_tensor(rstd[:, :], mean[:, :], power[:, :], ALU.pow).then_inc(rooted, 1)

            body(0)
            with pool.Fori(1, GROUPS) as i:
                body(i)

        @block.scalar
        def _(act):
            def take(i, m, first=False):
                if m % 2 == 0:
                    act.wait_ge(half_done, i * 2 + m // 2 + 1)
                else:
                    act.wait_ge(c.tile_used, 2 * UA(i) + 3 + m // 2)
                if not first:
                    act.wait_ge(conv_done, i * 4 + m - 3)
                nc.scalar.copy(raw[:, m, TAPS - 1:].rearrange("p (b n) -> p b n", b=2), chan_ps).then_inc(raw_taken, 1)

            def silu(i, m):
                chunk = (i * 2, i * 2 + 1, i + SSD_IN // P, i + (SSD_IN + D) // P)[m]
                act.wait_ge(conv_done, i * 4 + m + 1)
                at = vec_at("ssd_conv_b")
                nc.scalar.activation(xbc[:, m, :], xbc[:, m, :], ACT.Silu,
                                     bias=c.vec[:, bass.ds(chunk + at, 1)]).then_inc(silu_done, 1)

            def copy_rows(i, t):
                act.wait_ge(turned, i * 5 + t + 2)
                if t >= 2:
                    act.wait_ge(advanced, i * 5 + t)
                    act.wait_ge(skip_done, i * TC + t - 1)
                nc.scalar.copy(rows[:, t % 2, :], rows_ps).then_inc(rows_taken, 1)

            def decay(i, t):
                act.wait_ge(seg_min, i * TC + t + 1)
                nc.scalar.activation(seg[:, t % 2], seg[:, t % 2], ACT.Exp).then_inc(decayed, 1)

            def square(i, t):
                act.wait_ge(y_gated, i * TC + t + 1)
                if t or not (isinstance(i, int) and i == 0):
                    act.wait_ge(squared, i * TC + t)
                nc.scalar.activation(y_sq[:, :], y[:, t, :], ACT.Square, accum_out=mean[:, t:t + 1]
                                     ).then_inc(squared, 1)

            def body(i, more, more2):
                act.wait_ge(c.tile_used, 2 * UB(i) + 4)
                nc.scalar.activation(gate[:, :, :], gate_ps, ACT.Silu).then_inc(gate_taken, 1)
                silu(i, 0)
                if more:
                    take(i + 1, 0)
                silu(i, 1)
                silu(i, 2)
                if more:
                    take(i + 1, 1)
                    split_hi(c, act, UB(i + 1), 0, KD * P)
                silu(i, 3)
                if more:
                    take(i + 1, 2)
                act.wait_ge(turned, i * 5 + 1)
                nc.scalar.copy(meta_rows[:, :], rows_ps).then_inc(rows_taken, 1)
                copy_rows(i, 0)
                decay(i, 0)
                copy_rows(i, 1)
                decay(i, 1)
                square(i, 0)
                copy_rows(i, 2)
                decay(i, 2)
                square(i, 1)
                if more:
                    take(i + 1, 3)
                    split_hi(c, act, UB(i + 1), 1, KD * P)
                copy_rows(i, 3)
                decay(i, 3)
                square(i, 2)
                if more2:
                    split_hi(c, act, UA(i + 2), 0)
                square(i, 3)
                if more2:
                    split_hi(c, act, UA(i + 2), 1)

            act.wait_ge(zeroed, 2)
            for j in range(2):
                split_hi(c, act, UA(0), j)
            take(0, 0, True)
            take(0, 1, True)
            split_hi(c, act, UB(0), 0, KD * P)
            take(0, 2, True)
            take(0, 3, True)
            split_hi(c, act, UB(0), 1, KD * P)
            for j in range(2):
                split_hi(c, act, UA(1), j)
            body(0, True, True)
            with act.Fori(1, last - 1) as i:
                body(i, True, True)
            body(last - 1, True, False)
            body(last, False, False)

        @block.vector
        def _(dve):
            V = nc.vector

            def conv(i, m):
                chunk = (i * 2, i * 2 + 1, i + SSD_IN // P, i + (SSD_IN + D) // P)[m]
                tap = lambda k: conv_w[:, bass.ds(chunk, 1), k]
                dve.wait_ge(raw_taken, i * 4 + m + 1)
                V.tensor_scalar(xbc[:, m, :], raw[:, m, 0:TM], tap(0), None, ALU.mult).then_inc(conv_step, 1)
                for k in range(1, TAPS):
                    dve.wait_ge(conv_step, i * 12 + m * 3 + k)
                    V.scalar_tensor_tensor(xbc[:, m, :], raw[:, m, k:k + TM], tap(k), xbc[:, m, :], ALU.mult,
                                           ALU.add).then_inc(conv_step if k < TAPS - 1 else conv_done, 1)

            def pre(i, t):
                p, n = t % 2, i * TC + t
                later = not (isinstance(i, int) and i == 0 and t < 2)
                dve.wait_ge(sums_ready, n + 1)
                if later:
                    dve.wait_ge(advanced, i * 5 + (t if t >= 2 else t - 1))
                V.tensor_tensor(seg[:, p], sums_ps.rearrange("p (r l) -> p r l", r=G_HEADS),
                                wide(of_group(dec.sums[:, t, :], i), P), ALU.subtract).then_inc(seg_sub, 1)
                dve.wait_ge(seg_sub, n + 1)
                V.tensor_scalar(seg[:, p], seg[:, p], 0.0, None, ALU.min).then_inc(seg_min, 1)
                dve.wait_ge(rows_taken, i * 5 + t + 2)
                V.tensor_tensor(heads(x_dt[:, p, :]), heads(rows[:, p, 0:G_COLS]),
                                wide(of_group(dec.dt[:, t, :], i), HEAD), ALU.mult)
                V.tensor_tensor(cb[:, p, :], rows[:, p, 3 * P:4 * P], c.tri_up[:, :], ALU.mult).then_inc(cb_done, 1)
                dve.wait_ge(cb_done, n + 1)
                dve.wait_ge(decayed, n + 1)
                V.tensor_tensor(seg[:, p], seg[:, p], cb[:, p, :].unsqueeze(1).broadcast_to([P, G_HEADS, P]),
                                ALU.mult).then_inc(m_done, 1)

            def post(i, t):
                p, n = t % 2, i * TC + t
                dve.wait_ge(advanced, i * 5 + t + 2)
                V.tensor_tensor(heads(state[:, :]), heads(state[:, :]), wide(of_group(dec.whole[:, t, :], i), HEAD),
                                ALU.mult).then_inc(state_kept, 1)
                V.tensor_tensor(heads(y[:, t, :]), heads(y_ps[:, G_COLS:]),
                                wide(of_group(dec.from_start[:, t, :], i), HEAD), ALU.mult).then_inc(y_off_in, 1)
                dve.wait_ge(state_kept, n + 1)
                V.tensor_tensor(state[:, :], state[:, :], state_ps, ALU.add).then_inc(state_new, 1)
                dve.wait_ge(y_off_in, n + 1)
                V.tensor_tensor(y[:, t, :], y[:, t, :], y_ps[:, 0:G_COLS], ALU.add).then_inc(y_in, 1)
                dve.wait_ge(skip_done, n + 1)
                dve.wait_ge(y_in, n + 1)
                V.tensor_tensor(y[:, t, :], y[:, t, :], skip[:, p, :], ALU.add).then_inc(y_skipped, 1)
                dve.wait_ge(y_skipped, n + 1)
                dve.wait_ge(gate_taken, i + 1)
                V.tensor_tensor(y[:, t, :], y[:, t, :], gate[:, t, :], ALU.mult).then_inc(y_gated, 1)

            def take_y(i):
                dve.wait_ge(y_turned, i + 1)
                for j in range(2):
                    V.tensor_scalar(y_t[:, bass.ds(i * 2 + j, 1), :].rearrange("p k t -> p (k t)"), ps[:, 6 + j, :],
                                    c.vec[:, bass.ds(i * 2 + j + vec_at("ssd_norm"), 1)], None, ALU.mult).then_inc(y_taken, 1)

            def body(i, more, more2):
                for m in range(4):
                    conv(i, m)
                    if m == 1 and not (isinstance(i, int) and i == 0):
                        take_y(i - 1)
                if more:
                    split_lo(c, dve, UB(i + 1), 0, KD * P)
                dve.wait_ge(advanced, i * 5 + 1)
                V.tensor_copy(state[:, :], state_ps).then_inc(state_new, 1)
                pre(i, 0)
                pre(i, 1)
                post(i, 0)
                pre(i, 2)
                post(i, 1)
                if more:
                    split_lo(c, dve, UB(i + 1), 1, KD * P)
                pre(i, 3)
                post(i, 2)
                if more2:
                    split_lo(c, dve, UA(i + 2), 0)
                post(i, 3)
                dve.wait_ge(squared, i * TC + TC)
                V.tensor_scalar(mean[:, :], mean[:, :], 1.0 / G_COLS, EPS, ALU.mult, ALU.add).then_inc(mean_done, 1)
                dve.wait_ge(rooted, i + 1)
                dve.wait_ge(y_gated, i * TC + TC)
                V.tensor_tensor(y[:, :, :], y[:, :, :], rstd[:, :].unsqueeze(2).broadcast_to([P, TC, G_COLS]),
                                ALU.mult).then_inc(y_normed, 1)
                if more2:
                    split_lo(c, dve, UA(i + 2), 1)

            for u, j, cols in ((UA(0), 0, TILE), (UA(0), 1, TILE), (UB(0), 0, KD * P), (UB(0), 1, KD * P),
                               (UA(1), 0, TILE), (UA(1), 1, TILE)):
                split_lo(c, dve, u, j, cols)
            body(0, True, True)
            with dve.Fori(1, last - 1) as i:
                body(i, True, True)
            body(last - 1, True, False)
            body(last, False, False)
            take_y(last)

        @block.tensor
        def _(pe):
            def channels(i, m):
                j = m // 2
                if m % 2 == 0:
                    wait_tile(c, pe, UA(i), j)
                if not (isinstance(i, int) and i == 0 and m == 0):
                    pe.wait_ge(raw_taken, i * 4 + m)
                if j == 0:
                    w_hi, w_lo = (t[:, :, (m % 2) * P:(m % 2 + 1) * P] for t in w_tile(c, 0, KD, 256))
                else:
                    w_hi, w_lo = (part[:, 1, :].rearrange("p (j k n) -> p j k n", j=2, k=KD)[:, m % 2]
                                  for part in (c.hi, c.lo))
                for b in range(2):
                    tok = slice(b * HALF_TM, (b + 1) * HALF_TM)
                    mm = products(c, chan_ps[:, b, :], [
                        ((w_hi[:, k, :], w_lo[:, k, :]), (h[0][:, k, tok], h[1][:, k, tok])) for k in range(KD)])
                mm.then_inc(c.tile_used if m % 2 else half_done, 1)

            def gates(i, j):
                wait_tile(c, pe, UB(i), j)
                if not (isinstance(i, int) and i == 0):
                    pe.wait_ge(gate_taken, i)
                w_hi, w_lo = w_tile(c, j, KD // 2, G_COLS)
                for t in range(TC):
                    tok = slice(META + t * P, META + (t + 1) * P)
                    for n in range(KD // 2):
                        k = j * (KD // 2) + n
                        start, stop = k == 0 and t % 2 == 0, k == KD - 1
                        out = gate_ps[:, t, :]
                        nc.tensor.matmul(out, h[0][:, k, tok], w_hi[:, n, :], start=start, stop=False,
                                         skip_group_check=True)
                        nc.tensor.matmul(out, h[0][:, k, tok], w_lo[:, n, :], start=False, stop=False,
                                         skip_group_check=True)
                        mm = nc.tensor.matmul(out, h[1][:, k, tok], w_hi[:, n, :], start=False, stop=stop,
                                              skip_group_check=True)
                mm.then_inc(c.tile_used, 1)

            def turn(tok):
                for m in range(3):
                    mm = nc.tensor.transpose(rows_ps[:, m * P:(m + 1) * P], xbc[:, m, tok], c.ident[:, :])
                return nc.tensor.matmul(rows_ps[:, 3 * P:4 * P], xbc[:, 2, tok], xbc[:, 3, tok], start=True, stop=True)

            def first_half(i, t):
                pe.wait_ge(rows_taken, i * 5 + t + 1)
                turn(slice(META + t * P, META + (t + 1) * P)).then_inc(turned, 1)
                pe.wait_ge(spread_done, i * TC + t + 1)
                if not (isinstance(i, int) and i == 0 and t == 0):
                    pe.wait_ge(seg_sub, i * TC + t)
                nc.tensor.matmul(sums_ps, c.ones[:, :], spread[:, t % 2].rearrange("p r l -> p (r l)"), start=True,
                                 stop=True).then_inc(sums_ready, 1)

            def second_half(i, t):
                p = t % 2
                pe.wait_ge(x_end_done, i * 5 + t + 2)
                pe.wait_ge(m_done, i * TC + t + 1)
                pe.wait_ge(state_new, i * 5 + t + 1)
                if t:
                    pe.wait_ge(y_in, i * TC + t)
                for r in range(G_HEADS):
                    nc.tensor.matmul(y_ps[:, r * HEAD:(r + 1) * HEAD], seg[:, p, r, :],
                                     x_dt[:, p, r * HEAD:(r + 1) * HEAD], start=True, stop=True)
                nc.tensor.matmul(y_ps[:, G_COLS:], xbc[:, 3, META + t * P:META + (t + 1) * P], state[:, :], start=True,
                                 stop=True)
                nc.tensor.matmul(state_ps, rows[:, p, 2 * P:3 * P], x_end[:, p, :], start=True,
                                 stop=True).then_inc(advanced, 1)

            def turn_y(i):
                pe.wait_ge(y_normed, i + 1)
                for j in range(2):
                    for t in range(TC):
                        mm = nc.tensor.transpose(ps[:, 6 + j, t * P:(t + 1) * P], y[:, t, j * P:(j + 1) * P],
                                                 c.ident[:, :])
                mm.then_inc(y_turned, 1)

            def body(i, more):
                if more:
                    channels(i + 1, 0)
                if not (isinstance(i, int) and i == 0):
                    turn_y(i - 1)
                if more:
                    channels(i + 1, 1)
                    channels(i + 1, 2)
                pe.wait_ge(silu_done, i * 4 + 4)
                if not (isinstance(i, int) and i == 0):
                    pe.wait_ge(rows_taken, i * 5)
                turn(slice(0, P)).then_inc(turned, 1)
                pe.wait_ge(x_end_done, i * 5 + 1)
                if not (isinstance(i, int) and i == 0):
                    pe.wait_ge(y_taken, i * 2)
                nc.tensor.matmul(state_ps, meta_rows[0:META, 2 * P:3 * P], meta_in[:, :], start=True,
                                 stop=True).then_inc(advanced, 1)
                first_half(i, 0)
                first_half(i, 1)
                second_half(i, 0)
                first_half(i, 2)
                second_half(i, 1)
                if more:
                    channels(i + 1, 3)
                first_half(i, 3)
                second_half(i, 2)
                if more:
                    gates(i + 1, 0)
                second_half(i, 3)
                if more:
                    gates(i + 1, 1)

            for m in range(4):
                channels(0, m)
            for j in range(2):
                gates(0, j)
            body(0, True)
            with pe.Fori(1, last) as i:
                body(i, True)
            body(last, False)
            turn_y(last)
    c.use = u0 + 2 * GROUPS


def rows_first(c, w, use):
    def go(sp):
        for j in range(2):
            load_tile(c, sp, use, j, tall_parts(c, j, w, 0, 16, j * P))
    return go


def ssd_out(c, w, src, y, out, following):
    nc = c.nc
    u0 = c.use
    pairs = KD // 2
    with ExitStack() as ph:
        taken = sem(c, "so_taken")
        pre = Split(c, src, y, 2 * KD)
        ps = c.psum
        block = ph.enter_context(nc.Block())

        @block.sync
        def _(sp):
            with sp.Fori(1, pairs) as i:
                for j in range(2):
                    load_tile(c, sp, u0 + i, j, tall_parts(c, j, w, 0, 16, (i * 2 + j) * P))
            following(sp)

        @block.scalar
        def _(act):
            for j in range(2):
                split_hi(c, act, u0, j)
                pre.scalar(j * KD, (j + 1) * KD)
            with act.Fori(1, pairs) as i:
                for j in range(2):
                    split_hi(c, act, u0 + i, j)

        @block.vector
        def _(dve):
            for j in range(2):
                split_lo(c, dve, u0, j)
                pre.vector(dve, j * KD, (j + 1) * KD)

            def take(i, j):
                dve.wait_ge(c.tile_used, 2 * (u0 + i) + j + 3)
                nc.vector.tensor_copy(out[:, bass.ds(i * 2 + j, 1), :].rearrange("p k t -> p (k t)"), ps[:, j, :]
                                      ).then_inc(taken, 1)

            with dve.Fori(0, pairs - 1) as i:
                for j in range(2):
                    take(i, j)
                    split_lo(c, dve, u0 + i + 1, j)
            for j in range(2):
                take(pairs - 1, j)

        @block.tensor
        def _(pe):
            def pairs_of(j):
                w_hi, w_lo = w_tile(c, j, 2 * KD, P)
                return lambda k: ((w_hi[:, k, :], w_lo[:, k, :]), (y[0][:, k, :], y[1][:, k, :]))

            for j in range(2):
                wait_tile(c, pe, u0, j)
            products_as_ready(c, pe, pre, [(ps[:, j, :], pairs_of(j), c.tile_used) for j in range(2)])
            with pe.Fori(1, pairs) as i:
                for j in range(2):
                    wait_tile(c, pe, u0 + i, j)
                    pe.wait_ge(taken, i * 2 + j - 1)
                    w_hi, w_lo = w_tile(c, j, 16, P)
                    products(c, ps[:, j, :], [((w_hi[:, k, :], w_lo[:, k, :]), (y[0][:, k, :], y[1][:, k, :]))
                                              for k in range(16)]).then_inc(c.tile_used, 1)
    c.use = u0 + pairs


def sc_parts(c, w_in, slot, n):
    if slot == 0:
        return pair_parts(c, 0, w_in, n * P + SC_AT, n * P + SX_AT)
    return wide_parts(c, 1, w_in, n * P + SB_AT, P)


def sc_first(c, w_in, use):
    def go(sp):
        for j in range(2):
            load_tile(c, sp, use, j, sc_parts(c, w_in, j, 0))
    return go


def short_conv(c, w_in, h, conv_w, out, following):
    nc = c.nc
    u0 = c.use
    taps = 3
    with ExitStack() as ph:
        sb = lambda name, shape, dt=F32: ph.enter_context(nc.sbuf_tensor(f"sc_{name}", shape, dt))
        x = sb("x", [P, TM])
        prod = sb("prod", [P, taps - 1 + TM])
        conv = sb("conv", [P, T])
        zeroed, c_done, x_done, x_taken, prod_done, conv_step, out_done = (sem(c, f"sc_{n}") for n in (
            "zeroed", "c_done", "x_done", "x_taken", "prod_done", "conv_step", "out_done"))
        ps = c.psum
        block = ph.enter_context(nc.Block())

        @block.gpsimd
        def _(pool):
            pool.memset(prod[:, 0:taps - 1], 0.0).then_inc(zeroed, 1)

        @block.sync
        def _(sp):
            with sp.Fori(1, KD) as n:
                for j in range(2):
                    load_tile(c, sp, u0 + n, j, sc_parts(c, w_in, j, n))
            following(sp)

        @block.scalar
        def _(act):
            def split(n):
                split_hi(c, act, u0 + n, 0)
                split_hi(c, act, u0 + n, 1, KD * P)

            def take(n):
                act.wait_ge(c.tile_used, 2 * (u0 + n) + 3)
                act.wait_ge(prod_done, n + 1)
                nc.scalar.copy(x[:, :].rearrange("p (b n) -> p b n", b=2), ps[:, 2:4, 0:HALF_TM]).then_inc(x_taken, 1)

            split(0)
            with act.Fori(0, KD - 1) as n:
                take(n)
                split(n + 1)
            take(KD - 1)

        @block.vector
        def _(dve):
            def split(n):
                split_lo(c, dve, u0 + n, 0)
                split_lo(c, dve, u0 + n, 1, KD * P)

            def convolve(n, more):
                tap = lambda k: conv_w[:, bass.ds(n, 1), k]
                dve.wait_ge(x_taken, n + 1)
                nc.vector.tensor_tensor(prod[:, taps - 1:].rearrange("p (b n) -> p b n", b=2),
                                        x[:, :].rearrange("p (b n) -> p b n", b=2), ps[:, 0:2, 0:HALF_TM],
                                        ALU.mult).then_inc(prod_done, 1)
                if more:
                    split(n + 1)
                dve.wait_ge(prod_done, n + 2)
                nc.vector.tensor_scalar(conv[:, :], prod[:, META:META + T], tap(0), None, ALU.mult
                                        ).then_inc(conv_step, 1)
                for k in range(1, taps):
                    dve.wait_ge(conv_step, n * 3 + k)
                    nc.vector.scalar_tensor_tensor(conv[:, :], prod[:, META + k:META + k + T], tap(k), conv[:, :],
                                                   ALU.mult, ALU.add).then_inc(conv_step, 1)
                dve.wait_ge(conv_step, n * 3 + 3)
                dve.wait_ge(c.tile_used, 2 * (u0 + n) + 4)
                nc.vector.tensor_tensor(out[:, bass.ds(n, 1), :].rearrange("p k t -> p (k t)"), conv[:, :],
                                        ps[:, 4, :], ALU.mult).then_inc(out_done, 1)

            dve.sem_inc(prod_done, 1)
            dve.sem_inc(out_done, 1)
            split(0)
            dve.wait_ge(zeroed, 1)
            with dve.Fori(0, KD - 1) as n:
                convolve(n, True)
            convolve(KD - 1, False)

        @block.tensor
        def _(pe):
            with pe.Fori(0, KD) as n:
                wait_tile(c, pe, u0 + n, 0)
                pe.wait_ge(prod_done, n + 1)
                for m in range(2):
                    w_hi, w_lo = (part[:, 0, :].rearrange("p (j k n) -> p j k n", j=2, k=KD)[:, m]
                                  for part in (c.hi, c.lo))
                    for b in range(2):
                        tok = slice(b * HALF_TM, (b + 1) * HALF_TM)
                        mm = products(c, ps[:, 2 * m + b, 0:HALF_TM], [
                            ((w_hi[:, k, :], w_lo[:, k, :]), (h[0][:, k, tok], h[1][:, k, tok])) for k in range(KD)])
                mm.then_inc(c.tile_used, 1)
                wait_tile(c, pe, u0 + n, 1)
                pe.wait_ge(out_done, n + 1)
                w_hi, w_lo = w_tile(c, 1, KD, P)
                products(c, ps[:, 4, :], [((w_hi[:, k, :], w_lo[:, k, :]), (h[0][:, k, META:TM], h[1][:, k, META:TM]))
                                          for k in range(KD)]).then_inc(c.tile_used, 1)
    c.use = u0 + KD


def gate_parts(c, w_in, slot, i):
    return wide_parts(c, slot, w_in, i * 256 + GATE_AT + slot * D)


def gate_first(c, w_in, use):
    def go(sp):
        for j in range(2):
            load_tile(c, sp, use, j, gate_parts(c, w_in, j, 0))
    return go


def merge(c, w_in, h, branches, following):
    nc = c.nc
    u0 = c.use
    pairs = D // 256
    with ExitStack() as ph:
        gate = ph.enter_context(nc.sbuf_tensor("mg_gate", [P, 2, 2, T], F32))
        gate_done, gated = (sem(c, f"mg_{n}") for n in ("gate_done", "gated"))
        ps = c.psum
        block = ph.enter_context(nc.Block())

        @block.sync
        def _(sp):
            with sp.Fori(1, pairs) as i:
                for j in range(2):
                    load_tile(c, sp, u0 + i, j, gate_parts(c, w_in, j, i))
            following(sp)

        @block.scalar
        def _(act):
            def sigmoid(i, j):
                act.wait_ge(c.tile_used, 2 * (u0 + i) + j + 3)
                act.wait_ge(gated, i * 2 + j + 1)
                nc.scalar.activation(gate[:, j], ps[:, 2 * j:2 * j + 2, :], ACT.Sigmoid).then_inc(gate_done, 1)

            for j in range(2):
                split_hi(c, act, u0, j)
            with act.Fori(0, pairs - 1) as i:
                for j in range(2):
                    sigmoid(i, j)
                    split_hi(c, act, u0 + i + 1, j)
            for j in range(2):
                sigmoid(pairs - 1, j)

        @block.vector
        def _(dve):
            def apply(i, j):
                part = branches[j][:, bass.ds(i * 2, 2), :]
                dve.wait_ge(gate_done, i * 2 + j + 1)
                nc.vector.tensor_tensor(part, part, gate[:, j], ALU.mult).then_inc(gated, 1)

            def add(i):
                first, second = (t[:, bass.ds(i * 2, 2), :] for t in branches)
                dve.wait_ge(gated, i * 2 + 4)
                nc.vector.tensor_tensor(first, first, second, ALU.add)

            dve.sem_inc(gated, 2)
            for j in range(2):
                split_lo(c, dve, u0, j)
            with dve.Fori(0, pairs - 1) as i:
                for j in range(2):
                    apply(i, j)
                    split_lo(c, dve, u0 + i + 1, j)
                add(i)
            for j in range(2):
                apply(pairs - 1, j)
            add(pairs - 1)

        @block.tensor
        def _(pe):
            with pe.Fori(0, pairs) as i:
                for j in range(2):
                    wait_tile(c, pe, u0 + i, j)
                    pe.wait_ge(gated, i * 2 + j + 1)
                    w_hi, w_lo = w_tile(c, j, KD, 256)
                    for n in range(2):
                        col = slice(n * P, (n + 1) * P)
                        mm = products(c, ps[:, 2 * j + n, :], [
                            ((w_hi[:, k, col], w_lo[:, k, col]), (h[0][:, k, META:TM], h[1][:, k, META:TM]))
                            for k in range(KD)])
                    mm.then_inc(c.tile_used, 1)
    c.use = u0 + pairs


NH = 8
KEYS = 128
TOP = 16
SLOTS = NH * TOP
LOW = -3e38
TG = 64
N_TG = T // TG
PART = 16
N_PARTS = KEYS // PART


class Steps:

    def __init__(self, eng, handle, turn, per):
        self.eng, self.handle, self.turn, self.per, self.n = eng, handle, turn, per, 0

    def __call__(self, ins):
        self.n += 1
        ins.then_inc(self.handle, 1)
        self.eng.wait_ge(self.handle, self.turn * self.per + self.n)


def peer_choose(c, gain, w_q, sub_keys, h, chosen):
    nc = c.nc
    u0 = c.use
    units = 2 * TC
    with ExitStack() as ph:
        sb = lambda name, shape, dt=F32: ph.enter_context(nc.sbuf_tensor(f"pq_{name}", shape, dt))
        keys = sb("keys", [P, 2, 2, P])
        keys_t = sb("keys_t", [P, 2, 2, P])
        q = sb("q", [P, 2, 2, T])
        s = sb("s", [P, 2, units, KEYS])
        rest = sb("rest", [P, units, KEYS])
        val = sb("val", [P, 2, units, TOP])
        idx = sb("idx", [P, 2, units, TOP], U32)
        pad = sb("pad", [P, 1])
        place_f = sb("place_f", [P, units, TOP])
        cand = sb("cand", [P, TC, TOP * TOP])
        cand_rest = sb("cand_rest", [P, TC, TOP * TOP])
        best = sb("best", [P, TC, TOP])
        best_at = sb("best_at", [P, TC, TOP], U32)
        digit = sb("digit", [P, 2, TC * TOP], U32)
        digit_f = sb("digit_f", [P, 2, TC * TOP])
        hot = sb("hot", [P, 2, TC * TOP, TOP])
        weight = sb("weight", [P, TC, TOP])
        total = sb("total", [P, TC])
        rows = sb("rows", [P, 3, TC, SLOTS])
        keys_loaded = [sem(c, f"pq_keys_loaded{j}") for j in range(2)]
        (q_taken, keys_turned, keys_taken, scored, s_taken, topped, indexed, cut, stored, steps, shifted, weighed,
         hot_done, picked, turned) = (sem(c, f"pq_{n}") for n in (
             "q_taken", "keys_turned", "keys_taken", "scored", "s_taken", "topped", "indexed", "cut", "stored",
             "steps", "shifted", "weighed", "hot_done", "picked", "turned"))
        PER = 6 + 3 + 2 + 2
        ps = c.psum
        keys_ps = ps[:, 4, 0:2 * P]
        s_ps = ps[:, 5:7, :].rearrange("p b n -> p (b n)")
        pre = Norm(c, ph, "peer", gain, h)
        block = ph.enter_context(nc.Block())

        @block.sync
        def _(sp):
            def keys_of(i, j):
                sp.wait_ge(c.begun, 1)
                sp.wait_ge(keys_turned, i * 2 + j + 1)
                sp.dma_start(keys[:, j], sub_keys[bass.ds((i * 2 + j), 1)].rearrange("h j k d -> k (h j) d")
                             ).then_inc(keys_loaded[j], 16)

            for j in range(2):
                keys_of(0, j)
            with sp.Fori(1, NH // 2) as i:
                for j in range(2):
                    load_tile(c, sp, u0 + i, j, wide_parts(c, j, w_q, (i * 2 + j) * 256))
                    keys_of(i, j)

        @block.scalar
        def _(act):
            def head(i, j):
                n = i * 2 + j
                act.wait_ge(c.tile_used, 2 * (u0 + i) + j + 3)
                act.wait_ge(scored, n + 1)
                nc.scalar.copy(q[:, j], ps[:, 2 * j:2 * j + 2, :]).then_inc(q_taken, 1)
                act.wait_ge(keys_turned, n + 3)
                nc.scalar.copy(keys_t[:, j].rearrange("p j k -> p (j k)"), keys_ps).then_inc(keys_taken, 1)

            def scores(i, j):
                n = i * 2 + j
                act.wait_ge(scored, n + 3)
                act.wait_ge(stored, n + 1)
                nc.scalar.copy(s[:, j].rearrange("p u k -> p (u k)"), s_ps).then_inc(s_taken, 1)

            def splits():
                for j in range(2):
                    split_hi(c, act, u0, j)

            def weigh(n):
                act.wait_ge(shifted, n + 1)
                nc.scalar.activation(weight[:, :, :], weight[:, :, :], ACT.Exp).then_inc(weighed, 1)

            def turn(i, j):
                head(i, j)
                split_hi(c, act, u0 + i + 1, j)
                scores(i, j)

            pre.scalar(act, splits)
            turn(0, 0)
            turn(0, 1)
            weigh(0)
            with act.Fori(1, NH // 2 - 1) as i:
                for j in range(2):
                    turn(i, j)
                    weigh(i * 2 + j - 1)
            for j in range(2):
                head(NH // 2 - 1, j)
                scores(NH // 2 - 1, j)
                weigh(NH - 3 + j)
            weigh(NH - 1)
            act.wait_ge(turned, 1)
            nc.scalar.copy(chosen[:, :, :], ps[:, 0:3, :])

        @block.gpsimd
        def _(pool):
            with pool.Fori(0, NH // 2) as i:
                for j in range(2):
                    for half in range(2):
                        pool.wait_ge(c.begun, 1)
                        pool.wait_ge(picked, i * 4 + j * 2 + half + 1)
                        hot4 = hot[:, half].rearrange("p (t k) a -> p t k a", t=TC)
                        number = place_f[:, half * TC:(half + 1) * TC, :].unsqueeze(2)
                        pool.tensor_tensor(hot4, hot4, number.broadcast_to([P, TC, TOP, TOP]), ALU.mult
                                           ).then_inc(hot_done, 1)

        @block.vector
        def _(dve):
            V = nc.vector

            def rank(i, j):
                n = i * 2 + j

                def wait(handle, value):
                    dve.wait_ge(handle, value)
                    V.memset(pad[:, :], 0.0)

                wait(s_taken, n + 1)
                for half in range(2):
                    src = s[:, j] if half == 0 else rest
                    part = slice(half * 8, half * 8 + 8)
                    if half:
                        wait(cut, (n + 1) * units)
                    for u in range(units):
                        V.max(val[:, j, u, part], src[:, u, :]).then_inc(topped, 1)
                    wait(topped, (n * 2 + half + 1) * units)
                    for u in range(units):
                        V.max_index(idx[:, j, u, part], val[:, j, u, part], src[:, u, :]).then_inc(indexed, 1)
                    if half == 0:
                        for u in range(units):
                            V.match_replace(rest[:, u, :], val[:, j, u, part], src[:, u, :], LOW).then_inc(cut, 1)
                dve.wait_ge(indexed, (n * 2 + 2) * units)
                V.tensor_copy(place_f[:, :, :], idx[:, j]).then_inc(stored, 1)

            def choose(i, j):
                n = i * 2 + j
                step = Steps(dve, steps, n, PER)

                def settle(ins):
                    step(ins)
                    V.memset(pad[:, :], 0.0)

                first = val[:, j, 0:TC, :].unsqueeze(3).broadcast_to([P, TC, TOP, TOP])
                second = val[:, j, TC:, :].unsqueeze(2).broadcast_to([P, TC, TOP, TOP])
                settle(V.tensor_tensor(cand[:, :, :].rearrange("p t (a b) -> p t a b", a=TOP), first, second, ALU.add))
                for half in range(2):
                    src, part = (cand, cand_rest)[half], slice(half * 8, half * 8 + 8)
                    for t in range(TC):
                        ins = V.max(best[:, t, part], src[:, t, :])
                    settle(ins)
                    for t in range(TC):
                        ins = V.max_index(best_at[:, t, part], best[:, t, part], src[:, t, :])
                    settle(ins)
                    if half == 0:
                        for t in range(TC):
                            ins = V.match_replace(cand_rest[:, t, :], best[:, t, part], src[:, t, :], LOW)
                        settle(ins)
                V.tensor_tensor(weight[:, :, :], best[:, :, :], best[:, :, 0:1].broadcast_to([P, TC, TOP]),
                                ALU.subtract).then_inc(shifted, 1)
                flat = best_at[:, :, :].rearrange("p t k -> p (t k)")
                V.tensor_scalar(digit[:, 0, :], flat, 4, None, ALU.logical_shift_right)
                step(V.tensor_scalar(digit[:, 1, :], flat, 15, None, ALU.bitwise_and))
                step(V.tensor_copy(digit_f[:, :, :], digit[:, :, :]))
                for half in range(2):
                    V.tensor_tensor(hot[:, half], digit_f[:, half, :].unsqueeze(2).broadcast_to([P, TC * TOP, TOP]),
                                    c.iota[:, 0:TOP].unsqueeze(1).broadcast_to([P, TC * TOP, TOP]), ALU.is_equal
                                    ).then_inc(picked, 1)
                dve.wait_ge(weighed, n + 1)
                step(V.tensor_reduce(total[:, :], weight[:, :, :], AX, ALU.add))
                step(V.reciprocal(total[:, :], total[:, :]))
                slots = bass.ds(n * TOP, TOP)
                step(V.tensor_tensor(rows[:, 2, :, slots], weight[:, :, :],
                                     total[:, :].unsqueeze(2).broadcast_to([P, TC, TOP]), ALU.mult))
                for half in range(2):
                    dve.wait_ge(hot_done, n * 2 + half + 1)
                    step(V.tensor_reduce(rows[:, half, :, slots],
                                         hot[:, half].rearrange("p (t k) a -> p t k a", t=TC), AX, ALU.add))
                assert step.n == PER

            dve.sem_inc(stored, 2)
            pre.vector(dve, lambda: split_lo(c, dve, u0, 0))
            split_lo(c, dve, u0, 1)
            with dve.Fori(0, NH // 2 - 1) as i:
                for j in range(2):
                    split_lo(c, dve, u0 + i + 1, j)
                    rank(i, j)
                    choose(i, j)
            for j in range(2):
                rank(NH // 2 - 1, j)
                choose(NH // 2 - 1, j)

        @block.tensor
        def _(pe):
            def queries(i, j):
                n = i * 2 + j
                if not (isinstance(i, int) and i == 0):
                    wait_tile(c, pe, u0 + i, j)
                    pe.wait_ge(q_taken, n - 1)
                    w_hi, w_lo = w_tile(c, j, KD, 256)
                    for m in range(2):
                        col = slice(m * P, (m + 1) * P)
                        mm = products(c, ps[:, 2 * j + m, :], [
                            ((w_hi[:, k, col], w_lo[:, k, col]), (h[0][:, k, :], h[1][:, k, :])) for k in range(KD)])
                    mm.then_inc(c.tile_used, 1)
                pe.wait_ge(keys_loaded[j], i * 16 + 16)
                if not (isinstance(i, int) and i == 0 and j == 0):
                    pe.wait_ge(keys_taken, n)
                for m in range(2):
                    mm = nc.tensor.transpose(keys_ps[:, m * P:(m + 1) * P], keys[:, j, m, :], c.ident[:, :])
                mm.then_inc(keys_turned, 1)

            def scores(n, j):
                pe.wait_ge(q_taken, n + 1)
                pe.wait_ge(keys_taken, n + 1)
                if not (isinstance(n, int) and n == 0):
                    pe.wait_ge(s_taken, n)
                for m in range(2):
                    for t in range(TC):
                        u = m * TC + t
                        mm = nc.tensor.matmul(s_ps[:, u * KEYS:(u + 1) * KEYS], q[:, j, m, t * P:(t + 1) * P],
                                              keys_t[:, j, m, :], start=True, stop=True)
                mm.then_inc(scored, 1)

            pe.sem_inc(keys_turned, 2)
            pe.sem_inc(scored, 2)
            pre.tensor(pe)
            for j in range(2):
                wait_tile(c, pe, u0, j)
                products_as_ready(c, pe, pre, wide_jobs(c, h, j))
            queries(0, 0)
            queries(0, 1)
            scores(0, 0)
            with pe.Fori(1, NH // 2) as i:
                queries(i, 0)
                scores(i * 2 - 1, 1)
                queries(i, 1)
                scores(i * 2, 0)
            scores(NH - 1, 1)
            pe.wait_ge(steps, NH * PER)
            for r in range(3):
                for t in range(TC):
                    mm = nc.tensor.transpose(ps[:, r, t * P:(t + 1) * P], rows[:, r, t, :], c.ident[:, :])
            mm.then_inc(turned, 1)
    c.use = u0 + NH // 2


def peer_spread(c, chosen, gates, following):
    nc = c.nc
    QUADS = 4
    with ExitStack() as ph:
        sb = lambda name, shape, dt=F32: ph.enter_context(nc.sbuf_tensor(f"pg_{name}", shape, dt))
        second = sb("second", [P, QUADS, 4, KEYS])
        first = sb("first", [P, QUADS, 4, KEYS])
        staged = sb("staged", [P, 2, KEYS, TG])
        begun, built, weighed, spread, taken = (sem(c, f"pg_{n}") for n in (
            "begun", "built", "weighed", "spread", "taken"))
        written = [sem(c, f"pg_written{p}") for p in range(2)]
        ps = c.psum
        inner = TG // (4 * QUADS)
        block = ph.enter_context(nc.Block())

        def turns(eng, body):
            with eng.Fori(0, N_TG // 2) as o:
                for p in range(2):
                    with eng.Fori(0, inner) as n:
                        body((o * 2 + p) * inner + n, n, o, p)

        @block.vector
        def _(dve):
            V = nc.vector

            def body(m, n, o, p):
                for q in range(QUADS):
                    dve.wait_ge(spread, m * QUADS + q + 1)
                    number = lambda r: chosen[:, r, bass.ds(m * (4 * QUADS) + q * 4, 4)].unsqueeze(2).broadcast_to([P, 4, KEYS])
                    wide = c.iota[:, :].unsqueeze(1).broadcast_to([P, 4, KEYS])
                    V.tensor_tensor(second[:, q], number(1), wide, ALU.is_equal)
                    V.tensor_tensor(first[:, q], number(0), wide, ALU.is_equal).then_inc(built, 1)

            turns(dve, body)

        @block.gpsimd
        def _(pool):
            def body(m, n, o, p):
                for q in range(QUADS):
                    pool.wait_ge(begun, 1)
                    pool.wait_ge(built, m * QUADS + q + 1)
                    weight = chosen[:, 2, bass.ds(m * (4 * QUADS) + q * 4, 4)].unsqueeze(2).broadcast_to([P, 4, KEYS])
                    pool.tensor_tensor(first[:, q], first[:, q], weight, ALU.mult).then_inc(weighed, 1)

            pool.sem_inc(begun, 1)
            turns(pool, body)

        @block.tensor
        def _(pe):
            def body(m, n, o, p):
                for q in range(QUADS):
                    pe.wait_ge(weighed, m * QUADS + q + 1)
                    pe.wait_ge(taken, m * QUADS + q + 1)
                    for j in range(4):
                        mm = nc.tensor.matmul(ps[:, q, j * KEYS:(j + 1) * KEYS], second[:, q, j, :],
                                              first[:, q, j, :], start=True, stop=True)
                    mm.then_inc(spread, 1)

            pe.sem_inc(spread, QUADS)
            turns(pe, body)

        @block.scalar
        def _(act):
            def body(m, n, o, p):
                act.wait_ge(written[p], o * 16 + 16)
                for q in range(QUADS):
                    act.wait_ge(spread, m * QUADS + q + QUADS + 1)
                    nc.scalar.copy(staged[:, p, :, bass.ds(n * (4 * QUADS) + q * 4, 4)],
                                   ps[:, q, :].rearrange("p (t k) -> p k t", t=4)).then_inc(taken, 1)

            act.sem_inc(taken, QUADS)
            turns(act, body)

        @block.sync
        def _(sp):
            following(sp)
            for p in range(2):
                sp.sem_inc(written[p], 16)
            with sp.Fori(0, N_TG // 2) as o:
                for p in range(2):
                    sp.wait_ge(c.begun, 1)
                    sp.wait_ge(taken, (o * 2 + p + 1) * (inner * QUADS) + QUADS)
                    sp.dma_start(gates[bass.ds(o * 2 + p, 1)].rearrange("g p k t -> p (g k) t"), staged[:, p]
                                 ).then_inc(written[p], 16)
            for p in range(2):
                sp.wait_ge(written[p], 16 * (N_TG // 2) + 16)


def u_parts(c, slot, u, first):
    v = u.rearrange("(a b) d -> b a d", b=KEYS)
    dst = raw_tile(c, slot, 2, D)
    return [(dst[:, a:a + 1, :], v[:, bass.ds(first + a, 1), :]) for a in range(2)]


def v_parts(c, slot, w, first, half):
    v = w.rearrange("(a b) d -> b a d", b=KEYS)
    dst = raw_tile(c, slot, 4, D // 2)
    return [(dst[:, a:a + 2, :], v[:, bass.ds(first + a, 2), half * 512:half * 512 + 512]) for a in (0, 2)]


def u_first(c, u, use):
    def go(sp):
        for j in range(2):
            load_tile(c, sp, use, j, u_parts(c, j, u, 2 * j))
    return go


def peer_experts(c, u, v, h, gates, following):
    nc = c.nc
    u0 = c.use
    N_U = PART // 2
    PER = N_U
    with ExitStack() as ph:
        sb = lambda name, shape, dt=F32: ph.enter_context(nc.sbuf_tensor(f"pe_{name}", shape, dt))
        act_hi = sb("act_hi", [P, PART, T], F32R)
        act_lo = sb("act_lo", [P, PART, T], F32R)
        gate = sb("gate", [P, 2, N_TG, 2, TG])
        gelu = sb("gelu", [P, 2, T])
        prod = sb("prod", [P, 2, T])
        gate_loaded = [sem(c, f"pe_gate_loaded{j}") for j in range(2)]
        turned, hidden, gelued, gated, hi_done, lo_done, out_done, added = (sem(c, f"pe_{n}") for n in (
            "turned", "hidden", "gelued", "gated", "hi_done", "lo_done", "out_done", "added"))
        ps = c.psum
        turn_ps = ps[:, 0:4, :].rearrange("p b n -> p (b n)")
        block = ph.enter_context(nc.Block())

        @block.sync
        def _(sp):
            def gate_tile(q, i, j):
                sp.wait_ge(c.begun, 1)
                sp.wait_ge(gated, q * N_U + i * 2 + j + 1)
                src = gates[:, :, bass.ds(q * PART + i * 4 + j * 2, 2), :].rearrange("g p a t -> p g a t")
                sp.dma_start(gate[:, j], src).then_inc(gate_loaded[j], 16)

            def part(q, begun):
                use = u0 + q * PER
                for j in range(2):
                    if not begun:
                        load_tile(c, sp, use, j, u_parts(c, j, u, q * PART + j * 2))
                    gate_tile(q, 0, j)
                with sp.Fori(1, N_U // 2) as i:
                    for j in range(2):
                        load_tile(c, sp, use + i, j, u_parts(c, j, u, q * PART + i * 4 + j * 2))
                        gate_tile(q, i, j)
                for half in range(2):
                    for m in range(PART // 4):
                        load_tile(c, sp, use + N_U // 2 + half * 2 + m // 2, m % 2,
                                  v_parts(c, m % 2, v, q * PART + m * 4, half))

            part(0, True)
            with sp.Fori(1, N_PARTS) as q:
                part(q, False)
            following(sp)

        @block.tensor
        def _(pe):
            def turn(q, i, j):
                use = u0 + q * PER + i
                pe.wait_ge(c.tile_loaded[j], 32 * use + 32)
                pe.wait_ge(c.lo_ready, 2 * use + j + 2)
                rows = raw_tile(c, j, 2, D)
                for a in range(2):
                    for k in range(KD):
                        at = (a * KD + k) * P
                        mm = nc.tensor.transpose(turn_ps[:, at:at + P], rows[:, a, k * P:(k + 1) * P], c.ident[:, :])
                mm.then_inc(turned, 1)

            def hide(q, i, j):
                n = q * N_U + i * 2 + j
                wait_tile(c, pe, u0 + q * PER + i, j)
                pe.wait_ge(gelued, n + 1)
                if j == 0:
                    pe.wait_ge(added, q * 2 + 2)
                w_hi, w_lo = (t[:, j, :].rearrange("p (a k n) -> p a k n", a=2, k=KD) for t in (c.hi, c.lo))
                for a in range(2):
                    mm = products(c, ps[:, 4 + a, :], [
                        ((w_hi[:, a, k, :], w_lo[:, a, k, :]), (h[0][:, k, :], h[1][:, k, :])) for k in range(KD)])
                mm.then_inc(c.tile_used, 1)

            def outputs(q, half, more):
                if half == 1:
                    pe.wait_ge(gelued, q * N_U + N_U + 1)
                for m in range(PART // 4):
                    j = m % 2
                    if more and half == 1 and m == PART // 4 - 1:
                        pe.wait_ge(added, q * 2 + 3)
                        turn(q + 1, 0, 0)
                    wait_tile(c, pe, u0 + q * PER + N_U // 2 + half * 2 + m // 2, j)
                    pe.wait_ge(lo_done, q * N_U + 2 * m + 3)
                    w_hi, w_lo = w_tile(c, j, 4, D // 2)
                    for a in range(4):
                        e = m * 4 + a
                        for d in range(4):
                            out, col = ps[:, 4 * half + d, :], slice(d * P, (d + 1) * P)
                            start, stop = e == 0, e == PART - 1
                            nc.tensor.matmul(out, w_hi[:, a, col], act_hi[:, e, :], start=start, stop=False)
                            nc.tensor.matmul(out, w_hi[:, a, col], act_lo[:, e, :], start=False, stop=False)
                            mm = nc.tensor.matmul(out, w_lo[:, a, col], act_hi[:, e, :], start=False, stop=stop)
                    mm.then_inc(c.tile_used, 1)

            def part(q, more):
                with pe.Fori(0, N_U // 2 - 1) as i:
                    turn(q, i, 1)
                    hide(q, i, 0)
                    turn(q, i + 1, 0)
                    hide(q, i, 1)
                i = N_U // 2 - 1
                turn(q, i, 1)
                hide(q, i, 0)
                hide(q, i, 1)
                for half in range(2):
                    outputs(q, half, more)

            turn(0, 0, 0)
            with pe.Fori(0, N_PARTS - 1) as q:
                part(q, True)
            part(N_PARTS - 1, False)

        @block.scalar
        def _(act):
            def turned_hi(q, i, j):
                use = u0 + q * PER + i
                act.wait_ge(turned, q * N_U + i * 2 + j + 1)
                act.wait_ge(c.tile_used, 2 * use + j + 1)
                nc.scalar.copy(c.hi[:, j, :], turn_ps).then_inc(c.hi_ready, 1)

            def activate(q, i, j):
                n = q * N_U + i * 2 + j
                act.wait_ge(c.tile_used, 2 * (u0 + q * PER + i) + j + 3)
                act.wait_ge(gated, n + 2)
                nc.scalar.activation(gelu[:, :, :], ps[:, 4:6, :], ACT.Gelu).then_inc(gelued, 1)

            def high(q, i, j):
                n = q * N_U + i * 2 + j
                act.wait_ge(gated, n + 3)
                nc.scalar.copy(act_hi[:, bass.ds(i * 4 + j * 2, 2), :], prod[:, :, :]).then_inc(hi_done, 1)

            def part(q, more):
                with act.Fori(0, N_U // 2 - 1) as i:
                    turned_hi(q, i, 1)
                    activate(q, i, 0)
                    high(q, i, 0)
                    turned_hi(q, i + 1, 0)
                    activate(q, i, 1)
                    high(q, i, 1)
                i = N_U // 2 - 1
                turned_hi(q, i, 1)
                activate(q, i, 0)
                high(q, i, 0)
                split_hi(c, act, u0 + q * PER + N_U // 2, 0)
                activate(q, i, 1)
                high(q, i, 1)
                for m in range(1, N_U):
                    split_hi(c, act, u0 + q * PER + N_U // 2 + m // 2, m % 2)
                if more:
                    turned_hi(q + 1, 0, 0)

            act.sem_inc(gelued, 1)
            turned_hi(0, 0, 0)
            with act.Fori(0, N_PARTS - 1) as q:
                part(q, True)
            part(N_PARTS - 1, False)

        @block.gpsimd
        def _(pool):
            pool.sem_inc(gated, 2)
            with pool.Fori(0, N_PARTS * N_U // 2) as m:
                for j in range(2):
                    n = m * 2 + j
                    pool.wait_ge(c.begun, 1)
                    pool.wait_ge(gelued, n + 2)
                    pool.wait_ge(gate_loaded[j], m * 16 + 16)
                    pool.wait_ge(lo_done, n + 1)
                    pool.tensor_tensor(prod[:, :, :].rearrange("p a (g t) -> p a g t", g=N_TG),
                                       gelu[:, :, :].rearrange("p a (g t) -> p a g t", g=N_TG),
                                       gate[:, j].rearrange("p g a t -> p a g t"), ALU.mult).then_inc(gated, 1)

        @block.vector
        def _(dve):
            V = nc.vector

            def turned_lo(q, i, j):
                dve.wait_ge(c.hi_ready, 2 * (u0 + q * PER + i) + j + 1)
                V.tensor_tensor(c.lo[:, j, :], turn_ps, c.hi[:, j, :].bitcast(F32), ALU.subtract
                                ).then_inc(c.lo_ready, 1)

            def low(q, i, j):
                place = bass.ds(i * 4 + j * 2, 2)
                dve.wait_ge(hi_done, q * N_U + i * 2 + j + 1)
                V.tensor_tensor(act_lo[:, place, :], prod[:, :, :], act_hi[:, place, :].bitcast(F32),
                                ALU.subtract).then_inc(lo_done, 1)

            def add(q, half):
                dve.wait_ge(c.tile_used, 2 * (u0 + q * PER + N_U // 2 + half * 2 + 2) + 2)
                x = c.x_t[:, 4 * half:4 * half + 4, :]
                V.tensor_tensor(x, x, ps[:, 4 * half:4 * half + 4, :], ALU.add).then_inc(added, 1)

            def part(q, more):
                with dve.Fori(0, N_U // 2 - 1) as i:
                    turned_lo(q, i, 1)
                    low(q, i, 0)
                    turned_lo(q, i + 1, 0)
                    low(q, i, 1)
                i = N_U // 2 - 1
                turned_lo(q, i, 1)
                low(q, i, 0)
                split_lo(c, dve, u0 + q * PER + N_U // 2, 0)
                low(q, i, 1)
                for m in range(1, N_U):
                    split_lo(c, dve, u0 + q * PER + N_U // 2 + m // 2, m % 2)
                    if m == PART // 4 + 1:
                        add(q, 0)
                if more:
                    turned_lo(q + 1, 0, 0)
                add(q, 1)

            dve.sem_inc(added, 2)
            dve.sem_inc(lo_done, 1)
            turned_lo(0, 0, 0)
            with dve.Fori(0, N_PARTS - 1) as q:
                part(q, True)
            part(N_PARTS - 1, False)
    c.use = u0 + N_PARTS * PER


class Layer:

    def __init__(self, name, first, uses, run):
        self.name, self.first, self.uses, self.run = name, first, uses, run


def splits(c, ph, tag, width=T):
    return [ph.enter_context(c.nc.sbuf_tensor(f"h_{n}_{tag}", [P, KD, width], F32R)) for n in ("hi", "lo")]


def ffn_layer(c, w, layer, which):
    tag = f"ffn{layer}{which}"
    w_gu, w_down = w["ffn_w_gate_up"][layer, which], w["ffn_w_down"][layer, which]

    def run(following):
        with ExitStack() as ph:
            h = splits(c, ph, tag)
            ffn(c, tag, gain_of(c, layer, 2 * which), w_gu, w_down, h, following)

    return Layer(tag, lambda use: ffn_first(c, w_gu, use), F_FF // 256 + KD, run)


def gain_of(c, layer, which):
    return lambda k: vec_col(c, "norm_gains", (3 * layer + which) * KD + k)


def sb_layer(c, w):
    w_in, w_out = w["sb_w_in"][0], w["sb_w_out"][0]

    def first(use):
        def go(sp):
            for j in range(2):
                load_tile(c, sp, use, j, wide_parts(c, j, w_in, 2 * D + j * 256))
        return go

    def run(following):
        with ExitStack() as ph:
            h = splits(c, ph, "sb")
            o_t = ph.enter_context(c.nc.sbuf_tensor("sb_o_t", [P, KD, T], F32))
            sb_attention(c, gain_of(c, 0, 1), w_in, h, o_t, wide_first(c, w_out, c.use + 2 + SB_GROUPS))
            project(c, w_out, o_t, h, following)

    return Layer("sb", first, 2 + SB_GROUPS + 2, run)


def sw_layer(c, w):
    w_in, w_out = w["sw_w_in"][0], w["sw_w_out"][0]

    def run(following):
        with ExitStack() as ph:
            h = splits(c, ph, "sw")
            o_t = ph.enter_context(c.nc.sbuf_tensor("sw_o_t", [P, KD, T], F32))
            qk = ph.enter_context(c.nc.sbuf_tensor("sw_qk", [P, TC, SW_QK * HEAD], F32))
            v = ph.enter_context(c.nc.sbuf_tensor("sw_v", [P, TC, P], F32))
            sw_project(c, gain_of(c, 1, 1), w_in, h, qk, v, wide_first(c, w_out, c.use + 3))
            sw_rotate(c, w["positions"], qk)
            sw_attention(c, qk, v, o_t)
            project(c, w_out, o_t, h, following)

    return Layer("sw", lambda use: wide_first(c, w_in, use), 3 + 2, run)


def move(c, dst, src):
    with ExitStack() as ph:
        block = ph.enter_context(c.nc.Block())

        @block.scalar
        def _(act):
            c.nc.scalar.copy(dst[:, 0:KD // 2, :], src[:, 0:KD // 2, :])

        @block.vector
        def _(dve):
            c.nc.vector.tensor_copy(dst[:, KD // 2:, :], src[:, KD // 2:, :])


def mixer_layer(c, w):
    nc = c.nc
    w_in, ssd_w_out, sc_w_out, w_o = w["w_in"][0], w["ssd_w_out"][0], w["sc_w_out"][0], w["w_o"][0]

    def run(following):
        with ExitStack() as ph:
            sb = lambda name, shape, dt=F32, on=ph: on.enter_context(nc.sbuf_tensor(f"mix_{name}", shape, dt))
            h = [sb(f"h_{n}", [P, KD, TM], F32R) for n in ("hi", "lo")]
            conv_w = [sb("conv_w", [P, 32, 4]), sb("sc_conv_w", [P, KD, 3])]
            with ExitStack() as pre:
                xm = sb("xm", [P, KD, TM], on=pre)
                widen(c, w["meta_tokens"], xm)
                norm(c, "mix", lambda k: vec_col(c, "ln_mix", k), h, src=xm, width=TM)
            with ExitStack() as pre:
                dec = Decay()
                dec.dt, dec.adt, dec.sums, dec.dt_end = (sb(n, [P, TC + 1, 32], on=pre)
                                                         for n in ("dt", "adt", "sums", "dt_end"))
                dec.from_start, dec.whole = (sb(n, [P, TC, 32], on=pre) for n in ("from_start", "whole"))
                with ExitStack() as last:
                    ssd_times(c, w_in, h, dec, (w["ssd_conv_w"][0], w["sc_conv_w"][0]), conv_w)
                    y_t = sb("y_t", [P, 16, T], on=last)
                    ssd(c, w_in, h, dec, conv_w[0], y_t, rows_first(c, ssd_w_out, c.use + 16))
                y_lo, y_hi = (sb(n, [P, 16, T], F32R, on=pre) for n in ("y_lo", "y_hi"))
                branch = sb("branch0", [P, KD, T], on=pre)
                ssd_out(c, ssd_w_out, y_t, (y_hi, y_lo), branch, sc_first(c, w_in, c.use + 4))
            with ExitStack() as pre:
                ys = sb("branch_ssd", [P, KD, T], on=pre)
                move(c, ys, branch)
                s_t = sb("s_t", [P, KD, T], on=pre)
                short_conv(c, w_in, h, conv_w[1], s_t, wide_first(c, sc_w_out, c.use + KD))
                s_hi, s_lo = (sb(f"s_{n}", [P, KD, T], F32R, on=pre) for n in ("hi", "lo"))
                project(c, sc_w_out, s_t, (s_hi, s_lo), gate_first(c, w_in, c.use + 2), out=s_t)
                merge(c, w_in, h, (ys, s_t), wide_first(c, w_o, c.use + 4))
                project(c, w_o, ys, (s_hi, s_lo), following)

    return Layer("mixer", lambda use: ssd_first(c, w_in, use), 16 + 4 + KD + 2 + 4 + 2, run)


def peer_layer(c, w):
    nc = c.nc
    gates = nc.dram_tensor("peer_gates", [N_TG, P, KEYS, TG], F32).ap()
    w_q, keys, u, v = w["peer_w_q"][0], w["peer_sub_keys"][0], w["peer_u"][0], w["peer_v"][0]

    def run(following):
        with ExitStack() as ph:
            h = splits(c, ph, "peer")
            with ExitStack() as pre:
                chosen = pre.enter_context(nc.sbuf_tensor("chosen", [P, 3, T], F32))
                peer_choose(c, lambda k: vec_col(c, "ln_ffn", k), w_q, keys, h, chosen)
                peer_spread(c, chosen, gates, u_first(c, u, c.use))
            peer_experts(c, u, v, h, gates, following)

    return Layer("peer", lambda use: wide_first(c, w_q, use), NH // 2 + N_PARTS * PART // 2, run)


def final_layer(c, out):
    def run(following):
        with ExitStack() as ph:
            y = ph.enter_context(c.nc.sbuf_tensor("final", [P, KD, T], F32))
            norm(c, "final", lambda k: vec_col(c, "ln_final", k), None, out_f32=y)
            store(c, out, y)

    return Layer("final", lambda use: (lambda sp: None), 0, run)


def build(nc, args, out):
    w = {n.removesuffix("_2"): a for n, a in args.items()}
    with ExitStack() as ctx:
        c = Chip()
        c.nc, c.ctx, c.use, c.stages = nc, ctx, 0, {}
        sb = lambda name, shape, dt=F32: ctx.enter_context(nc.sbuf_tensor(name, shape, dt))
        c.x_t = sb("x_t", [P, KD, T])
        c.raw = sb("w_raw", [P, 2, TILE])
        c.hi = sb("w_hi", [P, 2, TILE], F32R)
        c.lo = sb("w_lo", [P, 2, TILE], F32R)
        c.ones = sb("ones", [P, P])
        c.neg_ones = sb("neg_ones", [P, P])
        c.ident = sb("ident", [P, P])
        c.tri_up = sb("tri_up", [P, P])
        c.neg_tri = sb("neg_tri", [P, P])
        c.swa_mask = sb("swa_mask", [P, TC, 2 * P])
        c.causal_cap = sb("causal_cap", [P, P])
        c.iota = sb("iota", [P, P])
        c.vec = sb("vec", [P, sum(n for _, n in VECTORS)])
        c.rows = sb("rows", [P, sum(n for _, n in ROWS)])
        c.psum = ctx.enter_context(nc.psum_tensor("psum", [P, 8, BANK], F32))
        c.tile_loaded = [sem(c, f"tile_loaded{j}") for j in range(2)]
        c.begun = sem(c, "begun")
        c.hi_ready, c.lo_ready, c.tile_used = (sem(c, n) for n in ("hi_ready", "lo_ready", "tile_used"))

        plan = [ffn_layer(c, w, 0, 0), sb_layer(c, w), ffn_layer(c, w, 0, 1),
                ffn_layer(c, w, 1, 0), sw_layer(c, w), ffn_layer(c, w, 1, 1),
                mixer_layer(c, w), peer_layer(c, w), final_layer(c, out)]
        following, at = [], 0
        for layer in plan:
            following.append(layer.first(at))
            at += layer.uses
        following.append(lambda sp: None)
        setup(c, w, following[0])
        for n, layer in enumerate(plan):
            layer.run(following[n + 1])
            assert c.use == sum(done.uses for done in plan[:n + 1]), layer.name


_INS = ["x", "positions", "norm_gains", "ffn_w_gate_up", "ffn_w_down", "sb_w_in", "sb_w_out", "sw_w_in", "sw_w_out",
        "sw_q_gain", "sw_k_gain", "sw_sinks", "meta_tokens_2", "ln_mix_2", "w_in_2", "ssd_conv_w_2", "ssd_conv_b_2",
        "ssd_dt_bias_2", "ssd_a_log_2", "ssd_d_2", "ssd_norm_2", "ssd_w_out_2", "sc_conv_w_2", "sc_w_out_2",
        "w_o_2", "ln_ffn_2", "peer_w_q_2", "peer_sub_keys_2", "peer_u_2", "peer_v_2", "ln_final_2"]
_OUTS = [((1, T, D), "float32")]


def kernel(**inputs):
    import numpy as _np
    import concourse.bacc as _bacc
    from concourse import mybir as _mybir
    from concourse.bass_utils import run_bass_kernel_spmd as _run

    nc = _bacc.Bacc("TRN2", target_bir_lowering=False, num_devices=1)
    arrays, args = {}, {}
    for name in _INS:
        a = _np.ascontiguousarray(inputs[name])
        arrays[f"in_{name}_dram"] = a
        args[name] = nc.dram_tensor(f"in_{name}_dram", a.shape, _mybir.dt.from_np(a.dtype), kind="ExternalInput").ap()
    out = nc.dram_tensor("out_0_dram", _OUTS[0][0], F32, kind="ExternalOutput").ap()
    build(nc, args, out)
    r = _run(nc, [arrays], core_ids=[0])
    return r.results[0]["out_0_dram"]
```
